# Optimizing a Trainium2 kernel written in Bass

```python
import jax
import jax.numpy as jnp
from jax import lax
import numpy as np
import math

D_MODEL = 1024
BATCH = 1
SEQ = 512
DEPTH = 2

N_MIXERS = 2
MIX_WIDTH = D_MODEL
X_WIDTH = D_MODEL // 4
N_X_HEADS = 4
X_HEAD_DIM = X_WIDTH // N_X_HEADS
SEQ_MIX_WIDTH = MIX_WIDTH - X_WIDTH
LIN_HEAD_DIM = 128
N_LIN_HEADS = SEQ_MIX_WIDTH // LIN_HEAD_DIM
CONV_WIDTH = 4
CHUNK = 64
SB_HEAD_DIM = 64
N_SB_HEADS = SEQ_MIX_WIDTH // SB_HEAD_DIM
SB_BLOCK = 128
N_MEM = 256
D_FF = 4 * D_MODEL
EPS = 1e-6
N_A_LAYERS = (DEPTH + 1) // 2
N_B_LAYERS = DEPTH // 2
IN_A = 4 * SEQ_MIX_WIDTH + 2 * N_LIN_HEADS + X_WIDTH
IN_B = 3 * SEQ_MIX_WIDTH + X_WIDTH


def rms_norm(x, g):
    xf = x.astype(jnp.float32)
    y = xf * lax.rsqrt(jnp.mean(xf * xf, axis=-1, keepdims=True) + EPS)
    return (y * g.astype(jnp.float32)).astype(x.dtype)

def l2norm(x):
    return x * lax.rsqrt(jnp.sum(x * x, axis=-1, keepdims=True) + EPS)

def causal_conv(x, w):
    c = x.shape[-1]
    return lax.conv_general_dilated(
        x, w[:, None, :].astype(x.dtype), window_strides=(1,),
        padding=[(CONV_WIDTH - 1, 0)], dimension_numbers=('NWC', 'WIO', 'NWC'),
        feature_group_count=c)

def gated_deltanet(p, conv_w, a_log, dt_bias, o_gain):
    B, S, _ = p.shape
    H, Dh, C, W = N_LIN_HEADS, LIN_HEAD_DIM, CHUNK, SEQ_MIX_WIDTH
    nc = S // C
    qkv = jax.nn.silu(causal_conv(p[..., :3 * W], conv_w)).astype(jnp.float32)
    gate = p[..., 3 * W:4 * W].astype(jnp.float32)
    beta = jax.nn.sigmoid(p[..., 4 * W:4 * W + H].astype(jnp.float32))
    g = -jnp.exp(a_log.astype(jnp.float32)) * jax.nn.softplus(
        p[..., 4 * W + H:].astype(jnp.float32) + dt_bias.astype(jnp.float32))
    q = l2norm(qkv[..., :W].reshape(B, S, H, Dh)) * (Dh ** -0.5)
    k = l2norm(qkv[..., W:2 * W].reshape(B, S, H, Dh))
    v = qkv[..., 2 * W:].reshape(B, S, H, Dh)

    def chunked(t):
        t = t.reshape((B, nc, C) + t.shape[2:])
        return jnp.moveaxis(jnp.moveaxis(t, 1, 0), 3, 2)

    q, k, v, beta = chunked(q), chunked(k), chunked(v), chunked(beta)
    gc = jnp.cumsum(chunked(g), axis=-1)
    idx = jnp.arange(C)
    causal = idx[:, None] >= idx[None, :]
    strict = idx[:, None] > idx[None, :]
    decay = jnp.exp(jnp.where(causal, gc[..., :, None] - gc[..., None, :], -jnp.inf))
    kb = k * beta[..., None]
    lower = jnp.where(strict, jnp.einsum('nbhcd,nbhsd->nbhcs', kb, k) * decay, 0.0)
    eye = jnp.eye(C, dtype=jnp.float32)
    rhs = jnp.concatenate([v * beta[..., None], kb * jnp.exp(gc)[..., None]], axis=-1)
    sol = lax.linalg.triangular_solve(eye + lower, rhs, left_side=True, lower=True,
                                      unit_diagonal=True)
    u, w = sol[..., :Dh], sol[..., Dh:]
    intra = jnp.einsum('nbhcd,nbhsd->nbhcs', q, k) * decay
    q_dec = q * jnp.exp(gc)[..., None]
    k_dec = k * jnp.exp(gc[..., -1:] - gc)[..., None]
    chunk_decay = jnp.exp(gc[..., -1])

    def step(state, inp):
        u_c, w_c, q_c, k_c, a_c, d_c = inp
        v_new = u_c - jnp.einsum('bhcd,bhde->bhce', w_c, state)
        o_c = jnp.einsum('bhcd,bhde->bhce', q_c, state) + jnp.einsum('bhcs,bhse->bhce', a_c, v_new)
        state = state * d_c[..., None, None] + jnp.einsum('bhcd,bhce->bhde', k_c, v_new)
        return state, o_c

    state0 = jnp.zeros((B, H, Dh, Dh), jnp.float32)
    _, o = lax.scan(step, state0, (u, w, q_dec, k_dec, intra, chunk_decay))
    o = jnp.swapaxes(jnp.moveaxis(o, 0, 1), 2, 3).reshape(B, S, H, Dh)
    o = o * lax.rsqrt(jnp.mean(o * o, axis=-1, keepdims=True) + EPS) * o_gain.astype(jnp.float32)
    o = o * jax.nn.silu(gate.reshape(B, S, H, Dh))
    return o.reshape(B, S, W)

def stick_breaking_attention(q, k, v):
    B, S, H, Dh = q.shape
    scale = Dh ** -0.5
    outs = []
    for blk in range(S // SB_BLOCK):
        t0 = blk * SB_BLOCK
        t1 = t0 + SB_BLOCK
        kb, vb = k[:, :t1], v[:, :t1]
        z = jnp.einsum('bthd,bshd->bhts', q[:, t0:t1], kb,
                       preferred_element_type=jnp.float32) * scale
        t_idx = t0 + jnp.arange(SB_BLOCK)[:, None]
        s_idx = jnp.arange(t1)[None, :]
        before = s_idx < t_idx
        log_beta = jax.nn.log_sigmoid(z)
        log_1m_beta = jnp.where(before, jax.nn.log_sigmoid(-z), 0.0)
        tail = lax.cumsum(log_1m_beta, axis=3, reverse=True) - log_1m_beta
        a = jnp.where(before, jnp.exp(log_beta + tail), 0.0)
        outs.append(jnp.einsum('bhts,bshd->bthd', a.astype(vb.dtype), vb))
    return jnp.concatenate(outs, axis=1).reshape(B, S, H * Dh)

def memory_attention(q, mem_kv):
    B, S, _ = q.shape
    q = q.reshape(B, S, N_X_HEADS, X_HEAD_DIM)
    k = mem_kv[..., :X_WIDTH].reshape(B, N_MEM, N_X_HEADS, X_HEAD_DIM)
    v = mem_kv[..., X_WIDTH:].reshape(B, N_MEM, N_X_HEADS, X_HEAD_DIM)
    s = jnp.einsum('bshd,bmhd->bhsm', q, k, preferred_element_type=jnp.float32) * (X_HEAD_DIM ** -0.5)
    p = jax.nn.softmax(s, axis=-1).astype(v.dtype)
    return jnp.einsum('bhsm,bmhd->bshd', p, v).reshape(B, S, X_WIDTH)

def first_inputs(seed: int = 0) -> dict:
    key = jax.random.key(seed)
    ks = jax.random.split(key, 18)
    f32 = jnp.float32
    nrm = lambda k, shape, scale: jax.random.normal(k, shape, f32) * scale
    gain = lambda k, shape: 1.0 + 0.1 * jax.random.normal(k, shape, f32)
    return {
        'x': nrm(ks[0], (BATCH, SEQ, D_MODEL), 1.0),
        'mem': nrm(ks[1], (BATCH, N_MEM, D_MODEL), 1.0),
        'mem_norm': gain(ks[2], (D_MODEL,)),
        'norm_pre_mix': gain(ks[3], (DEPTH, D_MODEL)),
        'norm_post_mix': gain(ks[4], (DEPTH, D_MODEL)),
        'norm_pre_mlp': gain(ks[5], (DEPTH, D_MODEL)),
        'norm_post_mlp': gain(ks[6], (DEPTH, D_MODEL)),
        'w_in_a': nrm(ks[7], (N_A_LAYERS, D_MODEL, IN_A), D_MODEL ** -0.5),
        'conv_w_a': nrm(ks[8], (N_A_LAYERS, CONV_WIDTH, 3 * SEQ_MIX_WIDTH), CONV_WIDTH ** -0.5),
        'a_log_a': jnp.log(jax.random.uniform(ks[9], (N_A_LAYERS, N_LIN_HEADS), f32, 0.01, 1.0)),
        'dt_bias_a': nrm(ks[10], (N_A_LAYERS, N_LIN_HEADS), 0.1),
        'onorm_a': gain(ks[11], (N_A_LAYERS, LIN_HEAD_DIM)),
        'w_in_b': nrm(ks[12], (N_B_LAYERS, D_MODEL, IN_B), D_MODEL ** -0.5),
        'w_mem_kv': nrm(ks[13], (DEPTH, D_MODEL, 2 * X_WIDTH), D_MODEL ** -0.5),
        'w_out': nrm(ks[14], (DEPTH, MIX_WIDTH, D_MODEL), MIX_WIDTH ** -0.5),
        'w_up': nrm(ks[15], (DEPTH, D_MODEL, D_FF), D_MODEL ** -0.5),
        'w_down': nrm(ks[16], (DEPTH, D_FF, D_MODEL), D_FF ** -0.5),
    }

def first_block(x, mem, mem_norm, norm_pre_mix, norm_post_mix, norm_pre_mlp, norm_post_mlp,
              w_in_a, conv_w_a, a_log_a, dt_bias_a, onorm_a, w_in_b, w_mem_kv, w_out,
              w_up, w_down):
    B, S, _ = x.shape
    mem_n = rms_norm(mem, mem_norm)
    for i in range(DEPTH):
        j = i // N_MIXERS
        h = rms_norm(x, norm_pre_mix[i])
        if i % N_MIXERS == 0:
            proj = h @ w_in_a[j]
            mix = gated_deltanet(proj[..., :IN_A - X_WIDTH], conv_w_a[j], a_log_a[j],
                                 dt_bias_a[j], onorm_a[j])
            mem_q = proj[..., IN_A - X_WIDTH:]
        else:
            proj = h @ w_in_b[j]
            W = SEQ_MIX_WIDTH
            q = proj[..., :W].reshape(B, S, N_SB_HEADS, SB_HEAD_DIM)
            k = proj[..., W:2 * W].reshape(B, S, N_SB_HEADS, SB_HEAD_DIM)
            v = proj[..., 2 * W:3 * W].reshape(B, S, N_SB_HEADS, SB_HEAD_DIM)
            mix = stick_breaking_attention(q, k, v)
            mem_q = proj[..., 3 * W:]
        cross = memory_attention(mem_q, mem_n @ w_mem_kv[i])
        y = jnp.concatenate([mix.astype(x.dtype), cross.astype(x.dtype)], axis=-1) @ w_out[i]
        x = x + rms_norm(y, norm_post_mix[i])
        h = rms_norm(x, norm_pre_mlp[i])
        y = jnp.square(jax.nn.relu(h @ w_up[i])) @ w_down[i]
        x = x + rms_norm(y, norm_post_mlp[i])
    return x


DEPTH_2 = 1

MEM_LEN = 256
POOL_WIDTH = D_MODEL // 2
POOL_WINDOWS = (2, 4, 8, 16)
POOL_GROUPS = len(POOL_WINDOWS)
POOL_GROUP_WIDTH = POOL_WIDTH // POOL_GROUPS
DIFF_HEADS = 4
DIFF_HEAD_DIM = 64
DIFF_V_DIM = 2 * DIFF_HEAD_DIM
Q_WIDTH = DIFF_HEADS * 2 * DIFF_HEAD_DIM
ATTN_WIDTH = DIFF_HEADS * DIFF_V_DIM
MIX_WIDTH_2 = POOL_WIDTH + ATTN_WIDTH
IN_PROJ_WIDTH = POOL_WIDTH + 2 * Q_WIDTH + ATTN_WIDTH + MIX_WIDTH_2
Q_BLOCK = 128
ROPE_THETA = 10000.0
CROSS_HEADS = 4
CROSS_HEAD_DIM = D_MODEL // CROSS_HEADS
D_FF_2 = 4 * D_MODEL
NORM_EPS = 1e-6
NEG_BIG = -1e30


def rms_norm_2(x, g):
    xf = x.astype(jnp.float32)
    y = xf * lax.rsqrt(jnp.mean(xf * xf, axis=-1, keepdims=True) + NORM_EPS)
    return (y * g.astype(jnp.float32)).astype(x.dtype)

def lambda_init_fn(layer_idx):
    return 0.8 - 0.6 * math.exp(-0.3 * layer_idx)

def apply_rope(t):
    S = t.shape[1]
    dh = t.shape[-1]
    inv_freq = ROPE_THETA ** (-jnp.arange(0, dh, 2, dtype=jnp.float32) / dh)
    ang = jnp.arange(S, dtype=jnp.float32)[:, None] * inv_freq[None, :]
    cos = jnp.cos(ang)[None, :, None, None, :].astype(t.dtype)
    sin = jnp.sin(ang)[None, :, None, None, :].astype(t.dtype)
    t1, t2 = jnp.split(t, 2, axis=-1)
    return jnp.concatenate([t1 * cos - t2 * sin, t2 * cos + t1 * sin], axis=-1)

def causal_multiscale_pool(u, w_pool, pool_scale):
    B, S, _ = u.shape
    ug = u.reshape(B, S, POOL_GROUPS, POOL_GROUP_WIDTH)
    pos = jnp.arange(S)
    outs = []
    for g, w in enumerate(POOL_WINDOWS):
        xg = ug[:, :, g].astype(jnp.float32)
        c = jnp.cumsum(xg, axis=1)
        lag = jnp.pad(c, ((0, 0), (w, 0), (0, 0)))[:, :S]
        cnt = jnp.minimum(pos + 1, w).astype(jnp.float32)[None, :, None]
        outs.append((c - lag) / cnt - xg)
    z = jnp.stack(outs, axis=2).astype(u.dtype)
    y = jnp.einsum('bsgc,gcd->bsgd', z, w_pool).reshape(B, S, POOL_WIDTH)
    return y * pool_scale

def diff_attention(q, k, v, lam):
    B, S, H, _, Dh = q.shape
    E = v.shape[-1]
    nb = S // Q_BLOCK
    scale = Dh ** -0.5
    qb = q.reshape(B, nb, Q_BLOCK, H, 2, Dh).transpose(1, 0, 2, 3, 4, 5)
    kpos = jnp.arange(S)

    def one_block(args):
        q_blk, i = args
        qpos = i * Q_BLOCK + jnp.arange(Q_BLOCK)
        s = jnp.einsum('bqhcd,bkhcd->bhcqk', q_blk, k,
                       preferred_element_type=jnp.float32) * scale
        mask = kpos[None, :] <= qpos[:, None]
        p = jax.nn.softmax(jnp.where(mask, s, NEG_BIG), axis=-1)
        a = p[:, :, 0] - lam * p[:, :, 1]
        return jnp.einsum('bhqk,bkhe->bqhe', a.astype(v.dtype), v)

    o = lax.map(one_block, (qb, jnp.arange(nb)))
    return o.transpose(1, 0, 2, 3, 4).reshape(B, S, H, E)

def memory_cross_attention(h, mem_n, w_cq, w_ckv, w_co):
    B, S, _ = h.shape
    M = mem_n.shape[1]
    q = (h @ w_cq).reshape(B, S, CROSS_HEADS, CROSS_HEAD_DIM)
    kv = (mem_n @ w_ckv).reshape(B, M, 2, CROSS_HEADS, CROSS_HEAD_DIM)
    k, v = kv[:, :, 0], kv[:, :, 1]
    s = jnp.einsum('bshd,bmhd->bhsm', q, k,
                   preferred_element_type=jnp.float32) * CROSS_HEAD_DIM ** -0.5
    p = jax.nn.softmax(s, axis=-1).astype(v.dtype)
    o = jnp.einsum('bhsm,bmhd->bshd', p, v).reshape(B, S, D_MODEL)
    return o @ w_co

def second_inputs(seed: int = 0) -> dict:
    key = jax.random.key(seed)
    ks = jax.random.split(key, 24)
    f32 = jnp.float32

    def nrm(k, shape, scale):
        return jax.random.normal(k, shape, f32) * scale

    def gain(k, shape):
        return 1.0 + 0.02 * jax.random.normal(k, shape, f32)

    L = DEPTH_2
    return {
        "x": jax.random.normal(ks[0], (BATCH, SEQ, D_MODEL), f32),
        "mem": jax.random.normal(ks[1], (BATCH, MEM_LEN, D_MODEL), f32),
        "g_mix": gain(ks[2], (L, D_MODEL)),
        "w_in": nrm(ks[3], (L, D_MODEL, IN_PROJ_WIDTH), D_MODEL ** -0.5),
        "w_pool": nrm(ks[4], (L, POOL_GROUPS, POOL_GROUP_WIDTH, POOL_GROUP_WIDTH), POOL_GROUP_WIDTH ** -0.5),
        "pool_scale": gain(ks[5], (L, POOL_WIDTH)),
        "lambda_q1": nrm(ks[6], (L, DIFF_HEAD_DIM), 0.1),
        "lambda_k1": nrm(ks[7], (L, DIFF_HEAD_DIM), 0.1),
        "lambda_q2": nrm(ks[8], (L, DIFF_HEAD_DIM), 0.1),
        "lambda_k2": nrm(ks[9], (L, DIFF_HEAD_DIM), 0.1),
        "g_subln": gain(ks[10], (L, DIFF_V_DIM)),
        "w_out": nrm(ks[11], (L, MIX_WIDTH_2, D_MODEL), MIX_WIDTH_2 ** -0.5),
        "g_cross": gain(ks[12], (L, D_MODEL)),
        "g_mem": gain(ks[13], (L, D_MODEL)),
        "w_cq": nrm(ks[14], (L, D_MODEL, D_MODEL), D_MODEL ** -0.5),
        "w_ckv": nrm(ks[15], (L, D_MODEL, 2 * D_MODEL), D_MODEL ** -0.5),
        "w_co": nrm(ks[16], (L, D_MODEL, D_MODEL), D_MODEL ** -0.5),
        "g_mlp": gain(ks[17], (L, D_MODEL)),
        "w_up": nrm(ks[18], (L, D_MODEL, D_FF_2), D_MODEL ** -0.5),
        "w_down": nrm(ks[19], (L, D_FF_2, D_MODEL), D_FF_2 ** -0.5),
        "g_final": gain(ks[20], (D_MODEL,)),
    }

def second_block(x, mem, g_mix, w_in, w_pool, pool_scale, lambda_q1, lambda_k1,
              lambda_q2, lambda_k2, g_subln, w_out, g_cross, g_mem, w_cq, w_ckv,
              w_co, g_mlp, w_up, w_down, g_final):
    B, S, _ = x.shape
    splits = [POOL_WIDTH, POOL_WIDTH + Q_WIDTH, POOL_WIDTH + 2 * Q_WIDTH,
              POOL_WIDTH + 2 * Q_WIDTH + ATTN_WIDTH]
    for l in range(DEPTH_2):
        lam_init = lambda_init_fn(l)
        h = rms_norm_2(x, g_mix[l])
        proj = h @ w_in[l]
        u, q, k, v, gate_logits = jnp.split(proj, splits, axis=-1)
        y_pool = causal_multiscale_pool(u, w_pool[l], pool_scale[l])
        q = apply_rope(q.reshape(B, S, DIFF_HEADS, 2, DIFF_HEAD_DIM))
        k = apply_rope(k.reshape(B, S, DIFF_HEADS, 2, DIFF_HEAD_DIM))
        v = v.reshape(B, S, DIFF_HEADS, DIFF_V_DIM)
        lam = (jnp.exp(jnp.sum(lambda_q1[l].astype(jnp.float32) * lambda_k1[l].astype(jnp.float32)))
               - jnp.exp(jnp.sum(lambda_q2[l].astype(jnp.float32) * lambda_k2[l].astype(jnp.float32)))
               + lam_init)
        o = diff_attention(q, k, v, lam)
        o = rms_norm_2(o, g_subln[l]) * (1.0 - lam_init)
        y_attn = o.reshape(B, S, ATTN_WIDTH)
        gates = jax.nn.sigmoid(gate_logits.astype(jnp.float32)).astype(x.dtype)
        mixed = jnp.concatenate([y_pool, y_attn], axis=-1) * gates
        x = x + mixed @ w_out[l]
        hc = rms_norm_2(x, g_cross[l])
        mem_n = rms_norm_2(mem, g_mem[l])
        x = x + memory_cross_attention(hc, mem_n, w_cq[l], w_ckv[l], w_co[l])
        hm = rms_norm_2(x, g_mlp[l])
        x = x + jnp.square(jax.nn.relu(hm @ w_up[l])) @ w_down[l]
    return rms_norm_2(x, g_final)


def setup_inputs(seed=0):
    out = dict(first_inputs(seed))
    for name, value in second_inputs(seed + 1).items():
        if name != "x":
            out[name + "_2"] = value
    return out


def reference(
    x, mem, mem_norm, norm_pre_mix, norm_post_mix, norm_pre_mlp, norm_post_mlp, w_in_a,
    conv_w_a, a_log_a, dt_bias_a, onorm_a, w_in_b, w_mem_kv, w_out, w_up, w_down, mem_2,
    g_mix_2, w_in_2, w_pool_2, pool_scale_2, lambda_q1_2, lambda_k1_2, lambda_q2_2, lambda_k2_2,
    g_subln_2, w_out_2, g_cross_2, g_mem_2, w_cq_2, w_ckv_2, w_co_2, g_mlp_2, w_up_2, w_down_2,
    g_final_2,
):
    x = first_block(
        x, mem, mem_norm, norm_pre_mix, norm_post_mix, norm_pre_mlp, norm_post_mlp, w_in_a,
        conv_w_a, a_log_a, dt_bias_a, onorm_a, w_in_b, w_mem_kv, w_out, w_up, w_down,
    )
    return second_block(
        x, mem_2, g_mix_2, w_in_2, w_pool_2, pool_scale_2, lambda_q1_2, lambda_k1_2,
        lambda_q2_2, lambda_k2_2, g_subln_2, w_out_2, g_cross_2, g_mem_2, w_cq_2, w_ckv_2,
        w_co_2, g_mlp_2, w_up_2, w_down_2, g_final_2,
    )


_drawn_inputs = setup_inputs


def setup_inputs(seed=0):
    import zlib

    import numpy as np

    out = dict(_drawn_inputs(seed))
    spreads = {}
    factors = {'mem_norm': 3.485,
     'dt_bias_a': 8.0,
     'g_mix_2': 8.0,
     'pool_scale_2': 8.0,
     'lambda_q1_2': 8.0,
     'lambda_k1_2': 8.0,
     'lambda_q2_2': 4.113,
     'lambda_k2_2': 8.0,
     'g_subln_2': 34.511,
     'g_cross_2': 8.0,
     'g_mem_2': 8.0,
     'g_mlp_2': 16.411,
     'g_final_2': 8.03}
    for name, (base, spread) in spreads.items():
        noise = np.random.default_rng([zlib.crc32(name.encode()), seed]).standard_normal(out[name].shape)
        drawn = base * np.exp(spread * noise) if base else spread * noise
        out[name] = jnp.asarray(drawn.astype(out[name].dtype))
    for name, factor in factors.items():
        out[name] = (out[name] * factor).astype(out[name].dtype)
    return out
```

```python
import numpy as np
import concourse.bass as bass
from concourse import mybir
from contextlib import ExitStack

F32 = mybir.dt.float32
F32R = mybir.dt.float32r
ALU = mybir.AluOpType
ACT = mybir.ActivationFunctionType
AX = mybir.AxisListType

P = 128
S = 512
D = 1024
KD = D // P
NB = S // P
MEM = 256
MB = MEM // P
W = 768
NT = W // P
H_LIN = 6
UC = 256
EPS = 1e-6
FF = 4096
QUARTERS = FF // D

PHASES = [
    ("A.mem", 2, "act"), ("B.mem", 2, "act"),
    ("A.qkv", 9, "dve"), ("A.memq", 1, "dve"), ("A.bg", 1, "dve"), ("A.gate", 3, "dve"),
    ("A.out", 4, "act"), ("A.mlp", 32, "dve"),
    ("B.qk", 6, "dve"), ("B.v", 3, "dve"), ("B.memq", 1, "dve"), ("B.out", 4, "act"), ("B.mlp", 32, "dve"),
    ("C.u", 2, "dve"), ("C.qk", 4, "dve"), ("C.v", 2, "dve"), ("C.gate", 4, "dve"), ("C.out", 4, "dve"),
    ("C.mem", 8, "act"), ("C.cq", 4, "dve"), ("C.co", 4, "dve"), ("C.mlp", 32, "dve"),
]
U0, NU, KIND = {}, {}, []
for _name, _n, _kind in PHASES:
    U0[_name], NU[_name] = len(KIND), _n
    KIND += [_kind] * _n
UNITS = len(KIND)
EMPTIED = {k: [2 * KIND[:u].count(k) for u in range(UNITS + 1)] for k in ("act", "dve")}

SPLITS = ["mem", "A.in", "A.mix", "A.mlp", "B.in", "B.mix", "B.mlp", "C.in", "C.mix", "mem2", "C.cross", "C.att", "C.mlp"]
SUMS = ["mem", "A.in", "A.post", "A.mlp", "A.post2", "B.in", "B.post", "B.mlp", "B.post2", "C.in", "mem2",
        "C.cross", "C.mlp", "final"]

PARAMS = [("mem_norm", KD), ("pre_mix0", KD), ("pre_mix1", KD), ("post_mix0", KD), ("post_mix1", KD),
          ("pre_mlp0", KD), ("pre_mlp1", KD), ("post_mlp0", KD), ("post_mlp1", KD),
          ("g_mix", KD), ("g_cross", KD), ("g_mem", KD), ("g_mlp", KD), ("g_final", KD),
          ("conv", 18 * 4), ("a_log", 24), ("dt", 24), ("onorm", 1), ("pool_scale", 4), ("g_subln", 1),
          ("lq1", 64), ("lk1", 64), ("lq2", 64), ("lk2", 64), ("w_pool", 4 * P)]
PCOL, _at = {}, 0
for _name, _n in PARAMS:
    PCOL[_name] = _at
    _at += _n
NPAR = _at

CONSTS = [("ident", P), ("tri_le", P), ("strict", P), ("cap", P), ("neg_tri", P), ("neg_ones", P), ("ones", P),
          ("level", 7 * P), ("causal_add", P), ("swap", P)]
CCOL, _at = {}, 0
for _name, _n in CONSTS:
    CCOL[_name] = _at
    _at += _n
NCON = _at

SB_OFF = [0, 512, 1024, 896]
SB_WID = [512, 384, 256, 128]
SB_ALL = 1280
DF_OFF = [896, 1024, 512, 0]
DF_WID = [128, 256, 384, 512]
LAM_INIT = 0.8 - 0.6


SEMAPHORES = """
at bc bcast_mm bg bg_tr bt cb_zero const_in conv conv0 df_a df_at df_bc df_bs df_exp df_mask df_max
df_nm df_o df_p1 df_ri df_rs df_rt df_s df_sq df_ss df_tr df_w dt_exp dt_pre dtm eg_exp emptied_act
emptied_dve eps gate_silu gated gc_mm head_sc hh hi hl kbt  kn kv_t kv_tr l2rt l2sq l2ss
lam lam_act lo load0 load1 lt lt_mm lv_p lv_x lv_y lv_yc ma_exp ma_max ma_nm ma_o ma_out ma_p ma_pt
ma_ri ma_s ma_tr mem2_in mem_in mixed o_done obc obs ors ort osq oss out_dma out_ready pool_mm
pool_ms pool_s pool_z q_scaled qd qn rcnt_in rk rope_cos rope_done rope_in rope_mm rope_sin rows rq
rs rsc rv sb_a sb_az sb_cap sb_e sb_l sb_m sb_o sb_rc sb_sp sb_t sb_z sc_act sc_dve sc_o sc_ws sig silu
sq sqa sqrt ss st tile u_mm u_sb uh ul v_copy vn vrow vtr w_sb x_in x_new y_scaled y_zero
"""


def program(nc, ws, xt_in, memt_in, memt2_in, par_in, con_in, rope_in, rcnt_in, out, stop=None):
    ctx = ExitStack()
    with ctx:
        def sb(name, shape, dt=F32, scope=ctx):
            return scope.enter_context(nc.sbuf_tensor(name, shape, dt))

        sems = {}

        for name in SEMAPHORES.split():
            sems[name] = ctx.enter_context(nc.semaphore(name))

        XT = sb("XT", [P, KD, S])
        HH = sb("HH", [P, KD, S], F32R)
        HL = sb("HL", [P, KD, S], F32R)
        STG = [sb(f"STG{i}", [P, KD, UC]) for i in range(2)]
        WH = [sb(f"WH{i}", [P, KD, UC], F32R) for i in range(2)]
        WL = [sb(f"WL{i}", [P, KD, UC], F32R) for i in range(2)]
        Y = sb("Y", [P, KD, S])
        SQ = sb("SQ", [P, 4, S])
        SQA = sb("SQA", [P, S])
        RS = sb("RS", [P, S])
        RT = sb("RT", [P, NB])
        RSC = sb("RSC", [P, NB])
        CON = sb("CON", [P, NCON])
        PAR = sb("PAR", [P, NPAR])
        EPST = sb("EPST", [P, 1])
        ONE1 = sb("ONE1", [P, 1])
        KT_MEM = [sb(f"KT_MEM{i}", [P, 2, MEM]) for i in range(2)]
        V_MEM = [sb(f"V_MEM{i}", [P, MB, UC]) for i in range(2)]
        MST = sb("MST", [P, 2, 4, NB])
        PS = ctx.enter_context(nc.psum_tensor("PS", [P, 8, 512], F32))
        PSF = PS[:, :, :].rearrange("p b n -> p (b n)")

        def con(name, width=P):
            return CON[:, CCOL[name]:CCOL[name] + width]

        def par(name, i=0, n=1):
            return PAR[:, PCOL[name] + i:PCOL[name] + i + n]

        def tile(t, i):
            if isinstance(i, int):
                return t[:, i, :]
            return t[:, bass.ds(i, 1), :].rearrange("p a n -> p (a n)")

        with ExitStack() as sc:
            MX = sb("MX", [P, KD, MEM], scope=sc)
            MH = sb("MH", [P, KD, MEM], F32R, scope=sc)
            ML = sb("ML", [P, KD, MEM], F32R, scope=sc)
            KR = sb("KR", [P, MB, UC], scope=sc)
        with ExitStack() as sc:
            QKV = sb("QKV", [P, 3 * NT, S], scope=sc)
            MQ = sb("MQ", [P, 2, S], scope=sc)
            CX = sb("CX", [P, 2, S], scope=sc)
            BGT = sb("BGT", [12, S], scope=sc)
            BG = sb("BG", [P, 12, NB], scope=sc)
            SC = sb("SC", [P, H_LIN, 8, NB], scope=sc)
            SMALL = sb("SMALL", [P, 8, 24], scope=sc)
            RQK = sb("RQK", [P, 2 * NT, NB], scope=sc)
            HS = [sb(f"HS{i}", [P, 8, NB], scope=sc) for i in range(2)]
            ORT = [sb(f"ORT{i}", [P, 2, NB], scope=sc) for i in range(2)]
            ST8 = [sb(f"ST8{i}", [P, P], scope=sc) for i in range(2)]
            VN = [sb(f"VN{i}", [P, P], scope=sc) for i in range(2)]
            TMP = [[sb(f"TMP{i}_{j}", [P, S], scope=sc) for j in range(3)] for i in range(2)]
        with ExitStack() as sc:
            UPH = sb("UPH", [P, KD, S], F32R, scope=sc)
            UPL = sb("UPL", [P, KD, S], F32R, scope=sc)
            RR = sb("RR", [P, 2, S], scope=sc)
            RQ = sb("RQ", [P, 2, S], scope=sc)
        with ExitStack() as sc:
            QKB = sb("QKB", [P, 2 * NT, S], scope=sc)
            QB, KB = QKB[:, 0:NT, :], QKB[:, NT:2 * NT, :]
            MO = sb("MO", [P, 2, S], scope=sc)
            VB = sb("VB", [P, NT, NB, P], scope=sc)
            MQB = sb("MQB", [P, 2, S], scope=sc)
            TAIL = sb("TAIL", [P, 2, 640], scope=sc)
            ABUF = sb("ABUF", [P, SB_ALL], scope=sc)
        with ExitStack() as sc:
            QC = sb("QC", [P, 4, S], scope=sc)
            KC = sb("KC", [P, 4, S], scope=sc)
            VC = sb("VC", [P, 4, NB, P], scope=sc)
            UT = sb("UT", [P, 4, 16 + S], scope=sc)
            GC_ = sb("GC_", [P, KD, S], scope=sc)
            COSIN = sb("COSIN", [P, 2, S], scope=sc)
            LAM = sb("LAM", [P, 8], scope=sc)
            PA = sb("PA", [P, 2, 16 + S], scope=sc)
            DST = sb("DST", [P, 2, 2, NB], scope=sc)
            DMX = sb("DMX", [P, 2, 2, NB], scope=sc)
        with ExitStack() as sc:
            CQ = sb("CQ", [P, KD, S], scope=sc)
            MX2 = sb("MX2", [P, KD, MEM], scope=sc)
            MH2 = sb("MH2", [P, KD, MEM], F32R, scope=sc)
            ML2 = sb("ML2", [P, KD, MEM], F32R, scope=sc)
            CK = sb("CK", [P, KD, MEM], scope=sc)
            CV = sb("CV", [P, MB, D], scope=sc)

        YF = Y[:, :, :].rearrange("p k n -> p (k n)")
        CONV_IN = [YF[:, 0:515], YF[:, 520:1035]]
        CONV_ACC = [YF[:, 1040:1552], YF[:, 1560:2072]]
        PROB = [YF[:, 1024 * e:1024 * e + 1024] for e in range(2)]
        PROBT = [YF[:, 2048 + 1024 * e:3072 + 1024 * e] for e in range(2)]
        SP = [YF[:, SB_ALL * e:SB_ALL * (e + 1)] for e in range(2)]
        AW = [ABUF[:, :], YF[:, 2 * SB_ALL:3 * SB_ALL]]
        DP = [YF[:, SB_ALL * c:SB_ALL * (c + 1)] for c in range(2)]
        DAT = YF[:, 2 * SB_ALL:3 * SB_ALL]
        RCNT = Y[:, 4:8, :]
        T9 = [[Y[:, 4 * e + i, :] for i in range(4)] + [SQ[:, 2 * e + i, :] for i in range(2)] +
              [TMP[e][i][:, :] for i in range(3)] for e in range(2)]
        KNS, KBT, DT, LT, AT, XTr, BT, RK, KDC = ([T9[e][i] for e in range(2)] for i in range(9))
        WT, XX, YT, VS, EG = KNS, KBT, DT, XTr, KDC

        def blk(ap, b, n=P):
            return ap[:, b * n:(b + 1) * n]

        def blocks(ap):
            return ap.rearrange("p (b n) -> p b n", b=NB)

        def lin(base, step, i):
            return base if i is None else i * step + base

        def bc_blocks(ap):
            return ap.unsqueeze(1).to_broadcast([P, NB, P])

        def per_block(ap):
            return ap.unsqueeze(2).to_broadcast([P, NB, P])

        def segments(name):
            u, n = U0[name], NU[name]
            head = n if n < 6 or name.endswith("mlp") else 2 + n % 2
            out_ = [(u + r, None) for r in range(head)]
            if head < n:
                out_.append((u + head, (n - head) // 2))
            return out_

        def run_phase(eng, name, fn):
            for u, pairs in segments(name):
                if pairs is None:
                    fn(u, None, 0)
                else:
                    with eng.Fori(0, pairs) as i:
                        fn(u, i, 2)
                        fn(u + 1, i, 2)

        def emptied(kind, u, j, i=None, step=0):
            return lin(EMPTIED[kind][u] + j + 1, 2 * step, i)

        SQ_BASE = {name: 8 * n for n, name in enumerate(SUMS)}
        NORMS = [n for n in SUMS if not n.startswith("mem")]

        def sums_done(n):
            return SUMS.index(n) + 1

        def bcast_done(n):
            return NORMS.index(n) + 1

        def split_done(q, k):
            return 8 * SPLITS.index(q) + k + 1

        def added(m):
            return 7 * (m // 8) + max(m % 8, 1)

        POSTS = ["A.post", "A.post2", "B.post", "B.post2"]
        VIDX = {"B.v": 0, "C.v": 6}

        block = ctx.enter_context(nc.Block())

        @block.sync
        def _(sp):
            for v in range(2):
                sp.dma_start(STG[v][:, :, :].rearrange("p k n -> p (k n)"), ws[v]).then_inc(sems[f"load{v}"], 16)
            with sp.Fori(1, UNITS // 2) as i:
                for j in range(2):
                    sp.wait_ge(sems["lo"], lin(j - 1, 2, i))
                    sp.dma_start(STG[j][:, :, :].rearrange("p k n -> p (k n)"),
                                 ws[bass.ds(i * 2 + j, 1)].rearrange("a p n -> p (a n)")).then_inc(sems[f"load{j}"], 16)
            for k in range(KD):
                sp.wait_ge(sems["out_ready"], k + 1)
                sp.dma_start(out[k * P:(k + 1) * P, :], Y[:, k, :]).then_inc(sems["out_dma"], 16)
            sp.wait_ge(sems["out_dma"], 16 * KD)

        @block.gpsimd
        def _(pool):
            pool.memset(EPST[:, :], EPS).then_inc(sems["eps"], 1)
            pool.memset(ONE1[:, :], 1.0).then_inc(sems["eps"], 1)
            for e in range(2):
                pool.memset(CONV_IN[e][:, 0:3], 0.0).then_inc(sems["cb_zero"], 1)

            def sum_squares(name, n=S):
                base = SQ_BASE[name]
                a0 = 7 * SUMS.index(name)
                for k in range(1, KD):
                    pool.wait_ge(sems["sq"], base + k + 1)
                    if k == 1:
                        if a0:
                            pool.wait_ge(sems["ss"], SUMS.index(name))
                        pool.tensor_tensor(SQA[:, 0:n], SQ[:, base % 4, 0:n], SQ[:, (base + 1) % 4, 0:n],
                                           ALU.add).then_inc(sems["sqa"], 1)
                    else:
                        pool.wait_ge(sems["sqa"], a0 + k - 1)
                        pool.tensor_tensor(SQA[:, 0:n], SQA[:, 0:n], SQ[:, (base + k) % 4, 0:n],
                                           ALU.add).then_inc(sems["sqa"], 1)

            def add_to_stream(name):
                for k in range(KD):
                    pool.wait_ge(sems["y_scaled"], 8 * POSTS.index(name) + k + 1)
                    pool.tensor_tensor(XT[:, k, :], XT[:, k, :], Y[:, k, :], ALU.add).then_inc(sems["x_new"], 1)

            def zero_y(L):
                pool.wait_ge(sems["x_new"], 16 * L + 8)
                pool.memset(Y[:, :, :], 0.0).then_inc(sems["y_zero"], 1)

            sum_squares("mem", MEM)
            sum_squares("A.in")
            with pool.Fori(0, H_LIN // 2) as g:
                for e in range(2):
                    pool.wait_ge(sems["lt"], lin(e + 1, 2, g))
                for lv in range(7):
                    for e in range(2):
                        if lv:
                            pool.wait_ge(sems["lv_y"], lin(2 * (lv - 1) + e + 1, 14, g))
                            if lv == 1:
                                pool.wait_ge(sems["lv_x"], lin(e + 1, 14, g))
                        pool.tensor_tensor(blocks(BT[e]), blocks(LT[e]), bc_blocks(con("level", 7 * P)[:, lv * P:(lv + 1) * P]),
                                           ALU.mult).then_inc(sems["bt"], 1)
                for e in range(2):
                    pool.wait_ge(sems["o_done"], lin(e + 1, 2, g))
            sum_squares("A.post")
            add_to_stream("A.post")
            zero_y(0)
            sum_squares("A.mlp")
            sum_squares("A.post2")
            add_to_stream("A.post2")
            sum_squares("B.in")
            sum_squares("B.post")
            add_to_stream("B.post")
            zero_y(1)
            sum_squares("B.mlp")
            sum_squares("B.post2")
            add_to_stream("B.post2")
            pool.wait_ge(sems["emptied_dve"], emptied("dve", U0["B.mlp"] + 31, 1))
            pool.dma_start(COSIN[:, :, :], rope_in).then_inc(sems["rope_in"], 16)
            sum_squares("C.in")
            pool.wait_ge(sems["x_new"], 32)
            pool.dma_start(RCNT, rcnt_in).then_inc(sems["rcnt_in"], 16)
            pool.wait_ge(sems["hl"], split_done("C.mix", 7))
            pool.dma_start(MX2[:, :, :], memt2_in).then_inc(sems["mem2_in"], 16)
            sum_squares("mem2", MEM)
            sum_squares("C.cross")
            sum_squares("C.mlp")
            sum_squares("final")

        @block.tensor
        def _(pe):
            I_ = con("ident")

            def mm(o, l, r, start, stop, **kw):
                return pe.matmul(o, l, r, start=start, stop=stop, **kw)

            def sum_tokens(name, nt=NB):
                pe.wait_ge(sems["sqa"], 7 * sums_done(name))
                before = sum(1 for x in NORMS if SUMS.index(x) < SUMS.index(name))
                if before:
                    pe.wait_ge(sems["rs"], before)
                for b in range(nt):
                    last = mm(PS[:, 4, b:b + 1], blk(SQA[:, :], b), con("ones")[:, 0:1], True, True)
                last.then_inc(sems["ss"], 1)

            def spread_tokens(name):
                pe.wait_ge(sems["rsc"], sums_done(name))
                for b in range(NB):
                    last = mm(PS[:, 4, b * P:(b + 1) * P], RSC[:, b:b + 1].to_broadcast([P, P]), I_, True, True)
                last.then_inc(sems["bc"], 1)

            def wait_bank(u, j, i=None, step=0):
                if u >= 2:
                    kind = KIND[u - 2]
                    pe.wait_ge(sems[f"emptied_{kind}"], emptied(kind, u - 2, j, i, step))

            def product(u, i, step, xh, xl, split=None, between=None, tiles=2, ready="hl"):
                s = u % 2
                pe.wait_ge(sems["lo"], lin(u + 1, step, i))

                def step_k(j, k):
                    bank = PS[:, 2 * s + j, :]
                    wh, wl = WH[s][:, k, j * P:(j + 1) * P], WL[s][:, k, j * P:(j + 1) * P]
                    mm(bank, wh, xh[:, k, :], k == 0, False)
                    mm(bank, wh, xl[:, k, :], False, False)
                    return mm(bank, wl, xh[:, k, :], False, k == KD - 1)

                if split is not None:
                    wait_bank(u, 0, i, step)
                    wait_bank(u, 1, i, step)
                    for k in range(KD):
                        pe.wait_ge(sems[ready], split(k))
                        for j in range(2):
                            last = step_k(j, k)
                            if k == KD - 1:
                                last.then_inc(sems["tile"], 1)
                    return
                for j in range(tiles):
                    wait_bank(u, j, i, step)
                    for k in range(KD):
                        last = step_k(j, k)
                    last.then_inc(sems["tile"], 3 - tiles)
                    if between and j == 0:
                        between()

            def projection(name, split=None, norm=None, after=None):
                def fn(u, i, step):
                    r = u - U0[name]
                    first = r == 0 and i is None
                    product(u, i, step, HH, HL,
                            split=(lambda k: split_done(split, k)) if first and split else None,
                            between=(lambda: spread_tokens(norm)) if norm and r == 1 and i is None else None,
                            tiles=1 if name == "A.bg" else 2)
                    if norm and first:
                        sum_tokens(norm)
                    if after and r:
                        after(r - 1)
                run_phase(pe, name, fn)
                if after:
                    after(NU[name] - 1)

            def memory_rows(name, xh, xl, r, split=None):
                u = U0[name] + 2 * r
                pe.wait_ge(sems["lo"], u + 2)
                for t in range(MB):
                    wait_bank(u + t, 0)
                    for k in range(KD):
                        if split is not None and t == 0:
                            pe.wait_ge(sems["hl"], split_done(split, k))
                        bank = PS[:, 2 * t, :].rearrange("p (a n) -> p a n", a=2)
                        xs = slice(t * P, (t + 1) * P)
                        for a in range(2):
                            mm(bank[:, a, :], xh[:, k, xs], WH[a][:, k, :], k == 0 and a == 0, False, skip_group_check=True)
                            mm(bank[:, a, :], xl[:, k, xs], WH[a][:, k, :], False, False, skip_group_check=True)
                            last = mm(bank[:, a, :], xh[:, k, xs], WL[a][:, k, :], False, k == KD - 1, skip_group_check=True)
                    last.then_inc(sems["tile"], 2)

            def memory_attention(a, q, k, v, chunks, dh):
                def scores(h):
                    e = h % 2
                    if h >= 2:
                        pe.wait_ge(sems["ma_out"], 4 * a + h - 1)
                    for b in range(NB):
                        for c in range(chunks):
                            last = mm(PSF[:, (4 * e) * 512 + b * MEM:(4 * e) * 512 + (b + 1) * MEM], blk(q(h, c), b), k(h, c),
                                      c == 0, c == chunks - 1)
                    last.then_inc(sems["ma_s"], 1)

                def weigh(h):
                    e = h % 2
                    pe.wait_ge(sems["ma_p"], 4 * a + h + 1)
                    for b in range(NB):
                        for m in range(MB):
                            last = pe.transpose(PS[:, 4 * e + 2 + m, b * P:(b + 1) * P],
                                                PROB[e][:, b * MEM + m * P:b * MEM + (m + 1) * P], I_)
                    last.then_inc(sems["ma_tr"], 1)
                    pe.wait_ge(sems["ma_pt"], 4 * a + h + 1)
                    for c in range(chunks):
                        for m in range(MB):
                            o = PS[(h % 2) * 64:(h % 2) * 64 + 64, 4 * e, :] if dh == 64 else PS[:, 4 * e + c, :]
                            last = mm(o, v(h, c, m), blk(PROBT[e], m, 512), m == 0, m == MB - 1)
                    last.then_inc(sems["ma_o"], 1)

                scores(0)
                for h in range(4):
                    if h + 1 < 4:
                        scores(h + 1)
                    weigh(h)

            def turn_values(name):
                def fn(r):
                    for j in range(2):
                        t = 2 * r + j
                        vi = VIDX[name] + t
                        pe.wait_ge(sems["emptied_dve"], emptied("dve", U0[name] + r, j))
                        if vi >= 2:
                            pe.wait_ge(sems["vrow"], vi - 1)
                        for b in range(NB):
                            last = pe.transpose(PS[:, 5 + t % 2, b * P:(b + 1) * P], blk(Y[:, t % 2, :], b), I_)
                        last.then_inc(sems["vtr"], 1)
                return fn

            def mlp(L):
                name = "ABC"[L] + ".mlp"
                ub = U0[name]
                n4 = 4
                for r in range(n4):
                    product(ub + r, None, 0, HH, HL, split=(lambda k: split_done(name, k)) if r == 0 else None,
                            between=(lambda: spread_tokens(name)) if r == 1 else None)
                    if r == 0:
                        sum_tokens(name)
                with pe.Fori(0, QUARTERS - 1) as q:
                    for r in range(n4):
                        product(ub + 4 + r, q, 8, UPH, UPL, ready="ul",
                                split=(lambda k: lin(32 * L + k + 1, 8, q)) if r == 0 else None)
                    for r in range(n4):
                        product(ub + 8 + r, q, 8, HH, HL)
                for r in range(n4):
                    product(ub + 28 + r, None, 0, UPH, UPL, ready="ul",
                            split=(lambda k: 32 * L + 24 + k + 1) if r == 0 else None)

            def finish_post(name):
                sum_tokens(name)
                spread_tokens(name)

            def delta_net():
                def per(n, k, e, g):
                    return lin(2 * (k - 1) + e + 1, 2 * n, g)
                with pe.Fori(0, H_LIN // 2) as g:
                    for e in range(2):
                        pe.wait_ge(sems["head_sc"], per(1, 1, e, g))
                        for ty, (o, r) in enumerate([(0, con("tri_le")), (1, I_), (2, I_), (3, I_)]):
                            for b in range(NB):
                                last = mm(PS[:, 4 * e + o, b * P:(b + 1) * P],
                                          HS[e][:, ty, b:b + 1].to_broadcast([P, P]), r, True, True)
                        last.then_inc(sems["bcast_mm"], 1)
                    for e in range(2):
                        pe.wait_ge(sems["kbt"], per(1, 1, e, g))
                        for b in range(NB):
                            last = mm(PS[:, 4 * e + 1, b * P:(b + 1) * P], blk(KNS[e], b), blk(KBT[e], b), True, True)
                        last.then_inc(sems["lt_mm"], 1)
                        qn = QKV[:, bass.ds(g * 2 + e, 1), :].rearrange("p a n -> p (a n)")
                        for b in range(NB):
                            mm(PS[:, 4 * e + 2, b * P:(b + 1) * P], blk(KNS[e], b), blk(qn, b), True, True)
                        for b in range(NB):
                            pe.transpose(PS[:, 4 * e + 3, b * P:(b + 1) * P], blk(KNS[e], b), I_)
                        pe.wait_ge(sems["v_copy"], per(1, 1, e, g))
                        pe.wait_ge(sems["eg_exp"], per(1, 1, e, g))
                        pe.wait_ge(sems["dt_pre"], per(1, 1, e, g))
                        for b in range(NB):
                            last = pe.transpose(PS[:, 4 * e, b * P:(b + 1) * P], blk(VS[e], b), I_)
                        last.then_inc(sems["rows"], 1)
                    for lv in range(7):
                        for e in range(2):
                            pe.wait_ge(sems["bt"], lin(2 * lv + e + 1, 14, g))
                            if lv:
                                pe.wait_ge(sems["lv_x"], per(7, lv, e, g))
                            for b in range(NB):
                                last = mm(PS[:, 4 * e + 1, b * P:(b + 1) * P], blk(BT[e], b),
                                          blk(XX[e], b) if lv else I_, True, True)
                            last.then_inc(sems["lv_y"], 1)
                        if lv == 0:
                            continue
                        for e in range(2):
                            pe.wait_ge(sems["lv_yc"], per(6, lv, e, g))
                            if lv == 1:
                                pe.wait_ge(sems["rk"], per(1, 1, e, g))
                                pe.wait_ge(sems["at"], per(1, 1, e, g))
                            if lv < 6:
                                for b in range(NB):
                                    mm(PS[:, 4 * e + 2, b * P:(b + 1) * P], blk(XTr[e], b), blk(YT[e], b), True, True)
                            for b in range(NB):
                                last = mm(PS[:, 4 * e + 3, b * P:(b + 1) * P], blk(YT[e], b), blk(XTr[e], b), True, True)
                            last.then_inc(sems["lv_p"], 1)
                    for e in range(2):
                        pe.wait_ge(sems["lv_x"], per(7, 7, e, g))
                        pe.wait_ge(sems["rv"], per(1, 1, e, g))
                        rv = QKV[:, bass.ds(g * 2 + 12 + e, 1), :].rearrange("p a n -> p (a n)")
                        for b in range(NB):
                            mm(PS[:, 4 * e, b * P:(b + 1) * P], blk(XTr[e], b), blk(rv, b), True, True)
                        for b in range(NB):
                            last = mm(PS[:, 4 * e + 1, b * P:(b + 1) * P], blk(RK[e], b), blk(XTr[e], b), True, True)
                        last.then_inc(sems["u_mm"], 1)
                    for b in range(NB):
                        if b:
                            for e in range(2):
                                pe.wait_ge(sems["st"], per(3, b, e, g))
                                pe.wait_ge(sems["w_sb"], per(1, 1, e, g))
                                mm(PS[:, 4 * e + 2, 0:P], blk(WT[e], b), ST8[e][:, :], True, True).then_inc(sems["sc_ws"], 1)
                        for e in range(2):
                            qd = QKV[:, bass.ds(g * 2 + e, 1), :].rearrange("p a n -> p (a n)")
                            pe.wait_ge(sems["vn"], per(4, b + 1, e, g))
                            o = PS[:, 4 * e + 3, b * P:(b + 1) * P]
                            if b:
                                mm(o, ST8[e][:, :], blk(qd, b), True, False)
                            mm(o, VN[e][:, :], blk(AT[e], b), b == 0, True)
                            last = mm(PS[:, 4 * e + 2, P:2 * P], blk(KDC[e], b), VN[e][:, :], True, True)
                            last.then_inc(sems["sc_o"], 1)
                    for e in range(2):
                        pe.wait_ge(sems["osq"], per(1, 1, e, g))
                        for b in range(NB):
                            last = mm(PS[:, 4 * e + 1, b:b + 1], blk(YT[e], b), con("ones")[:, 0:1], True, True)
                        last.then_inc(sems["oss"], 1)
                    for e in range(2):
                        pe.wait_ge(sems["ors"], per(1, 1, e, g))
                        for b in range(NB):
                            last = mm(PS[:, 4 * e, b * P:(b + 1) * P], ORT[e][:, 1, b:b + 1].to_broadcast([P, P]), I_, True, True)
                        last.then_inc(sems["obc"], 1)
                    for e in range(2):
                        pe.wait_ge(sems["o_done"], per(1, 1, e, g))

            def stick_breaking():
                def head(x, n):
                    return x[(n % 2) * 64:(n % 2) * 64 + 64, n // 2, :]

                def region(n, j, skip=0):
                    o = 1536 * (n % 2) + SB_OFF[j]
                    return PSF[:, o + skip * P:o + SB_WID[j]]

                def scores(n):
                    if n >= 2:
                        pe.wait_ge(sems["sb_a"], n - 1)
                    for j in (0, 1, 3, 2):
                        last = mm(region(n, j), blk(head(KB, n), j), head(QB, n)[:, j * P:S], j != 3, False,
                                  skip_group_check=True)
                    last.then_inc(sems["sb_z"], 1)

                def tails(n):
                    e = n % 2
                    pe.wait_ge(sems["sb_t"], 2 * n + 2)
                    for j in range(NB):
                        if j < NB - 1:
                            src = SP[e][:, SB_OFF[3]:SB_OFF[3] + P] if j == 2 else \
                                TAIL[:, e, 256:640] if j == 0 else TAIL[:, e, 0:256]
                            mm(region(n, j, 1), con("neg_ones"), src, False, False, skip_group_check=True)
                        last = mm(region(n, j), con("neg_tri"), SP[e][:, SB_OFF[j]:SB_OFF[j] + SB_WID[j]],
                                  False, True, skip_group_check=True)
                    last.then_inc(sems["sb_rc"], 1)

                def apply(n):
                    e = n % 2
                    pe.wait_ge(sems["sb_cap"], 2 * n + 2)
                    if n >= 4:
                        pe.wait_ge(sems["hl"], split_done("B.mix", n // 2 - 2))
                    for j in range(NB):
                        last = mm(PS[64 * e:64 * e + 64, 6 + n // 2 % 2, j * P:S], VB[:, n // 2, j, 64 * e:64 * e + 64],
                                  AW[e][:, SB_OFF[j]:SB_OFF[j] + SB_WID[j]], j == 0, j == NB - 1)
                    last.then_inc(sems["sb_o"], 1)

                scores(0)
                scores(1)
                for n in range(12):
                    tails(n)
                    if n:
                        apply(n - 1)
                    if n + 2 < 12:
                        scores(n + 2)
                apply(11)
                pe.wait_ge(sems["hl"], split_done("B.mix", NT - 1))

            def layer_c_mixer():
                for t in range(8):
                    pe.wait_ge(sems["vrow"], 10)
                    if t >= 2:
                        pe.wait_ge(sems["rope_sin"], t - 1)
                    x = (QC if t < 4 else KC)[:, t % 4, :]
                    mm(PS[:, 5 + t % 2, :], con("swap"), x, True, True).then_inc(sems["rope_mm"], 1)
                for g in range(4):
                    pe.wait_ge(sems["pool_z"], g + 1)
                    if g >= 1:
                        pe.wait_ge(sems["mixed"], g)
                    mm(PS[:, 7, :], par("w_pool", g * P, P), Y[:, 2 + g % 2, :], True, True).then_inc(sems["pool_mm"], 1)
                for h in range(4):
                    for c in range(2):
                        if h == 0:
                            pe.wait_ge(sems["rope_done"], 8)
                            pe.wait_ge(sems["emptied_dve"], emptied("dve", U0["C.gate"] + 3, 1))
                        else:
                            pe.wait_ge(sems["df_at"], h)
                        for b in (3, 2, 0, 1):
                            o = 1536 * c + DF_OFF[b]
                            last = mm(PSF[:, o:o + DF_WID[b]], QC[64 * c:64 * c + 64, h, b * P:(b + 1) * P],
                                      KC[64 * c:64 * c + 64, h, 0:DF_WID[b]], True, True)
                        last.then_inc(sems["df_s"], 1)
                    pe.wait_ge(sems["df_a"], 4 * h + 4)
                    for b in range(NB):
                        for j in range(b + 1):
                            last = pe.transpose(PSF[:, SB_OFF[j] + (b - j) * P:SB_OFF[j] + (b - j + 1) * P],
                                                DP[0][:, DF_OFF[b] + j * P:DF_OFF[b] + (j + 1) * P], I_)
                    last.then_inc(sems["df_tr"], 1)
                    pe.wait_ge(sems["df_at"], h + 1)
                    if h:
                        pe.wait_ge(sems["df_w"], 2 * h)
                    for j in range(NB):
                        last = mm(PS[:, 6, j * P:S], VC[:, h, j, :], DAT[:, SB_OFF[j]:SB_OFF[j] + SB_WID[j]], j == 0, j == NB - 1)
                    last.then_inc(sems["df_o"], 1)
                    pe.wait_ge(sems["df_sq"], h + 1)
                    for b in range(NB):
                        last = mm(PS[:, 7, b:b + 1], blk(SQ[:, 0, :], b), con("ones")[:, 0:1], True, True)
                    last.then_inc(sems["df_ss"], 1)
                    pe.wait_ge(sems["df_rs"], h + 1)
                    for b in range(NB):
                        last = mm(PS[:, 7, b * P:(b + 1) * P], DST[:, 0, 0, b:b + 1].to_broadcast([P, P]), I_, True, True)
                    last.then_inc(sems["df_bc"], 1)

            pe.wait_ge(sems["const_in"], 32)
            for L in range(2):
                memory_rows("AB"[L] + ".mem", MH, ML, 0, "mem" if L == 0 else None)
                if L == 0:
                    sum_tokens("mem", MB)
                pe.wait_ge(sems["emptied_act"], emptied("act", U0["AB"[L] + ".mem"] + 1, 1))
                if L:
                    pe.wait_ge(sems["kv_t"], 1)
                for f in range(2):
                    for t in range(MB):
                        last = pe.transpose(PS[:, 5, f * MEM + t * P:f * MEM + (t + 1) * P], KR[:, t, f * P:(f + 1) * P], I_)
                last.then_inc(sems["kv_tr"], 1)

            projection("A.qkv", split="A.in", norm="A.in")
            projection("A.memq")
            projection("A.bg")
            pe.wait_ge(sems["kv_t"], 2)
            for t in range(2 * NT):
                pe.wait_ge(sems["l2sq"], t + 1)
                for b in range(NB):
                    last = mm(PS[:, 6, NB * t + b:NB * t + b + 1], blk(SQ[:, t % 4, :], b), con("ones")[:, 0:1], True, True)
                last.then_inc(sems["l2ss"], 1)
            pe.wait_ge(sems["emptied_dve"], emptied("dve", U0["A.bg"], 1))
            for b in range(NB):
                last = pe.transpose(PS[:, 5, b * 12:(b + 1) * 12], blk(BGT[:, :], b), I_[0:12, 0:12])
            last.then_inc(sems["bg_tr"], 1)
            pe.wait_ge(sems["sc_dve"], 4)
            mm(PS[:, 5, 64:88], con("tri_le"), SC[:, :, 0, :], True, True)
            mm(PS[:, 5, 96:120], con("ones"), SC[:, :, 0, :], True, True).then_inc(sems["gc_mm"], 1)
            delta_net()
            projection("A.gate")
            pe.wait_ge(sems["emptied_dve"], emptied("dve", U0["A.gate"] + 2, 1))
            memory_attention(0, lambda h, c: MQ[(h % 2) * 64:(h % 2) * 64 + 64, h // 2, :],
                             lambda h, c: KT_MEM[0][(h % 2) * 64:(h % 2) * 64 + 64, h // 2, :],
                             lambda h, c, m: V_MEM[0][:, m, h * 64:h * 64 + 64], 1, 64)
            projection("A.out", split="A.mix")
            finish_post("A.post")
            mlp(0)
            finish_post("A.post2")

            projection("B.qk", split="B.in", norm="B.in")
            projection("B.v", after=turn_values("B.v"))
            projection("B.memq")
            pe.wait_ge(sems["vrow"], 6)
            pe.wait_ge(sems["q_scaled"], 1)
            stick_breaking()
            memory_attention(1, lambda h, c: MQB[(h % 2) * 64:(h % 2) * 64 + 64, h // 2, :],
                             lambda h, c: KT_MEM[1][(h % 2) * 64:(h % 2) * 64 + 64, h // 2, :],
                             lambda h, c, m: V_MEM[1][:, m, h * 64:h * 64 + 64], 1, 64)
            projection("B.out", split="B.mix")
            finish_post("B.post")
            mlp(1)
            finish_post("B.post2")

            projection("C.u", split="C.in", norm="C.in")
            projection("C.qk")
            projection("C.v", after=turn_values("C.v"))
            projection("C.gate")
            layer_c_mixer()
            projection("C.out", split="C.mix")
            for r in range(4):
                memory_rows("C.mem", MH2, ML2, r, "mem2" if r == 0 else None)
                if r == 0:
                    sum_tokens("mem2", MB)
                if r in (1, 2):
                    pr = r - 1
                    pe.wait_ge(sems["emptied_act"], emptied("act", U0["C.mem"] + 2 * pr + 1, 1))
                    if pr:
                        pe.wait_ge(sems["kv_t"], 4)
                    for f in range(4):
                        for t in range(MB):
                            last = pe.transpose(PS[:, 5 + f // 2, (f % 2) * MEM + t * P:(f % 2) * MEM + (t + 1) * P],
                                                Y[:, 2 * pr + t, f * P:(f + 1) * P], I_)
                        if f % 2:
                            last.then_inc(sems["kv_tr"], 1)
            projection("C.cq", split="C.cross", norm="C.cross")
            pe.wait_ge(sems["kv_t"], 6)
            pe.wait_ge(sems["emptied_dve"], emptied("dve", U0["C.cq"] + 3, 1))
            memory_attention(2, lambda h, c: CQ[:, 2 * h + c, :], lambda h, c: CK[:, 2 * h + c, :],
                             lambda h, c, m: CV[:, m, h * 256 + c * P:h * 256 + (c + 1) * P], 2, 256)
            projection("C.co", split="C.att")
            mlp(2)
            finish_post("final")

        @block.scalar
        def _(act):
            def A(o, i, f, **kw):
                return act.activation(o, i, f, **kw)

            def split_hi(u, i=None, step=0):
                s = u % 2
                act.wait_ge(sems[f"load{s}"], lin(16 * (u // 2 + 1), 8 * step, i))
                if u >= 2:
                    act.wait_ge(sems["tile"], lin(2 * u - 2, 2 * step, i))
                A(WH[s][:, :, :], STG[s][:, :, :], ACT.Copy).then_inc(sems["hi"], 1)

            def square(name, k, src, n=S):
                m = SQ_BASE[name] + k
                if m >= 4:
                    act.wait_ge(sems["sqa"], added(m - 4))
                A(SQ[:, m % 4, 0:n], src, ACT.Square).then_inc(sems["sq"], 1)

            def operand(q, sums, src, gain, ready, used=None, hh=HH, n=S):
                if used is not None:
                    act.wait_ge(sems["tile"], 2 * used)
                for k in range(KD):
                    ready(k)
                    A(hh[:, k, 0:n], src[:, k, 0:n], ACT.Copy, scale=par(gain, k)).then_inc(sems["hh"], 1)
                    square(sums, k, src[:, k, 0:n], n)

            def root(name, nt=NB):
                act.wait_ge(sems["ss"], sums_done(name))
                A(RT[:, 0:nt], PS[:, 4, 0:nt], ACT.Sqrt, scale=1.0 / D, bias=EPST[:, 0:1]).then_inc(sems["sqrt"], 1)

            def factor(name):
                act.wait_ge(sems["bc"], bcast_done(name))
                A(RS[:, :], PS[:, 4, :], ACT.Copy).then_inc(sems["rs"], 1)

            def units(name, norm=None, evac=None):
                def fn(u, i, step):
                    first = u == U0[name] and i is None
                    if norm and first:
                        root(norm)
                        if u + 2 < UNITS:
                            split_hi(u + 2)
                        factor(norm)
                    if evac:
                        for j in range(2):
                            evac(u, i, step, j)
                    if not (norm and first) and u + 2 < UNITS:
                        split_hi(u + 2, i, step)
                run_phase(act, name, fn)

            def memory_units(name, r, kdst, vdst, norm=None):
                u = U0[name] + 2 * r
                if norm:
                    root(norm, MB)
                    act.wait_ge(sems["rsc"], sums_done(norm))
                for t in range(MB):
                    act.wait_ge(sems["tile"], 2 * u + 2 * t + 2)
                    last = None
                    for dst, c0, c1 in ((kdst, 0, 256), (vdst, 256, 512)):
                        last = A(dst(t), PS[:, 2 * t, c0:c1], ACT.Copy, scale=RSC[:, t:t + 1])
                    last.then_inc(sems["emptied_act"], 2)
                for t in range(2):
                    split_hi(u + 2 + t)

            def mlp(L):
                name = "ABC"[L] + ".mlp"
                ub = U0[name]

                def up(u, i, step, t, j, q):
                    act.wait_ge(sems["emptied_dve"], emptied("dve", u, j, i, step))
                    A(UPH[:, t, :], RR[:, t % 2, :], ACT.Square).then_inc(sems["uh"], 1)

                for r in range(4):
                    if r == 0:
                        root(name)
                        split_hi(ub + 2)
                        factor(name)
                    for j in range(2):
                        up(ub + r, None, 0, 2 * r + j, j, 0)
                    if r:
                        split_hi(ub + r + 2)
                with act.Fori(0, QUARTERS - 1) as q:
                    for r in range(4):
                        split_hi(ub + 4 + r + 2, q, 8)
                    for r in range(4):
                        for j in range(2):
                            up(ub + 8 + r, q, 8, 2 * r + j, j, q)
                        split_hi(ub + 8 + r + 2, q, 8)
                for r in range(4):
                    if ub + 28 + r + 2 < UNITS:
                        split_hi(ub + 28 + r + 2)

            def squares_of_y(name, u):
                for k in range(KD):
                    act.wait_ge(sems["emptied_dve"], emptied("dve", u + k // 2, k % 2))
                    square(name, k, Y[:, k, :])

            def post_factor(name):
                root(name)
                factor(name)

            def out_tile(name, sums):
                def evac(u, i, step, j):
                    k = 2 * (u - U0[name]) + j
                    act.wait_ge(sems["tile"], 2 * u + j + 1)
                    bank = PS[:, 2 * (u % 2) + j, :]
                    square(sums, k, bank)
                    A(Y[:, k, :], bank, ACT.Copy).then_inc(sems["emptied_act"], 1)
                return evac

            def x_new(name, k):
                act.wait_ge(sems["x_new"], 8 * POSTS.index(name) + k + 1)

            def memory_attention(a, dh, dst, scale):
                def soft(h):
                    e = h % 2
                    act.wait_ge(sems["ma_nm"], 4 * a + h + 1)
                    for b in range(NB):
                        A(PROB[e][:, b * MEM:(b + 1) * MEM], PSF[:, 2048 * e + b * MEM:2048 * e + (b + 1) * MEM], ACT.Exp,
                          scale=scale, bias=MST[:, e, 1, b:b + 1], accum_out=MST[:, e, 2, b:b + 1]).then_inc(sems["ma_exp"], 1)

                def turned(h):
                    e = h % 2
                    act.wait_ge(sems["ma_tr"], 4 * a + h + 1)
                    A(PROBT[e], PSF[:, 2048 * e + 1024:2048 * e + 2048], ACT.Copy).then_inc(sems["ma_pt"], 1)

                def result(h):
                    e = h % 2
                    act.wait_ge(sems["ma_o"], 4 * a + h + 1)
                    if dh == 64:
                        last = A(dst(h, 0), PS[64 * e:64 * e + 64, 4 * e, :], ACT.Copy)
                    else:
                        for c in range(2):
                            last = A(dst(h, c), PS[:, 4 * e + c, :], ACT.Copy)
                    last.then_inc(sems["ma_out"], 1)

                soft(0)
                for h in range(4):
                    if h + 1 < 4:
                        soft(h + 1)
                    turned(h)
                    result(h)

            def mix_hi(q, k, src):
                A(HH[:, k, :], src, ACT.Copy).then_inc(sems["hh"], 1)

            def delta_net():
                def per(n, k, e, g):
                    return lin(2 * (k - 1) + e + 1, 2 * n, g)
                with act.Fori(0, H_LIN // 2) as g:
                    for e in range(2):
                        vt = QKV[:, bass.ds(g * 2 + 12 + e, 1), :].rearrange("p a n -> p (a n)")
                        A(VS[e], vt, ACT.Copy).then_inc(sems["v_copy"], 1)
                    for e in range(2):
                        act.wait_ge(sems["bcast_mm"], per(1, 1, e, g))
                        A(EG[e], PS[:, 4 * e, :], ACT.Exp).then_inc(sems["eg_exp"], 1)
                    for e in range(2):
                        act.wait_ge(sems["dt_pre"], per(1, 1, e, g))
                        A(DT[e], DT[e], ACT.Exp).then_inc(sems["dt_exp"], 1)
                    for lv in range(1, 7):
                        for e in range(2):
                            act.wait_ge(sems["lv_y"], per(7, lv + 1, e, g))
                            if lv == 1:
                                act.wait_ge(sems["at"], per(1, 1, e, g))
                            A(YT[e], PS[:, 4 * e + 1, :], ACT.Copy).then_inc(sems["lv_yc"], 1)
                    for e in range(2):
                        act.wait_ge(sems["sc_o"], per(4, 4, e, g))
                        A(YT[e], PS[:, 4 * e + 3, :], ACT.Square).then_inc(sems["osq"], 1)
                    for e in range(2):
                        act.wait_ge(sems["oss"], per(1, 1, e, g))
                        A(ORT[e][:, 0, :], PS[:, 4 * e + 1, 0:NB], ACT.Sqrt, scale=1.0 / P, bias=EPST[:, 0:1])\
                            .then_inc(sems["ort"], 1)
                    for e in range(2):
                        act.wait_ge(sems["obc"], per(1, 1, e, g))
                        A(BT[e], PS[:, 4 * e, :], ACT.Copy).then_inc(sems["obs"], 1)
                    for e in range(2):
                        act.wait_ge(sems["o_done"], per(1, 1, e, g))

            def stick_breaking():
                def logs(n):
                    e = n % 2
                    act.wait_ge(sems["sb_z"], n + 1)
                    if n >= 2:
                        act.wait_ge(sems["sb_rc"], n - 1)
                    A(SP[e], PSF[:, 1536 * e:1536 * e + SB_ALL], ACT.Abs).then_inc(sems["sb_az"], 1)
                    act.wait_ge(sems["sb_az"], n + 1)
                    A(SP[e], SP[e], ACT.Exp, scale=-1.0).then_inc(sems["sb_e"], 1)
                    act.wait_ge(sems["sb_e"], n + 1)
                    A(SP[e], SP[e], ACT.Ln, bias=ONE1[:, 0:1]).then_inc(sems["sb_l"], 1)

                logs(0)
                logs(1)
                for n in range(12):
                    e = n % 2
                    act.wait_ge(sems["sb_rc"], n + 1)
                    if n >= 2:
                        act.wait_ge(sems["sb_o"], n - 1)
                    A(AW[e], PSF[:, 1536 * e:1536 * e + SB_ALL], ACT.Exp).then_inc(sems["sb_a"], 1)
                    if n % 2 == 1 and n >= 3:
                        pair_out(n // 2 - 1)
                    if n + 2 < 12:
                        logs(n + 2)
                pair_out(NT - 1)

            def pair_out(g):
                act.wait_ge(sems["sb_o"], 2 * g + 2)
                A(HH[:, g, :], PS[:, 6 + g % 2, :], ACT.Copy).then_inc(sems["hh"], 1)

            def values(name, dst):
                def fn(r):
                    for j in range(2):
                        t = 2 * r + j
                        act.wait_ge(sems["vtr"], VIDX[name] + t + 1)
                        A(dst[:, t, :, :].rearrange("p b n -> p (b n)"), PS[:, 5 + t % 2, :], ACT.Copy).then_inc(sems["vrow"], 1)
                return fn

            def value_units(name, dst):
                turned = values(name, dst)
                for r in range(NU[name]):
                    if r:
                        turned(r - 1)
                    split_hi(U0[name] + r + 2)
                turned(NU[name] - 1)

            act.dma_start(MX[:, :, :], memt_in).then_inc(sems["mem_in"], 16)
            act.dma_start(PAR[:, :], par_in).then_inc(sems["const_in"], 16)
            act.dma_start(CON[:, :], con_in).then_inc(sems["const_in"], 16)
            act.dma_start(XT[:, :, :], xt_in).then_inc(sems["x_in"], 16)

            act.wait_ge(sems["mem_in"], 16)
            act.wait_ge(sems["const_in"], 32)
            act.wait_ge(sems["eps"], 2)
            operand("mem", "mem", MX, "mem_norm", lambda k: None, hh=MH, n=MEM)
            split_hi(0)
            split_hi(1)
            act.wait_ge(sems["x_in"], 16)
            for L in range(2):
                if L:
                    act.wait_ge(sems["kv_tr"], 1)
                memory_units("AB"[L] + ".mem", 0, lambda t: KR[:, t, :], lambda t: V_MEM[L][:, t, :],
                             norm="mem" if L == 0 else None)
                if L == 0:
                    operand("A.in", "A.in", XT, "pre_mix0", lambda k: None)
                act.wait_ge(sems["kv_tr"], L + 1)
                A(KT_MEM[L][:, :, :].rearrange("p f n -> p (f n)"), PS[:, 5, :], ACT.Copy).then_inc(sems["kv_t"], 1)

            def conv_tile(u, i, step, j):
                t = 2 * (u - U0["A.qkv"]) + j
                act.wait_ge(sems["emptied_dve"], emptied("dve", u, j, i, step))
                w = par("conv", 4 * t) if i is None else PAR[:, bass.ds(i * (8 * step) + (PCOL["conv"] + 4 * t), 1)]
                if u > U0["A.qkv"]:
                    act.wait_ge(sems["silu"], lin(t - 1, 2 * step, i))
                A(CONV_ACC[j], CONV_IN[j][:, 0:S], ACT.Copy, scale=w).then_inc(sems["conv0"], 1)
                if j:
                    for jj in range(2):
                        tt = 2 * (u - U0["A.qkv"]) + jj
                        act.wait_ge(sems["conv"], lin(3 * (tt - jj) + 5 + jj, 6 * step, i))
                        A(tile(QKV, tt if i is None else i * (2 * step) + tt), CONV_ACC[jj], ACT.Silu).then_inc(sems["silu"], 1)

            units("A.qkv", norm="A.in", evac=conv_tile)
            units("A.memq")
            units("A.bg")
            for t in range(2 * NT):
                if t >= 4:
                    act.wait_ge(sems["l2ss"], t - 3)
                elif t == 0:
                    act.wait_ge(sems["sqa"], 14)
                act.wait_ge(sems["silu"], t + 1)
                A(SQ[:, t % 4, :], QKV[:, t, :], ACT.Square).then_inc(sems["l2sq"], 1)
            act.wait_ge(sems["l2ss"], 2 * NT)
            A(RQK[:, :, :].rearrange("p t b -> p (t b)"), PS[:, 6, 0:48], ACT.Sqrt, bias=EPST[:, 0:1]).then_inc(sems["l2rt"], 1)
            act.wait_ge(sems["bg"], 1)
            sm = [SMALL[:, r, :] for r in range(8)]
            A(sm[1], par("a_log", 0, 24), ACT.Exp).then_inc(sems["sc_act"], 1)
            A(sm[5], BG[:, 0:6, :].rearrange("p h b -> p (h b)"), ACT.Exp, scale=-1.0).then_inc(sems["sc_act"], 1)
            act.wait_ge(sems["sc_dve"], 2)
            A(sm[2], sm[2], ACT.Exp, scale=-1.0).then_inc(sems["sc_act"], 1)
            act.wait_ge(sems["sc_act"], 3)
            A(sm[2], sm[2], ACT.Ln, bias=ONE1[:, 0:1]).then_inc(sems["sc_act"], 1)
            act.wait_ge(sems["gc_mm"], 1)
            gc = PS[:, 5, 64:88].rearrange("p (h b) -> p h b", b=NB)
            gl = PS[:, 5, 96:120].rearrange("p (h b) -> p h b", b=NB)
            A(SC[:, :, 4, :], gc, ACT.Copy).then_inc(sems["sc_act"], 1)
            A(sm[7], PS[:, 5, 64:88], ACT.Exp).then_inc(sems["sc_act"], 1)
            A(SC[:, :, 7, :], gl, ACT.Exp).then_inc(sems["sc_act"], 1)
            act.wait_ge(sems["sc_dve"], 7)
            A(SC[:, :, 6, :], SMALL[:, 0, :].rearrange("p (h b) -> p h b", b=NB), ACT.Exp).then_inc(sems["sc_act"], 1)
            delta_net()

            def gate_tile(u, i, step, j):
                act.wait_ge(sems["emptied_dve"], emptied("dve", u, j))
                A(TMP[0][j][:, :], TMP[0][j][:, :], ACT.Silu).then_inc(sems["gate_silu"], 1)

            units("A.gate", evac=gate_tile)
            memory_attention(0, 64, lambda h, c: CX[(h % 2) * 64:(h % 2) * 64 + 64, h // 2, :], 64 ** -0.5)
            for k in range(KD):
                if k < NT:
                    act.wait_ge(sems["gated"], k + 1)
                elif k == NT:
                    act.wait_ge(sems["ma_out"], 4)
                mix_hi("A.mix", k, QKV[:, k, :] if k < NT else CX[:, k - NT, :])
            units("A.out", evac=out_tile("A.out", "A.post"))
            post_factor("A.post")
            operand("A.mlp", "A.mlp", XT, "pre_mlp0", lambda k: x_new("A.post", k), used=U0["A.mlp"])
            mlp(0)
            squares_of_y("A.post2", U0["A.mlp"] + 28)
            post_factor("A.post2")

            operand("B.in", "B.in", XT, "pre_mix1", lambda k: x_new("A.post2", k), used=U0["B.qk"])
            units("B.qk", norm="B.in")
            value_units("B.v", VB)
            units("B.memq")
            act.wait_ge(sems["emptied_dve"], emptied("dve", U0["B.memq"], 1))
            act.wait_ge(sems["tile"], 2 * U0["B.out"])
            stick_breaking()
            memory_attention(1, 64, lambda h, c: MO[(h % 2) * 64:(h % 2) * 64 + 64, h // 2, :], 64 ** -0.5)
            act.wait_ge(sems["ma_out"], 8)
            for k in (6, 7):
                mix_hi("B.mix", k, MO[:, k - NT, :])
            units("B.out", evac=out_tile("B.out", "B.post"))
            post_factor("B.post")
            operand("B.mlp", "B.mlp", XT, "pre_mlp1", lambda k: x_new("B.post", k), used=U0["B.mlp"])
            mlp(1)
            squares_of_y("B.post2", U0["B.mlp"] + 28)
            post_factor("B.post2")

            operand("C.in", "C.in", XT, "g_mix", lambda k: x_new("B.post2", k), used=U0["C.u"])
            units("C.u", norm="C.in")
            units("C.qk")
            value_units("C.v", VC)

            def gate_sig(u, i, step, j):
                k = 2 * (u - U0["C.gate"]) + j
                act.wait_ge(sems["emptied_dve"], emptied("dve", u, j))
                A(GC_[:, k, :], GC_[:, k, :], ACT.Sigmoid).then_inc(sems["sig"], 1)

            units("C.gate", evac=gate_sig)
            act.wait_ge(sems["lam"], 2)
            A(LAM[:, 2:4], LAM[:, 0:2], ACT.Exp).then_inc(sems["lam_act"], 1)
            act.wait_ge(sems["tile"], 2 * U0["C.out"])
            for g in range(4):
                act.wait_ge(sems["mixed"], g + 1)
                mix_hi("C.mix", g, Y[:, g % 2, :])
            for h in range(4):
                for c in range(2):
                    act.wait_ge(sems["df_nm"], 2 * h + c + 1)
                    for b in range(NB):
                        A(DP[c][:, DF_OFF[b]:DF_OFF[b] + DF_WID[b]], PSF[:, 1536 * c + DF_OFF[b]:1536 * c + DF_OFF[b] + DF_WID[b]],
                          ACT.Exp, scale=64 ** -0.5, bias=DMX[:, c, 1, b:b + 1], accum_out=DST[:, 1, c, b:b + 1])\
                            .then_inc(sems["df_exp"], 1)
                act.wait_ge(sems["df_tr"], h + 1)
                A(DAT[:, 0:SB_ALL], PSF[:, 0:SB_ALL], ACT.Copy).then_inc(sems["df_at"], 1)
                act.wait_ge(sems["df_o"], h + 1)
                if h:
                    act.wait_ge(sems["df_w"], 2 * h)
                A(SQ[:, 0, :], PS[:, 6, :], ACT.Square).then_inc(sems["df_sq"], 1)
                act.wait_ge(sems["df_ss"], h + 1)
                A(DST[:, 0, 1, :], PS[:, 7, 0:NB], ACT.Sqrt, scale=1.0 / P, bias=EPST[:, 0:1]).then_inc(sems["df_rt"], 1)
                act.wait_ge(sems["df_bc"], h + 1)
                A(SQ[:, 1, :], PS[:, 7, :], ACT.Copy).then_inc(sems["df_bs"], 1)
                act.wait_ge(sems["df_w"], 2 * h + 2)
                mix_hi("C.mix", 4 + h, SQ[:, 3, :])

            units("C.out")
            act.wait_ge(sems["mem2_in"], 16)
            operand("mem2", "mem2", MX2, "g_mem", lambda k: None, hh=MH2, n=MEM)
            for r in range(4):
                kv = (lambda t: Y[:, 2 * r + t, 0:256], lambda t: Y[:, 2 * r + t, 256:512]) if r < 2 else \
                     (lambda t: CV[:, t, 512 * (r - 2):512 * (r - 2) + 256], lambda t: CV[:, t, 512 * (r - 2) + 256:512 * (r - 1)])
                memory_units("C.mem", r, *kv, norm="mem2" if r == 0 else None)
                if r in (1, 2):
                    for f in range(2):
                        act.wait_ge(sems["kv_tr"], 2 + 2 * (r - 1) + f + 1)
                        A(CK[:, 4 * (r - 1) + 2 * f:4 * (r - 1) + 2 * f + 2, :].rearrange("p f n -> p (f n)"),
                          PS[:, 5 + f, :], ACT.Copy).then_inc(sems["kv_t"], 1)
            operand("C.cross", "C.cross", XT, "g_cross",
                    lambda k: act.wait_ge(sems["emptied_dve"], emptied("dve", U0["C.out"] + k // 2, k % 2)), used=U0["C.mem"])
            units("C.cq", norm="C.cross")
            memory_attention(2, 256, lambda h, c: CQ[:, 2 * h + c, :], 256 ** -0.5)
            act.wait_ge(sems["tile"], 2 * U0["C.co"])
            act.wait_ge(sems["ma_out"], 12)
            for k in range(KD):
                mix_hi("C.att", k, CQ[:, k, :])
            units("C.co")
            operand("C.mlp", "C.mlp", XT, "g_mlp",
                    lambda k: act.wait_ge(sems["emptied_dve"], emptied("dve", U0["C.co"] + k // 2, k % 2)), used=U0["C.mlp"])
            mlp(2)
            for k in range(KD):
                act.wait_ge(sems["emptied_dve"], emptied("dve", U0["C.mlp"] + 28 + k // 2, k % 2))
                square("final", k, XT[:, k, :])
            post_factor("final")

        @block.vector
        def _(dve):
            def stt(o, a, s_, b, op0, op1):
                return dve.scalar_tensor_tensor(out=o, in0=a, scalar=s_, in1=b, op0=op0, op1=op1)

            def tt(o, a, b, op):
                return dve.tensor_tensor(o, a, b, op)

            def split_lo(u, i=None, step=0):
                s = u % 2
                dve.wait_ge(sems["hi"], lin(u + 1, step, i))
                tt(WL[s][:, :, :], STG[s][:, :, :], WH[s][:, :, :].bitcast(F32), ALU.subtract).then_inc(sems["lo"], 1)

            def operand_lo(q, src, gain, hh=HH, hl=HL, n=S, k0=0, k1=KD):
                for k in range(k0, k1):
                    dve.wait_ge(sems["hh"], split_done(q, k))
                    stt(hl[:, k, 0:n], src[:, k, 0:n], par(gain, k), hh[:, k, 0:n].bitcast(F32), ALU.mult, ALU.subtract)\
                        .then_inc(sems["hl"], 1)

            def invert(name, nt=NB):
                dve.wait_ge(sems["sqrt"], sums_done(name))
                dve.reciprocal(RSC[:, 0:nt], RT[:, 0:nt]).then_inc(sems["rsc"], 1)

            def units(name, norm=None, evac=None, lead=True):
                def fn(u, i, step):
                    first = u == U0[name] and i is None
                    if norm and first:
                        invert(norm)
                        split_lo(u + 2)
                        dve.wait_ge(sems["rs"], bcast_done(norm))
                    if evac:
                        for j in range(2):
                            dve.wait_ge(sems["tile"], lin(2 * u + j + 1, 2 * step, i))
                            evac(u, i, step, j)
                    if not (norm and first) and u + 2 < UNITS:
                        split_lo(u + 2, i, step)
                run_phase(dve, name, fn)

            def scaled_to(dst, name):
                def evac(u, i, step, j):
                    t = 2 * (u - U0[name]) + j
                    o = dst(t) if i is None else dst(i * (2 * step) + t)
                    tt(o, PS[:, 2 * (u % 2) + j, :], RS[:, :], ALU.mult).then_inc(sems["emptied_dve"], 1)
                return evac

            def add_to(dst, name):
                def evac(u, i, step, j):
                    k = 2 * (u - U0[name]) + j
                    tt(dst[:, k, :], dst[:, k, :], PS[:, 2 * (u % 2) + j, :], ALU.add).then_inc(sems["emptied_dve"], 1)
                return evac

            def mlp(L):
                name = "ABC"[L] + ".mlp"
                ub = U0[name]
                dst = XT if L == 2 else Y

                def up(u, i, step, t, j):
                    m = lin(32 * L + 8 * ((u - ub) // 8) + t, step, i)
                    bank = PS[:, 2 * (u % 2) + j, :]
                    dve.wait_ge(sems["tile"], lin(2 * u + j + 1, 2 * step, i))
                    stt(RR[:, t % 2, :], bank, 0.0, RS[:, :], ALU.max, ALU.mult).then_inc(sems["emptied_dve"], 1)
                    dve.wait_ge(sems["emptied_dve"], emptied("dve", u, j, i, step))
                    tt(RQ[:, t % 2, :], RR[:, t % 2, :], RR[:, t % 2, :], ALU.mult).then_inc(sems["rq"], 1)
                    dve.wait_ge(sems["rq"], m + 1)
                    dve.wait_ge(sems["uh"], m + 1)
                    tt(UPL[:, t, :], RQ[:, t % 2, :], UPH[:, t, :].bitcast(F32), ALU.subtract).then_inc(sems["ul"], 1)

                def down(u, i, step, t, j):
                    dve.wait_ge(sems["tile"], lin(2 * u + j + 1, 2 * step, i))
                    tt(dst[:, t, :], dst[:, t, :], PS[:, 2 * (u % 2) + j, :], ALU.add).then_inc(sems["emptied_dve"], 1)

                for r in range(4):
                    if r == 0:
                        invert(name)
                        split_lo(ub + 2)
                        dve.wait_ge(sems["rs"], bcast_done(name))
                    for j in range(2):
                        up(ub + r, None, 0, 2 * r + j, j)
                    if r:
                        split_lo(ub + r + 2)
                if L < 2:
                    dve.wait_ge(sems["y_zero"], L + 1)
                with dve.Fori(0, QUARTERS - 1) as q:
                    for r in range(4):
                        for j in range(2):
                            down(ub + 4 + r, q, 8, 2 * r + j, j)
                        split_lo(ub + 4 + r + 2, q, 8)
                    for r in range(4):
                        for j in range(2):
                            up(ub + 8 + r, q, 8, 2 * r + j, j)
                        split_lo(ub + 8 + r + 2, q, 8)
                for r in range(4):
                    for j in range(2):
                        down(ub + 28 + r, None, 0, 2 * r + j, j)
                    if ub + 28 + r + 2 < UNITS:
                        split_lo(ub + 28 + r + 2)

            def post_and_operand(post, gain, q, gain_in):
                invert(post)
                dve.wait_ge(sems["rs"], bcast_done(post))
                if post in ("A.post", "B.post"):
                    dve.wait_ge(sems["emptied_act"], emptied("act", U0[post[0] + ".out"] + 3, 1))
                for k in range(KD + 3):
                    if k < KD:
                        stt(Y[:, k, :], Y[:, k, :], par(gain, k), RS[:, :], ALU.mult, ALU.mult).then_inc(sems["y_scaled"], 1)
                    if k >= 3:
                        operand_lo(q, XT, gain_in, k0=k - 3, k1=k - 2)

            def memory_attention(a, scale):
                def top(h):
                    e = h % 2
                    n = 4 * a + h
                    dve.wait_ge(sems["ma_s"], n + 1)
                    dve.tensor_reduce(MST[:, e, 0, :], PSF[:, 2048 * e:2048 * e + 1024].rearrange("p (b m) -> p b m", b=NB),
                                      AX.X, ALU.max).then_inc(sems["ma_max"], 1)
                    dve.wait_ge(sems["ma_max"], n + 1)
                    dve.tensor_scalar(MST[:, e, 1, :], MST[:, e, 0, :], -scale, None, ALU.mult).then_inc(sems["ma_nm"], 1)

                def normalise(h):
                    e = h % 2
                    n = 4 * a + h
                    dve.wait_ge(sems["ma_exp"], 4 * n + 4)
                    dve.reciprocal(MST[:, e, 3, :], MST[:, e, 2, :]).then_inc(sems["ma_ri"], 1)
                    dve.wait_ge(sems["ma_ri"], n + 1)
                    p = PROB[e].rearrange("p (b m) -> p b m", b=NB)
                    tt(p, p, MST[:, e, 3, :].unsqueeze(2).to_broadcast([P, NB, MEM]), ALU.mult).then_inc(sems["ma_p"], 1)

                top(0)
                for h in range(4):
                    if h + 1 < 4:
                        top(h + 1)
                    normalise(h)

            def mix_lo(q, k, src):
                dve.wait_ge(sems["hh"], split_done(q, k))
                tt(HL[:, k, :], src, HH[:, k, :].bitcast(F32), ALU.subtract).then_inc(sems["hl"], 1)

            def delta_net():
                def per(n, k, e, g):
                    return lin(2 * (k - 1) + e + 1, 2 * n, g)

                def row(base, e, g):
                    return QKV[:, bass.ds(g * 2 + base + e, 1), :].rearrange("p a n -> p (a n)")

                with dve.Fori(0, H_LIN // 2) as g:
                    for e in range(2):
                        src = SC[:, bass.ds(g * 2 + e, 1), :, :].rearrange("p a c b -> p (a c b)")
                        dve.tensor_copy(HS[e][:, :, :].rearrange("p c b -> p (c b)"), src).then_inc(sems["head_sc"], 1)
                    for e in range(2):
                        dve.wait_ge(sems["bcast_mm"], per(1, 1, e, g))
                        dve.wait_ge(sems["head_sc"], per(1, 1, e, g))
                        bank = lambda o: PS[:, 4 * e + o, :]
                        tt(KNS[e], row(6, e, g), bank(2), ALU.mult).then_inc(sems["kn"], 1)
                        dve.wait_ge(sems["eg_exp"], per(1, 1, e, g))
                        for b in range(NB):
                            last = dve.tensor_scalar(blk(DT[e], b), blk(bank(0), b), HS[e][:, 4, b:b + 1], 0.0,
                                                     ALU.subtract, ALU.min)
                        last.then_inc(sems["dt_pre"], 1)
                        tt(row(0, e, g), row(0, e, g), bank(3), ALU.mult).then_inc(sems["qn"], 1)
                        dve.wait_ge(sems["kn"], per(1, 1, e, g))
                        tt(KBT[e], KNS[e], bank(1), ALU.mult).then_inc(sems["kbt"], 1)
                    for e in range(2):
                        bank = lambda o: PS[:, 4 * e + o, :]
                        dve.wait_ge(sems["dt_exp"], per(1, 1, e, g))
                        dve.wait_ge(sems["lt_mm"], per(1, 1, e, g))
                        tt(LT[e], bank(1), DT[e], ALU.mult).then_inc(sems["lt"], 1)
                        dve.wait_ge(sems["lt"], per(1, 1, e, g))
                        tt(blocks(DT[e]), blocks(DT[e]), bc_blocks(con("tri_le")), ALU.mult).then_inc(sems["dtm"], 1)
                        dve.wait_ge(sems["rows"], per(1, 1, e, g))
                        dve.wait_ge(sems["dtm"], per(1, 1, e, g))
                        tt(AT[e], bank(2), DT[e], ALU.mult).then_inc(sems["at"], 1)
                        dve.wait_ge(sems["eg_exp"], per(1, 1, e, g))
                        tt(row(0, e, g), row(0, e, g), EG[e], ALU.mult).then_inc(sems["qd"], 1)
                        dve.wait_ge(sems["qd"], per(1, 1, e, g))
                        tt(blocks(RK[e]), blocks(bank(3)), per_block(HS[e][:, 5, :]), ALU.mult)
                        tt(blocks(KDC[e]), blocks(bank(3)), per_block(HS[e][:, 6, :]), ALU.mult).then_inc(sems["rk"], 1)
                        tt(blocks(row(12, e, g)), blocks(bank(0)), per_block(HS[e][:, 1, :]), ALU.mult).then_inc(sems["rv"], 1)
                    for e in range(2):
                        dve.wait_ge(sems["lv_y"], per(7, 1, e, g))
                        tt(blocks(XX[e]), bc_blocks(con("ident")), blocks(PS[:, 4 * e + 1, :]), ALU.subtract)
                        tt(blocks(XTr[e]), bc_blocks(con("ident")), blocks(BT[e]), ALU.subtract).then_inc(sems["lv_x"], 1)
                    for lv in range(1, 7):
                        for e in range(2):
                            dve.wait_ge(sems["lv_p"], per(6, lv, e, g))
                            dve.wait_ge(sems["lv_x"], per(7, lv, e, g))
                            if lv < 6:
                                tt(XX[e], XX[e], PS[:, 4 * e + 2, :], ALU.subtract)
                            tt(XTr[e], XTr[e], PS[:, 4 * e + 3, :], ALU.subtract).then_inc(sems["lv_x"], 1)
                    for e in range(2):
                        dve.wait_ge(sems["u_mm"], per(1, 1, e, g))
                        dve.tensor_scalar(row(12, e, g), PS[:, 4 * e, :], 1.0, None, ALU.mult).then_inc(sems["u_sb"], 1)
                        dve.tensor_copy(WT[e], PS[:, 4 * e + 1, :]).then_inc(sems["w_sb"], 1)
                    for b in range(NB):
                        for e in range(2):
                            ub = blk(row(12, e, g), b)
                            if b == 0:
                                dve.wait_ge(sems["u_sb"], per(1, 1, e, g))
                                dve.tensor_scalar(VN[e][:, :], ub, 1.0, None, ALU.mult).then_inc(sems["vn"], 1)
                            else:
                                dve.wait_ge(sems["sc_ws"], per(3, b, e, g))
                                tt(VN[e][:, :], ub, PS[:, 4 * e + 2, 0:P], ALU.subtract).then_inc(sems["vn"], 1)
                        for e in range(2):
                            if b == NB - 1:
                                continue
                            dve.wait_ge(sems["sc_o"], per(4, b + 1, e, g))
                            if b == 0:
                                dve.tensor_copy(ST8[e][:, :], PS[:, 4 * e + 2, P:2 * P]).then_inc(sems["st"], 1)
                            else:
                                dve.wait_ge(sems["st"], per(3, b, e, g))
                                stt(ST8[e][:, :], ST8[e][:, :], HS[e][:, 7, b:b + 1], PS[:, 4 * e + 2, P:2 * P],
                                    ALU.mult, ALU.add).then_inc(sems["st"], 1)
                    for e in range(2):
                        dve.wait_ge(sems["ort"], per(1, 1, e, g))
                        dve.reciprocal(ORT[e][:, 1, :], ORT[e][:, 0, :]).then_inc(sems["ors"], 1)
                    for e in range(2):
                        dve.wait_ge(sems["obs"], per(1, 1, e, g))
                        stt(row(0, e, g), PS[:, 4 * e + 3, :], par("onorm"), BT[e], ALU.mult, ALU.mult).then_inc(sems["o_done"], 1)
                    for e in range(2):
                        dve.wait_ge(sems["o_done"], per(1, 1, e, g))

            def diagonals(ap):
                v = ap[:, 0:1152].rearrange("p (a n) -> p a n", n=P)
                return v[:, 0:9:4, :], ap[:, SB_OFF[3]:SB_OFF[3] + P]

            def stick_breaking():
                def softplus(n):
                    e = n % 2
                    dve.wait_ge(sems["sb_l"], n + 1)
                    stt(SP[e], PSF[:, 1536 * e:1536 * e + SB_ALL], 0.0, SP[e], ALU.max, ALU.add).then_inc(sems["sb_sp"], 1)
                    dve.wait_ge(sems["sb_sp"], n + 1)
                    three, one = diagonals(SP[e])
                    tt(three, three, con("strict").unsqueeze(1).to_broadcast([P, 3, P]), ALU.mult)
                    tt(one, one, con("strict"), ALU.mult).then_inc(sems["sb_m"], 1)
                    dve.wait_ge(sems["sb_m"], n + 1)
                    two = TAIL[:, e, 0:256]
                    dve.tensor_copy(TAIL[:, e, 0:P], SP[e][:, SB_OFF[2]:SB_OFF[2] + P])
                    tt(TAIL[:, e, P:2 * P], SP[e][:, SB_OFF[2] + P:SB_OFF[2] + 2 * P], SP[e][:, SB_OFF[3]:SB_OFF[3] + P], ALU.add)\
                        .then_inc(sems["sb_t"], 1)
                    dve.wait_ge(sems["sb_t"], 2 * n + 1)
                    dve.tensor_copy(TAIL[:, e, 256:384], SP[e][:, SB_OFF[1]:SB_OFF[1] + P])
                    tt(TAIL[:, e, 384:640], SP[e][:, SB_OFF[1] + P:SB_OFF[1] + 3 * P], two, ALU.add).then_inc(sems["sb_t"], 1)

                softplus(0)
                softplus(1)
                for n in range(12):
                    e = n % 2
                    dve.wait_ge(sems["sb_a"], n + 1)
                    three, one = diagonals(AW[e])
                    tt(three, three, con("cap").unsqueeze(1).to_broadcast([P, 3, P]), ALU.min).then_inc(sems["sb_cap"], 1)
                    tt(one, one, con("cap"), ALU.min).then_inc(sems["sb_cap"], 1)
                    if n % 2 == 1 and n >= 3:
                        mix_lo("B.mix", n // 2 - 1, PS[:, 6 + (n // 2 - 1) % 2, :])
                    if n + 2 < 12:
                        softplus(n + 2)
                mix_lo("B.mix", NT - 1, PS[:, 6 + (NT - 1) % 2, :])

            def vstage(name):
                def evac(u, i, step, j):
                    t = 2 * (u - U0[name]) + j
                    if t >= 2:
                        dve.wait_ge(sems["vtr"], VIDX[name] + t - 1)
                    tt(Y[:, t % 2, :], PS[:, 2 * (u % 2) + j, :], RS[:, :], ALU.mult).then_inc(sems["emptied_dve"], 1)
                return evac

            dve.wait_ge(sems["const_in"], 32)
            dve.wait_ge(sems["mem_in"], 16)
            operand_lo("mem", MX, "mem_norm", MH, ML, MEM)
            split_lo(0)
            split_lo(1)
            invert("mem", MB)
            split_lo(2)
            split_lo(3)
            operand_lo("A.in", XT, "pre_mix0")
            split_lo(4)
            split_lo(5)

            dve.wait_ge(sems["cb_zero"], 2)

            def conv_tile(u, i, step, j):
                r = u - U0["A.qkv"]
                if r:
                    dve.wait_ge(sems["conv"], lin(6 * r - 1 + j, 6 * step, i))
                tt(CONV_IN[j][:, 3:3 + S], PS[:, 2 * (u % 2) + j, :], RS[:, :], ALU.mult).then_inc(sems["emptied_dve"], 1)
                if j:
                    for tap in range(1, 4):
                        for jj in range(2):
                            tj = 2 * (u - U0["A.qkv"]) + jj
                            if tap == 1:
                                dve.wait_ge(sems["conv0"], lin(tj + 1, 2 * step, i))
                            else:
                                dve.wait_ge(sems["conv"], lin(6 * (tj // 2) + 2 * (tap - 2) + jj + 1, 6 * step, i))
                            c = PCOL["conv"] + 4 * tj + tap
                            w = PAR[:, c:c + 1] if i is None else PAR[:, bass.ds(i * (8 * step) + c, 1)]
                            stt(CONV_ACC[jj], CONV_IN[jj][:, tap:tap + S], w, CONV_ACC[jj], ALU.mult, ALU.add)\
                                .then_inc(sems["conv"], 1)

            units("A.qkv", norm="A.in", evac=conv_tile)
            units("A.memq", evac=scaled_to(lambda t: MQ[:, t, :], "A.memq"))

            def bg_tile(u, i, step, j):
                if j == 0:
                    tt(BGT[:, :], PS[0:12, 2 * (u % 2), :], RS[0:12, :], ALU.mult).then_inc(sems["emptied_dve"], 2)

            units("A.bg", evac=bg_tile)
            hb = lambda ap: ap.rearrange("p (h b) -> p h b", b=NB)
            dve.wait_ge(sems["bg_tr"], 1)
            dve.tensor_copy(BG[:, :, :], PS[:, 5, 0:48].rearrange("p (b h) -> p h b", b=NB)).then_inc(sems["bg"], 1)
            dve.wait_ge(sems["bg"], 1)
            sm = [SMALL[:, r, :] for r in range(8)]
            step_ = [0]

            def sc(ins):
                step_[0] += 1
                ins.then_inc(sems["sc_dve"], 1)
                dve.wait_ge(sems["sc_dve"], step_[0])

            sc(tt(sm[0], BG[:, 6:12, :].rearrange("p h b -> p (h b)"), par("dt", 0, 24), ALU.add))
            sc(stt(sm[2], sm[0], -1.0, sm[0], ALU.mult, ALU.max))
            dve.wait_ge(sems["sc_act"], 4)
            sc(stt(sm[3], sm[0], 0.0, sm[2], ALU.max, ALU.add))
            sc(stt(SC[:, :, 0, :], hb(sm[3]), -1.0, hb(sm[1]), ALU.mult, ALU.mult))
            sc(dve.tensor_scalar(sm[5], sm[5], 1.0, None, ALU.add))
            sc(dve.reciprocal(SC[:, :, 1, :], hb(sm[5])))
            dve.wait_ge(sems["sc_act"], 7)
            sc(tt(hb(sm[0]), hb(PS[:, 5, 96:120]), SC[:, :, 4, :], ALU.subtract))
            sc(tt(SC[:, :, 5, :], SC[:, :, 1, :], hb(sm[7]), ALU.mult))
            dve.wait_ge(sems["l2rt"], 1)
            rq = RQK[:, :, :].rearrange("p t b -> p (t b)")
            sc(dve.reciprocal(rq, rq))
            sc(dve.tensor_scalar(SC[:, :, 3, :], RQK[:, 0:6, :], P ** -0.5, None, ALU.mult))
            sc(dve.tensor_copy(SC[:, :, 2, :], RQK[:, 6:12, :]))
            dve.wait_ge(sems["sc_act"], 8)
            delta_net()

            def gate_tile(u, i, step, j):
                t = 2 * (u - U0["A.gate"]) + j
                if t >= 2:
                    dve.wait_ge(sems["gated"], t - 1)
                tt(TMP[0][j][:, :], PS[:, 2 * (u % 2) + j, :], RS[:, :], ALU.mult).then_inc(sems["emptied_dve"], 1)
                if j:
                    for jj in range(2):
                        tj = t - 1 + jj
                        dve.wait_ge(sems["gate_silu"], tj + 1)
                        tt(QKV[:, tj, :], QKV[:, tj, :], TMP[0][jj][:, :], ALU.mult).then_inc(sems["gated"], 1)

            units("A.gate", evac=gate_tile)
            memory_attention(0, 64 ** -0.5)
            for k in range(KD):
                mix_lo("A.mix", k, QKV[:, k, :] if k < NT else CX[:, k - NT, :])
            units("A.out")
            post_and_operand("A.post", "post_mix0", "A.mlp", "pre_mlp0")
            mlp(0)
            post_and_operand("A.post2", "post_mlp0", "B.in", "pre_mix1")

            def qk_tile(u, i, step, j):
                t = 2 * (u - U0["B.qk"]) + j
                if i is None:
                    o = QB[:, t, :] if t < NT else KB[:, t - NT, :]
                else:
                    o = tile(QKB, i * (2 * step) + t)
                stt(o, PS[:, 2 * (u % 2) + j, :], 1.0, RS[:, :], ALU.mult, ALU.mult).then_inc(sems["emptied_dve"], 1)

            units("B.qk", norm="B.in", evac=qk_tile)
            units("B.v", evac=vstage("B.v"))
            units("B.memq", evac=scaled_to(lambda t: MQB[:, t, :], "B.memq"))
            dve.wait_ge(sems["emptied_dve"], emptied("dve", U0["B.memq"], 1))
            dve.tensor_scalar(QB[:, :, :], QB[:, :, :], 64 ** -0.5, None, ALU.mult).then_inc(sems["q_scaled"], 1)
            stick_breaking()
            memory_attention(1, 64 ** -0.5)
            for k in (6, 7):
                mix_lo("B.mix", k, MO[:, k - NT, :])
            units("B.out")
            post_and_operand("B.post", "post_mix1", "B.mlp", "pre_mlp1")
            mlp(1)
            post_and_operand("B.post2", "post_mlp1", "C.in", "g_mix")

            for n in range(2):
                dve.tensor_tensor_reduce(out=PA[:, n, 64:128], in0=par(("lq1", "lq2")[n], 0, 64), in1=par(("lk1", "lk2")[n], 0, 64),
                                         scale=1.0, scalar=0.0, op0=ALU.mult, op1=ALU.add, accum_out=LAM[:, n:n + 1])\
                    .then_inc(sems["lam"], 1)
            units("C.u", norm="C.in", evac=scaled_to(lambda t: UT[:, t, 16:16 + S], "C.u"))
            units("C.qk", evac=scaled_to(lambda t: QC[:, t, :] if t < 4 else KC[:, t - 4, :], "C.qk"))
            units("C.v", evac=vstage("C.v"))
            units("C.gate", evac=scaled_to(lambda t: GC_[:, t, :], "C.gate"))
            dve.wait_ge(sems["lam_act"], 1)
            tt(LAM[:, 4:5], LAM[:, 3:4], LAM[:, 2:3], ALU.subtract).then_inc(sems["lam"], 1)
            dve.wait_ge(sems["lam"], 3)
            dve.tensor_scalar(LAM[:, 5:6], LAM[:, 4:5], -LAM_INIT, None, ALU.add).then_inc(sems["lam"], 1)
            dve.wait_ge(sems["rope_in"], 16)
            for t in range(8):
                x = (QC if t < 4 else KC)[:, t % 4, :]
                r = PA[:, t % 2, 0:S]
                dve.wait_ge(sems["rope_mm"], t + 1)
                tt(r, PS[:, 5 + t % 2, :], COSIN[:, 1, :], ALU.mult).then_inc(sems["rope_sin"], 1)
                tt(x, x, COSIN[:, 0, :], ALU.mult).then_inc(sems["rope_cos"], 1)
                dve.wait_ge(sems["rope_cos"], t + 1)
                tt(x, x, r, ALU.add).then_inc(sems["rope_done"], 1)
            dve.wait_ge(sems["rope_done"], 8)
            dve.wait_ge(sems["rcnt_in"], 16)
            dve.memset(PA[:, :, 0:16], 0.0).then_inc(sems["pool_s"], 1)
            dve.memset(UT[:, :, 0:16], 0.0).then_inc(sems["pool_s"], 1)
            n_s = 2
            dve.wait_ge(sems["sig"], 8)
            for g in range(4):
                src = UT[:, g, :]
                for lv in range(g + 1):
                    dve.wait_ge(sems["pool_s"], n_s)
                    dst = PA[:, lv % 2, :]
                    sh = 2 ** lv
                    tt(dst[:, 16:16 + S], src[:, 16:16 + S], src[:, 16 - sh:16 - sh + S], ALU.add).then_inc(sems["pool_s"], 1)
                    n_s += 1
                    src = dst
                dve.wait_ge(sems["pool_s"], n_s)
                if g >= 2:
                    dve.wait_ge(sems["pool_mm"], g - 1)
                z = Y[:, 2 + g % 2, :]
                tt(z, src[:, 16:16 + S], RCNT[:, g, :], ALU.mult).then_inc(sems["pool_s"], 1)
                n_s += 1
                dve.wait_ge(sems["pool_s"], n_s)
                tt(z, z, UT[:, g, 16:16 + S], ALU.subtract).then_inc(sems["pool_z"], 1)
                dve.wait_ge(sems["pool_mm"], g + 1)
                if g >= 2:
                    dve.wait_ge(sems["hh"], split_done("C.mix", g - 2))
                stt(Y[:, g % 2, :], PS[:, 7, :], par("pool_scale", g), GC_[:, g, :], ALU.mult, ALU.mult)\
                    .then_inc(sems["mixed"], 1)
                dve.wait_ge(sems["mixed"], g + 1)
                mix_lo("C.mix", g, Y[:, g % 2, :])
            dve.wait_ge(sems["lam"], 4)
            for h in range(4):
                for c in range(2):
                    dve.wait_ge(sems["df_s"], 2 * h + c + 1)
                    s0 = PSF[:, 1536 * c:1536 * c + SB_ALL]
                    three = s0[:, 384:1280].rearrange("p (a n) -> p a n", n=P)[:, 0:7:3, :]
                    tt(three, three, con("causal_add").unsqueeze(1).to_broadcast([P, 3, P]), ALU.add).then_inc(sems["df_mask"], 1)
                    tt(s0[:, 896:1024], s0[:, 896:1024], con("causal_add"), ALU.add).then_inc(sems["df_mask"], 1)
                    dve.wait_ge(sems["df_mask"], 4 * h + 2 * c + 2)
                    for b in range(NB):
                        last = dve.tensor_reduce(DMX[:, c, 0, b:b + 1], s0[:, DF_OFF[b]:DF_OFF[b] + DF_WID[b]], AX.X, ALU.max)
                    last.then_inc(sems["df_max"], 1)
                    dve.wait_ge(sems["df_max"], 2 * h + c + 1)
                    dve.tensor_scalar(DMX[:, c, 1, :], DMX[:, c, 0, :], -(64 ** -0.5), None, ALU.mult).then_inc(sems["df_nm"], 1)
                dve.wait_ge(sems["df_exp"], 8 * h + 8)
                ri = DST[:, 1, :, :].rearrange("p c b -> p (c b)")
                dve.reciprocal(ri, ri).then_inc(sems["df_ri"], 1)
                dve.wait_ge(sems["df_ri"], 2 * h + 1)
                dve.tensor_scalar(DST[:, 1, 1, :], DST[:, 1, 1, :], LAM[:, 5:6], None, ALU.mult).then_inc(sems["df_ri"], 1)
                dve.wait_ge(sems["df_ri"], 2 * h + 2)
                for b in range(NB):
                    last = dve.tensor_scalar(DP[1][:, DF_OFF[b]:DF_OFF[b] + DF_WID[b]], DP[1][:, DF_OFF[b]:DF_OFF[b] + DF_WID[b]],
                                             DST[:, 1, 1, b:b + 1], None, ALU.mult)
                last.then_inc(sems["df_p1"], 1)
                dve.wait_ge(sems["df_p1"], h + 1)
                for b in range(NB):
                    o = slice(DF_OFF[b], DF_OFF[b] + DF_WID[b])
                    stt(DP[0][:, o], DP[0][:, o], DST[:, 1, 0, b:b + 1], DP[1][:, o], ALU.mult, ALU.add).then_inc(sems["df_a"], 1)
                dve.wait_ge(sems["df_rt"], h + 1)
                dve.reciprocal(DST[:, 0, 0, :], DST[:, 0, 1, :]).then_inc(sems["df_rs"], 1)
                dve.wait_ge(sems["df_bs"], h + 1)
                stt(SQ[:, 2, :], PS[:, 6, :], par("g_subln"), SQ[:, 1, :], ALU.mult, ALU.mult).then_inc(sems["df_w"], 1)
                dve.wait_ge(sems["df_w"], 2 * h + 1)
                stt(SQ[:, 3, :], SQ[:, 2, :], 1.0 - LAM_INIT, GC_[:, 4 + h, :], ALU.mult, ALU.mult).then_inc(sems["df_w"], 1)
                dve.wait_ge(sems["df_w"], 2 * h + 2)
                mix_lo("C.mix", 4 + h, SQ[:, 3, :])

            units("C.out", evac=add_to(XT, "C.out"))
            operand_lo("mem2", MX2, "g_mem", MH2, ML2, MEM)
            for r in range(4):
                if r == 0:
                    invert("mem2", MB)
                split_lo(U0["C.mem"] + 2 * r + 2)
                split_lo(U0["C.mem"] + 2 * r + 3)
            operand_lo("C.cross", XT, "g_cross")
            units("C.cq", norm="C.cross", evac=scaled_to(lambda t: CQ[:, t, :], "C.cq"))
            memory_attention(2, 256 ** -0.5)
            for k in range(KD):
                mix_lo("C.att", k, CQ[:, k, :])
            units("C.co", evac=add_to(XT, "C.co"))
            operand_lo("C.mlp", XT, "g_mlp")
            mlp(2)
            invert("final")
            dve.wait_ge(sems["rs"], bcast_done("final"))
            for k in range(KD):
                stt(Y[:, k, :], XT[:, k, :], par("g_final", k), RS[:, :], ALU.mult, ALU.mult).then_inc(sems["out_ready"], 1)


def kernel(**inputs):
    import concourse.bacc as bacc
    from concourse.bass_utils import run_bass_kernel_spmd

    a = {k: np.asarray(v) for k, v in inputs.items()}
    f = np.float32

    def unit(w, c0, r0=0):
        return w[r0:r0 + D, c0:c0 + UC].reshape(KD, P, UC).transpose(1, 0, 2).reshape(P, KD * UC)

    ws = np.zeros((UNITS, P, KD * UC), f)

    def place(name, w, c0=0, r0=0, at=0, n=None):
        for r in range(NU[name] if n is None else n):
            ws[U0[name] + at + r] = unit(w, c0 + UC * r, r0)

    def place_mlp(name, up, down):
        for q in range(QUARTERS):
            place(name, up, c0=D * q, at=8 * q, n=4)
            place(name, down, r0=D * q, at=8 * q + 4, n=4)

    wa, wb, wc = a["w_in_a"][0], a["w_in_b"][0], a["w_in_2"][0]
    place("A.mem", a["w_mem_kv"][0])
    place("B.mem", a["w_mem_kv"][1])
    place("A.qkv", wa)
    place("A.gate", wa, 3 * W)
    ws[U0["A.bg"]].reshape(P, KD, UC)[:, :, 0:12] = wa[:, 4 * W:4 * W + 12].reshape(KD, P, 12).transpose(1, 0, 2)
    place("A.memq", wa, 4 * W + 12)
    place("A.out", a["w_out"][0])
    place_mlp("A.mlp", a["w_up"][0], a["w_down"][0])
    place("B.qk", wb)
    place("B.v", wb, 2 * W)
    place("B.memq", wb, 3 * W)
    place("B.out", a["w_out"][1])
    place_mlp("B.mlp", a["w_up"][1], a["w_down"][1])
    place("C.u", wc)
    place("C.qk", wc, 512)
    place("C.v", wc, 1536)
    place("C.gate", wc, 2048)
    place("C.out", a["w_out_2"][0])
    place("C.mem", a["w_ckv_2"][0])
    place("C.cq", a["w_cq_2"][0])
    place("C.co", a["w_co_2"][0])
    place_mlp("C.mlp", a["w_up_2"][0], a["w_down_2"][0])

    par = np.zeros((P, NPAR), f)

    def put(name, v):
        par[:, PCOL[name]:PCOL[name] + v.shape[1]] = v

    cols = lambda v: v.reshape(-1, P).T
    rows = lambda v: np.broadcast_to(v.reshape(1, -1), (P, v.size))
    put("mem_norm", cols(a["mem_norm"]))
    for i in range(2):
        for p, n in (("pre_mix", "norm_pre_mix"), ("post_mix", "norm_post_mix"), ("pre_mlp", "norm_pre_mlp"),
                     ("post_mlp", "norm_post_mlp")):
            put(f"{p}{i}", cols(a[n][i]))
    for p, n in (("g_mix", "g_mix_2"), ("g_cross", "g_cross_2"), ("g_mem", "g_mem_2"), ("g_mlp", "g_mlp_2"),
                 ("g_final", "g_final_2"), ("pool_scale", "pool_scale_2")):
        put(p, cols(a[n]))
    put("conv", a["conv_w_a"][0].reshape(4, 18, P).transpose(2, 1, 0).reshape(P, 72))
    put("a_log", rows(np.repeat(a["a_log_a"][0], NB)))
    put("dt", rows(np.repeat(a["dt_bias_a"][0], NB)))
    put("onorm", cols(a["onorm_a"][0]))
    put("g_subln", cols(a["g_subln_2"][0]))
    for p, n in (("lq1", "lambda_q1_2"), ("lk1", "lambda_k1_2"), ("lq2", "lambda_q2_2"), ("lk2", "lambda_k2_2")):
        put(p, rows(a[n][0]))
    put("w_pool", a["w_pool_2"][0].transpose(1, 0, 2).reshape(P, 4 * P))

    con = np.zeros((P, NCON), f)
    r, c = np.arange(P)[:, None], np.arange(P)[None, :]

    def const(name, v, at=0):
        con[:, CCOL[name] + at:CCOL[name] + at + P] = v

    const("ident", r == c)
    const("tri_le", r <= c)
    const("strict", r < c)
    const("cap", np.where(r < c, 3e38, 0))
    const("neg_tri", -(r >= c).astype(f))
    const("neg_ones", -1)
    const("ones", 1)
    const("causal_add", np.where(c <= r, 0, -1e30))
    const("swap", r == (c ^ 32))
    for lv in range(7):
        b = 2 ** lv
        const("level", (r // (2 * b) == c // (2 * b)) & (r % (2 * b) < b) & (c % (2 * b) >= b), lv * P)

    inv = f(10000.0) ** (-np.arange(0, 64, 2, dtype=f) / f(64))
    ang = (np.arange(S, dtype=f)[:, None] * inv[None, :]).astype(f)
    cos, sin = np.cos(ang).T, np.sin(ang).T
    rope = np.stack([np.concatenate([cos] * 4), np.concatenate([-sin, sin] * 2)], 1).astype(f)
    cnt = np.minimum(np.arange(S) + 1, np.array([2, 4, 8, 16])[:, None])
    rcnt = np.ascontiguousarray(np.broadcast_to((1.0 / cnt).astype(f), (P, 4, S)))

    def turned(x):
        return np.ascontiguousarray(x.T.reshape(KD, P, -1).transpose(1, 0, 2))

    arrays = {"weights": ws, "x_t": turned(a["x"][0]), "mem_t": turned(a["mem"][0]), "mem2_t": turned(a["mem_2"][0]),
              "params": par, "consts": con, "rope": rope, "recip_counts": rcnt}
    nc = bacc.Bacc("TRN2", target_bir_lowering=False, num_devices=1)
    aps = [nc.dram_tensor(k, v.shape, mybir.dt.from_np(v.dtype), kind="ExternalInput").ap() for k, v in arrays.items()]
    out = nc.dram_tensor("out_t", (D, S), F32, kind="ExternalOutput").ap()
    program(nc, *aps, out)
    r = run_bass_kernel_spmd(nc, [arrays], core_ids=[0])
    return np.ascontiguousarray(r.results[0]["out_t"].T)[None]
```

```python
import numpy as np
import concourse.bass as bass
from concourse import mybir
from contextlib import ExitStack

F32 = mybir.dt.float32
F32R = mybir.dt.float32r
ALU = mybir.AluOpType
ACT = mybir.ActivationFunctionType
AX = mybir.AxisListType

P = 128
S = 512
D = 1024
KD = D // P
NB = S // P
MEM = 256
MB = MEM // P
W = 768
NT = W // P
H_LIN = 6
UC = 256
EPS = 1e-6
FF = 4096
QUARTERS = FF // D

PHASES = [
    ("A.mem", 2, "act"), ("B.mem", 2, "act"),
    ("A.qkv", 9, "dve"), ("A.memq", 1, "dve"), ("A.bg", 1, "dve"), ("A.gate", 3, "dve"),
    ("A.out", 4, "act"), ("A.mlp", 32, "dve"),
    ("B.qk", 6, "dve"), ("B.v", 3, "dve"), ("B.memq", 1, "dve"), ("B.out", 4, "act"), ("B.mlp", 32, "dve"),
    ("C.u", 2, "dve"), ("C.qk", 4, "dve"), ("C.v", 2, "dve"), ("C.gate", 4, "dve"), ("C.out", 4, "dve"),
    ("C.mem", 8, "act"), ("C.cq", 4, "dve"), ("C.co", 4, "dve"), ("C.mlp", 32, "dve"),
]
U0, NU, KIND = {}, {}, []
for _name, _n, _kind in PHASES:
    U0[_name], NU[_name] = len(KIND), _n
    KIND += [_kind] * _n
UNITS = len(KIND)
EMPTIED = {k: [2 * KIND[:u].count(k) for u in range(UNITS + 1)] for k in ("act", "dve")}

SPLITS = ["mem", "A.in", "A.mix", "A.mlp", "B.in", "B.mix", "B.mlp", "C.in", "C.mix", "mem2", "C.cross", "C.att", "C.mlp"]
SUMS = ["mem", "A.in", "A.post", "A.mlp", "A.post2", "B.in", "B.post", "B.mlp", "B.post2", "C.in", "mem2",
        "C.cross", "C.mlp", "final"]

PARAMS = [("mem_norm", KD), ("pre_mix0", KD), ("pre_mix1", KD), ("post_mix0", KD), ("post_mix1", KD),
          ("pre_mlp0", KD), ("pre_mlp1", KD), ("post_mlp0", KD), ("post_mlp1", KD),
          ("g_mix", KD), ("g_cross", KD), ("g_mem", KD), ("g_mlp", KD), ("g_final", KD),
          ("conv", 18 * 4), ("a_log", 24), ("dt", 24), ("onorm", 1), ("pool_scale", 4), ("g_subln", 1),
          ("lq1", 64), ("lk1", 64), ("lq2", 64), ("lk2", 64), ("w_pool", 4 * P)]
PCOL, _at = {}, 0
for _name, _n in PARAMS:
    PCOL[_name] = _at
    _at += _n
NPAR = _at

CONSTS = [("ident", P), ("tri_le", P), ("strict", P), ("cap", P), ("neg_tri", P), ("neg_ones", P), ("ones", P),
          ("level", 7 * P), ("causal_add", P), ("swap", P)]
CCOL, _at = {}, 0
for _name, _n in CONSTS:
    CCOL[_name] = _at
    _at += _n
NCON = _at

SB_OFF = [0, 512, 1024, 896]
SB_WID = [512, 384, 256, 128]
SB_ALL = 1280
DF_OFF = [896, 1024, 512, 0]
DF_WID = [128, 256, 384, 512]
LAM_INIT = 0.8 - 0.6


SEMAPHORES = """
at bc bcast_mm bg bg_tr bt cb_zero const_in conv conv0 df_a df_at df_bc df_exp df_g df_mask df_max
df_nm df_o df_r0 df_ri df_rs df_rt df_s df_sq df_ss df_tr df_w dt_exp dt_pre dtm eg_exp
emptied_act emptied_dve eps gate_silu gated gc_mm head_sc hh hi hl kbt kn kv_t kv_tr l2rt l2sq
l2ss lam lam_act lo load0 load1 lt lt_mm lv_p lv_x lv_y lv_yc ma_exp ma_max ma_nm ma_o ma_out ma_p
ma_pt ma_ri ma_s ma_tr mem2_in mem_in0 mem_in1 mixed o_done obc obs ors ort osq oss out_dma
out_ready ow par_in pool_mm pool_s pool_z q_scaled qd rcnt_in rk rope_cos rope_done rope_in
rope_mm rope_sin rows rq rs rsc rv sb_a sb_az sb_cap sb_e sb_l sb_m sb_o sb_rc sb_sp sb_t sb_z
sc_act sc_dve sc_o sc_ws sig silu sq sqa sqrt ss st tile u_mm u_sb uh ul v_copy vn vrow vtr w_sb
x_in x_new y_scaled y_zero
"""


def program(nc, ws, xt_in, memt_in, memt2_in, par_in, con_in, rope_in, rcnt_in, out):
    ctx = ExitStack()
    with ctx:
        def sb(name, shape, dt=F32, scope=ctx):
            return scope.enter_context(nc.sbuf_tensor(name, shape, dt))

        sems = {}

        for name in SEMAPHORES.split():
            sems[name] = ctx.enter_context(nc.semaphore(name))

        with ExitStack() as sc:
            GATES = sb("GATES", [P, NT, S], scope=sc)
        HL = sb("HL", [P, KD, S], F32R)
        HH = sb("HH", [P, KD, S], F32R)
        XT = sb("XT", [P, KD, S])
        STG = [sb(f"STG{i}", [P, KD, UC]) for i in range(2)]
        WH = [sb(f"WH{i}", [P, KD, UC], F32R) for i in range(2)]
        WL = [sb(f"WL{i}", [P, KD, UC], F32R) for i in range(2)]
        Y = sb("Y", [P, KD, S])
        SQ = sb("SQ", [P, 4, S])
        SQA = sb("SQA", [P, S])
        RS = sb("RS", [P, S])
        RT = sb("RT", [P, NB])
        RSC = sb("RSC", [P, NB])
        CON = sb("CON", [P, NCON])
        PAR = sb("PAR", [P, NPAR])
        EPST = sb("EPST", [P, 1])
        ONE1 = sb("ONE1", [P, 1])
        KT_MEM = [sb(f"KT_MEM{i}", [P, 2, MEM]) for i in range(2)]
        V_MEM = [sb(f"V_MEM{i}", [P, MB, UC]) for i in range(2)]
        MST = sb("MST", [P, 2, 4, NB])
        PS = ctx.enter_context(nc.psum_tensor("PS", [P, 8, 512], F32))
        PSF = PS[:, :, :].rearrange("p b n -> p (b n)")

        def con(name, width=P):
            return CON[:, CCOL[name]:CCOL[name] + width]

        def par(name, i=0, n=1):
            return PAR[:, PCOL[name] + i:PCOL[name] + i + n]

        def tile(t, i):
            if isinstance(i, int):
                return t[:, i, :]
            return t[:, bass.ds(i, 1), :].rearrange("p a n -> p (a n)")

        with ExitStack() as sc:
            MX = sb("MX", [P, KD, MEM], scope=sc)
            MH = sb("MH", [P, KD, MEM], F32R, scope=sc)
            ML = sb("ML", [P, KD, MEM], F32R, scope=sc)
            KR = sb("KR", [P, MB, UC], scope=sc)
        with ExitStack() as sc:
            QKV = sb("QKV", [P, 3 * NT, S], scope=sc)
            MQ = sb("MQ", [P, 2, S], scope=sc)
            CX = sb("CX", [P, 2, S], scope=sc)
            BGT = sb("BGT", [12, S], scope=sc)
            BG = sb("BG", [P, 12, NB], scope=sc)
            SC = sb("SC", [P, H_LIN, 8, NB], scope=sc)
            SMALL = sb("SMALL", [P, 8, 24], scope=sc)
            RQK = sb("RQK", [P, 2 * NT, NB], scope=sc)
            HS = [sb(f"HS{i}", [P, 8, NB], scope=sc) for i in range(2)]
            ORT = [sb(f"ORT{i}", [P, 2, NB], scope=sc) for i in range(2)]
            ST8 = [sb(f"ST8{i}", [P, P], scope=sc) for i in range(2)]
            VN = [sb(f"VN{i}", [P, P], scope=sc) for i in range(2)]
            TMP = [[sb(f"TMP{i}_{j}", [P, S], scope=sc) for j in range(3)] for i in range(2)]
        with ExitStack() as sc:
            UPH = sb("UPH", [P, KD, S], F32R, scope=sc)
            UPL = sb("UPL", [P, KD, S], F32R, scope=sc)
            RR = sb("RR", [P, 2, S], scope=sc)
            RQ = sb("RQ", [P, 2, S], scope=sc)
        with ExitStack() as sc:
            QKB = sb("QKB", [P, 2 * NT, S], scope=sc)
            QB, KB = QKB[:, 0:NT, :], QKB[:, NT:2 * NT, :]
            MO = sb("MO", [P, 2, S], scope=sc)
            VB = sb("VB", [P, NT, NB, P], scope=sc)
            MQB = sb("MQB", [P, 2, S], scope=sc)
            TAIL = sb("TAIL", [P, 2, 640], scope=sc)
            ABUF = sb("ABUF", [P, SB_ALL], scope=sc)
        with ExitStack() as sc:
            QC = sb("QC", [P, 4, S], scope=sc)
            KC = sb("KC", [P, 4, S], scope=sc)
            VC = sb("VC", [P, 4, NB, P], scope=sc)
            UT = sb("UT", [P, 4, 16 + S], scope=sc)
            GC_ = sb("GC_", [P, KD, S], scope=sc)
            COSIN = sb("COSIN", [P, 2, S], scope=sc)
            LAM = sb("LAM", [P, 8], scope=sc)
            PA = sb("PA", [P, 2, 16 + S], scope=sc)
            DST = sb("DST", [P, 5, 4 * NB], scope=sc)
            DMX = sb("DMX", [P, 2, 2, NB], scope=sc)
        with ExitStack() as sc:
            CQ = sb("CQ", [P, KD, S], scope=sc)
            MX2 = sb("MX2", [P, KD, MEM], scope=sc)
            MH2 = sb("MH2", [P, KD, MEM], F32R, scope=sc)
            ML2 = sb("ML2", [P, KD, MEM], F32R, scope=sc)
            CK = sb("CK", [P, KD, MEM], scope=sc)
            CV = sb("CV", [P, MB, D], scope=sc)

        YF = Y[:, :, :].rearrange("p k n -> p (k n)")
        CONV_IN = [YF[:, 0:515], YF[:, 520:1035]]
        CONV_ACC = [YF[:, 1040:1552], YF[:, 1560:2072]]
        PROB = [YF[:, 1024 * e:1024 * e + 1024] for e in range(2)]
        PROBT = [YF[:, 2048 + 1024 * e:3072 + 1024 * e] for e in range(2)]
        SP = [YF[:, SB_ALL * e:SB_ALL * (e + 1)] for e in range(2)]
        AW = [ABUF[:, :], YF[:, 2 * SB_ALL:3 * SB_ALL]]
        DP0 = [YF[:, SB_ALL * e:SB_ALL * (e + 1)] for e in range(2)]
        DP1 = YF[:, 2 * SB_ALL:3 * SB_ALL]
        DAT = UT[:, :, :].rearrange("p g n -> p (g n)")
        SUM0, SUM1, COEF, RI0, RMSD = (DST[:, i, :] for i in range(5))
        RCNT = Y[:, 4:8, :]
        T9 = [[Y[:, 4 * e + i, :] for i in range(4)] + [SQ[:, 2 * e + i, :] for i in range(2)] +
              [TMP[e][i][:, :] for i in range(3)] for e in range(2)]
        KNS, KBT, DT, LT, AT, XTr, BT, RK, KDC = ([T9[e][i] for e in range(2)] for i in range(9))
        WT, XX, YT, VS, EG = KNS, KBT, DT, XTr, KDC

        def blk(ap, b, n=P):
            return ap[:, b * n:(b + 1) * n]

        def blocks(ap):
            return ap.rearrange("p (b n) -> p b n", b=NB)

        def lin(base, step, i):
            return base if i is None else i * step + base

        def bc_blocks(ap):
            return ap.unsqueeze(1).to_broadcast([P, NB, P])

        def per_block(ap):
            return ap.unsqueeze(2).to_broadcast([P, NB, P])

        def segments(name):
            u, n = U0[name], NU[name]
            head = n if n < 6 or name.endswith("mlp") else 2 + n % 2
            out_ = [(u + r, None) for r in range(head)]
            if head < n:
                out_.append((u + head, (n - head) // 2))
            return out_

        def run_phase(eng, name, fn):
            for u, pairs in segments(name):
                if pairs is None:
                    fn(u, None, 0)
                else:
                    with eng.Fori(0, pairs) as i:
                        fn(u, i, 2)
                        fn(u + 1, i, 2)

        def emptied(kind, u, j, i=None, step=0):
            return lin(EMPTIED[kind][u] + j + 1, 2 * step, i)

        SQ_BASE = {name: 8 * n for n, name in enumerate(SUMS)}
        NORMS = [n for n in SUMS if not n.startswith("mem")]

        def sums_done(n):
            return SUMS.index(n) + 1

        def bcast_done(n):
            return NORMS.index(n) + 1

        def split_done(q, k):
            return 8 * SPLITS.index(q) + k + 1

        def added(m):
            return 7 * (m // 8) + max(m % 8, 1)

        POSTS = ["A.post", "A.post2", "B.post", "B.post2"]
        VIDX = {"B.v": 0, "C.v": 6}

        block = ctx.enter_context(nc.Block())

        @block.sync
        def _(sp):
            for v in range(2):
                sp.dma_start(STG[v][:, :, :].rearrange("p k n -> p (k n)"), ws[v]).then_inc(sems[f"load{v}"], 16)
            with sp.Fori(1, UNITS // 2) as i:
                for j in range(2):
                    sp.wait_ge(sems["lo"], lin(j - 1, 2, i))
                    sp.dma_start(STG[j][:, :, :].rearrange("p k n -> p (k n)"),
                                 ws[bass.ds(i * 2 + j, 1)].rearrange("a p n -> p (a n)")).then_inc(sems[f"load{j}"], 16)
            for k in range(KD):
                sp.wait_ge(sems["out_ready"], k + 1)
                sp.dma_start(out[k * P:(k + 1) * P, :], Y[:, k, :]).then_inc(sems["out_dma"], 16)
            sp.wait_ge(sems["out_dma"], 16 * KD)

        @block.gpsimd
        def _(pool):
            pool.memset(EPST[:, :], EPS).then_inc(sems["eps"], 1)
            pool.memset(ONE1[:, :], 1.0).then_inc(sems["eps"], 1)
            for e in range(2):
                pool.memset(CONV_IN[e][:, 0:3], 0.0).then_inc(sems["cb_zero"], 1)

            def sum_squares(name, n=S):
                base = SQ_BASE[name]
                a0 = 7 * SUMS.index(name)
                for k in range(1, KD):
                    pool.wait_ge(sems["sq"], base + k + 1)
                    if k == 1:
                        if a0:
                            pool.wait_ge(sems["ss"], SUMS.index(name))
                        pool.tensor_tensor(SQA[:, 0:n], SQ[:, base % 4, 0:n], SQ[:, (base + 1) % 4, 0:n],
                                           ALU.add).then_inc(sems["sqa"], 1)
                    else:
                        pool.wait_ge(sems["sqa"], a0 + k - 1)
                        pool.tensor_tensor(SQA[:, 0:n], SQA[:, 0:n], SQ[:, (base + k) % 4, 0:n],
                                           ALU.add).then_inc(sems["sqa"], 1)

            def add_to_stream(name):
                for k in range(KD):
                    pool.wait_ge(sems["y_scaled"], 8 * POSTS.index(name) + k + 1)
                    pool.tensor_tensor(XT[:, k, :], XT[:, k, :], Y[:, k, :], ALU.add).then_inc(sems["x_new"], 1)

            def zero_y(L):
                pool.wait_ge(sems["x_new"], 16 * L + 8)
                pool.memset(Y[:, :, :], 0.0).then_inc(sems["y_zero"], 1)

            sum_squares("mem", MEM)
            sum_squares("A.in")
            pool.wait_ge(sems["gate_silu"], NT)
            with pool.Fori(0, H_LIN // 2) as g:
                for e in range(2):
                    pool.wait_ge(sems["lt"], lin(e + 1, 2, g))
                for lv in range(7):
                    for e in range(2):
                        if lv:
                            pool.wait_ge(sems["lv_y"], lin(2 * (lv - 1) + e + 1, 14, g))
                            if lv == 1:
                                pool.wait_ge(sems["lv_x"], lin(e + 1, 14, g))
                        pool.tensor_tensor(blocks(BT[e]), blocks(LT[e]), bc_blocks(con("level", 7 * P)[:, lv * P:(lv + 1) * P]),
                                           ALU.mult).then_inc(sems["bt"], 1)
                for e in range(2):
                    pool.wait_ge(sems["o_done"], lin(e + 1, 2, g))
            sum_squares("A.post")
            add_to_stream("A.post")
            zero_y(0)
            sum_squares("A.mlp")
            sum_squares("A.post2")
            add_to_stream("A.post2")
            sum_squares("B.in")
            sum_squares("B.post")
            add_to_stream("B.post")
            zero_y(1)
            sum_squares("B.mlp")
            sum_squares("B.post2")
            add_to_stream("B.post2")
            pool.wait_ge(sems["emptied_dve"], emptied("dve", U0["B.mlp"] + 31, 1))
            pool.dma_start(COSIN[:, :, :], rope_in).then_inc(sems["rope_in"], 16)
            sum_squares("C.in")
            pool.wait_ge(sems["x_new"], 32)
            pool.dma_start(RCNT, rcnt_in).then_inc(sems["rcnt_in"], 16)
            pool.wait_ge(sems["hl"], split_done("C.mix", 7))
            pool.dma_start(MX2[:, :, :], memt2_in).then_inc(sems["mem2_in"], 16)
            sum_squares("mem2", MEM)
            sum_squares("C.cross")
            sum_squares("C.mlp")
            sum_squares("final")

        @block.tensor
        def _(pe):
            I_ = con("ident")

            def mm(o, l, r, start, stop, **kw):
                return pe.matmul(o, l, r, start=start, stop=stop, **kw)

            def sum_tokens(name, nt=NB):
                pe.wait_ge(sems["sqa"], 7 * sums_done(name))
                before = sum(1 for x in NORMS if SUMS.index(x) < SUMS.index(name))
                if before:
                    pe.wait_ge(sems["rs"], before)
                for b in range(nt):
                    last = mm(PS[:, 4, b:b + 1], blk(SQA[:, :], b), con("ones")[:, 0:1], True, True)
                last.then_inc(sems["ss"], 1)

            def spread_tokens(name):
                pe.wait_ge(sems["rsc"], sums_done(name))
                for b in range(NB):
                    last = mm(PS[:, 4, b * P:(b + 1) * P], RSC[:, b:b + 1].to_broadcast([P, P]), I_, True, True)
                last.then_inc(sems["bc"], 1)

            def wait_bank(u, j, i=None, step=0):
                if u >= 2:
                    kind = KIND[u - 2]
                    pe.wait_ge(sems[f"emptied_{kind}"], emptied(kind, u - 2, j, i, step))

            def product(u, i, step, xh, xl, split=None, between=None, tiles=2, ready="hl", halfway=None):
                s = u % 2
                pe.wait_ge(sems["lo"], lin(u + 1, step, i))

                def step_k(j, k):
                    bank = PS[:, 2 * s + j, :]
                    wh, wl = WH[s][:, k, j * P:(j + 1) * P], WL[s][:, k, j * P:(j + 1) * P]
                    mm(bank, wh, xh[:, k, :], k == 0, False)
                    mm(bank, wh, xl[:, k, :], False, False)
                    return mm(bank, wl, xh[:, k, :], False, k == KD - 1)

                if split is not None:
                    wait_bank(u, 0, i, step)
                    wait_bank(u, 1, i, step)
                    for k in range(KD):
                        if halfway and k == KD // 2:
                            halfway()
                        pe.wait_ge(sems[ready], split(k))
                        for j in range(2):
                            last = step_k(j, k)
                            if k == KD - 1:
                                last.then_inc(sems["tile"], 1)
                    return
                for j in range(tiles):
                    wait_bank(u, j, i, step)
                    for k in range(KD):
                        last = step_k(j, k)
                    last.then_inc(sems["tile"], 3 - tiles)
                    if between and j == 0:
                        between()

            def projection(name, split=None, norm=None, after=None, halfway=None):
                def fn(u, i, step):
                    r = u - U0[name]
                    first = r == 0 and i is None
                    product(u, i, step, HH, HL,
                            split=(lambda k: split_done(split, k)) if first and split else None,
                            between=(lambda: spread_tokens(norm)) if norm and r == 1 and i is None else None,
                            tiles=1 if name == "A.bg" else 2, halfway=halfway if first else None)
                    if norm and first:
                        sum_tokens(norm)
                    if after and r:
                        after(r - 1)
                run_phase(pe, name, fn)
                if after:
                    after(NU[name] - 1)

            def memory_rows(u, xh, xl, split=None):
                s = u % 2
                pe.wait_ge(sems["lo"], u + 1)
                for t in range(MB):
                    wait_bank(u, t)
                    bank = PS[:, 2 * s + t, 0:UC]
                    xs = slice(t * P, (t + 1) * P)
                    for k in range(KD):
                        if split is not None and t == 0:
                            pe.wait_ge(sems["hl"], split_done(split, k))
                        mm(bank, xh[:, k, xs], WH[s][:, k, :], k == 0, False)
                        mm(bank, xl[:, k, xs], WH[s][:, k, :], False, False)
                        last = mm(bank, xh[:, k, xs], WL[s][:, k, :], False, k == KD - 1)
                    last.then_inc(sems["tile"], 1)

            def memory_attention(a, q, k, v, chunks, dh):
                def scores(h):
                    e = h % 2
                    if h >= 2:
                        pe.wait_ge(sems["ma_exp"], 4 * (4 * a + h - 1))
                    for b in range(NB):
                        for c in range(chunks):
                            last = mm(PSF[:, (4 * e) * 512 + b * MEM:(4 * e) * 512 + (b + 1) * MEM], blk(q(h, c), b), k(h, c),
                                      c == 0, c == chunks - 1)
                    last.then_inc(sems["ma_s"], 1)

                def turn(h):
                    e = h % 2
                    pe.wait_ge(sems["ma_p"], 4 * a + h + 1)
                    if h >= 2:
                        pe.wait_ge(sems["ma_out"], 4 * a + h - 1)
                    for b in range(NB):
                        for m in range(MB):
                            last = pe.transpose(PS[:, 4 * e + 2 + m, b * P:(b + 1) * P],
                                                PROB[e][:, b * MEM + m * P:b * MEM + (m + 1) * P], I_)
                    last.then_inc(sems["ma_tr"], 1)

                def weigh(h):
                    e = h % 2
                    pe.wait_ge(sems["ma_pt"], 4 * a + h + 1)
                    for c in range(chunks):
                        for m in range(MB):
                            o = PS[e * 64:e * 64 + 64, 4 * e + 2, :] if dh == 64 else PS[:, 4 * e + 2 + c, :]
                            last = mm(o, v(h, c, m), blk(PROBT[e], m, 512), m == 0, m == MB - 1)
                    last.then_inc(sems["ma_o"], 1)

                scores(0)
                scores(1)
                for h in range(4):
                    if h + 2 < 4:
                        scores(h + 2)
                    turn(h)
                    if h:
                        weigh(h - 1)
                weigh(3)

            def turn_values(name):
                def fn(r):
                    for j in range(2):
                        t = 2 * r + j
                        vi = VIDX[name] + t
                        pe.wait_ge(sems["emptied_dve"], emptied("dve", U0[name] + r, j))
                        if vi >= 2:
                            pe.wait_ge(sems["vrow"], vi - 1)
                        for b in range(NB):
                            last = pe.transpose(PS[:, 5 + t % 2, b * P:(b + 1) * P], blk(Y[:, t % 2, :], b), I_)
                        last.then_inc(sems["vtr"], 1)
                return fn

            def mlp(L):
                name = "ABC"[L] + ".mlp"
                ub = U0[name]
                n4 = 4
                for r in range(n4):
                    product(ub + r, None, 0, HH, HL, split=(lambda k: split_done(name, k)) if r == 0 else None,
                            between=(lambda: spread_tokens(name)) if r == 1 else None)
                    if r == 0:
                        sum_tokens(name)
                with pe.Fori(0, QUARTERS - 1) as q:
                    for r in range(n4):
                        product(ub + 4 + r, q, 8, UPH, UPL, ready="ul",
                                split=(lambda k: lin(32 * L + k + 1, 8, q)) if r == 0 else None)
                    for r in range(n4):
                        product(ub + 8 + r, q, 8, HH, HL)
                for r in range(n4):
                    product(ub + 28 + r, None, 0, UPH, UPL, ready="ul",
                            split=(lambda k: 32 * L + 24 + k + 1) if r == 0 else None)

            def finish_post(name):
                sum_tokens(name)
                spread_tokens(name)

            def delta_net():
                def per(n, k, e, g):
                    return lin(2 * (k - 1) + e + 1, 2 * n, g)
                with pe.Fori(0, H_LIN // 2) as g:
                    for e in range(2):
                        pe.wait_ge(sems["head_sc"], per(1, 1, e, g))
                        for ty, (o, r) in enumerate([(0, con("tri_le")), (1, I_), (2, I_)]):
                            for b in range(NB):
                                last = mm(PS[:, 4 * e + o, b * P:(b + 1) * P],
                                          HS[e][:, ty, b:b + 1].to_broadcast([P, P]), r, True, True)
                        last.then_inc(sems["bcast_mm"], 1)
                    for e in range(2):
                        pe.wait_ge(sems["kbt"], per(1, 1, e, g))
                        for b in range(NB):
                            last = mm(PS[:, 4 * e + 1, b * P:(b + 1) * P], blk(KNS[e], b), blk(KBT[e], b), True, True)
                        last.then_inc(sems["lt_mm"], 1)
                        qn = QKV[:, bass.ds(g * 2 + e, 1), :].rearrange("p a n -> p (a n)")
                        for b in range(NB):
                            mm(PS[:, 4 * e + 2, b * P:(b + 1) * P], blk(KNS[e], b), blk(qn, b), True, True)
                        for b in range(NB):
                            pe.transpose(PS[:, 4 * e + 3, b * P:(b + 1) * P], blk(KNS[e], b), I_)
                        pe.wait_ge(sems["v_copy"], per(1, 1, e, g))
                        pe.wait_ge(sems["eg_exp"], per(1, 1, e, g))
                        pe.wait_ge(sems["dt_pre"], per(1, 1, e, g))
                        for b in range(NB):
                            last = pe.transpose(PS[:, 4 * e, b * P:(b + 1) * P], blk(VS[e], b), I_)
                        last.then_inc(sems["rows"], 1)
                    for lv in range(7):
                        for e in range(2):
                            pe.wait_ge(sems["bt"], lin(2 * lv + e + 1, 14, g))
                            if lv:
                                pe.wait_ge(sems["lv_x"], per(7, lv, e, g))
                            for b in range(NB):
                                last = mm(PS[:, 4 * e + 1, b * P:(b + 1) * P], blk(BT[e], b),
                                          blk(XX[e], b) if lv else I_, True, True)
                            last.then_inc(sems["lv_y"], 1)
                        if lv == 0:
                            continue
                        for e in range(2):
                            pe.wait_ge(sems["lv_yc"], per(6, lv, e, g))
                            if lv == 1:
                                pe.wait_ge(sems["rk"], per(1, 1, e, g))
                                pe.wait_ge(sems["at"], per(1, 1, e, g))
                            if lv < 6:
                                for b in range(NB):
                                    mm(PS[:, 4 * e + 2, b * P:(b + 1) * P], blk(XTr[e], b), blk(YT[e], b), True, True)
                            for b in range(NB):
                                last = mm(PS[:, 4 * e + 3, b * P:(b + 1) * P], blk(YT[e], b), blk(XTr[e], b), True, True)
                            last.then_inc(sems["lv_p"], 1)
                    for e in range(2):
                        pe.wait_ge(sems["lv_x"], per(7, 7, e, g))
                        pe.wait_ge(sems["rv"], per(1, 1, e, g))
                        rv = QKV[:, bass.ds(g * 2 + 12 + e, 1), :].rearrange("p a n -> p (a n)")
                        for b in range(NB):
                            mm(PS[:, 4 * e, b * P:(b + 1) * P], blk(XTr[e], b), blk(rv, b), True, True)
                        for b in range(NB):
                            last = mm(PS[:, 4 * e + 1, b * P:(b + 1) * P], blk(RK[e], b), blk(XTr[e], b), True, True)
                        last.then_inc(sems["u_mm"], 1)
                    for b in range(NB):
                        if b:
                            for e in range(2):
                                pe.wait_ge(sems["st"], per(3, b, e, g))
                                pe.wait_ge(sems["w_sb"], per(1, 1, e, g))
                                mm(PS[:, 4 * e + 2, 0:P], blk(WT[e], b), ST8[e][:, :], True, True).then_inc(sems["sc_ws"], 1)
                        for e in range(2):
                            qd = QKV[:, bass.ds(g * 2 + e, 1), :].rearrange("p a n -> p (a n)")
                            pe.wait_ge(sems["vn"], per(4, b + 1, e, g))
                            o = PS[:, 4 * e + 3, b * P:(b + 1) * P]
                            if b:
                                mm(o, ST8[e][:, :], blk(qd, b), True, False)
                            mm(o, VN[e][:, :], blk(AT[e], b), b == 0, True)
                            last = mm(PS[:, 4 * e + 2, P:2 * P], blk(KDC[e], b), VN[e][:, :], True, True)
                            last.then_inc(sems["sc_o"], 1)
                    for e in range(2):
                        pe.wait_ge(sems["osq"], per(1, 1, e, g))
                        for b in range(NB):
                            last = mm(PS[:, 4 * e + 1, b:b + 1], blk(YT[e], b), con("ones")[:, 0:1], True, True)
                        last.then_inc(sems["oss"], 1)
                    for e in range(2):
                        pe.wait_ge(sems["ors"], per(1, 1, e, g))
                        for b in range(NB):
                            last = mm(PS[:, 4 * e, b * P:(b + 1) * P], ORT[e][:, 1, b:b + 1].to_broadcast([P, P]), I_, True, True)
                        last.then_inc(sems["obc"], 1)
                    for e in range(2):
                        pe.wait_ge(sems["o_done"], per(1, 1, e, g))

            def stick_breaking():
                def head(x, n):
                    return x[(n % 2) * 64:(n % 2) * 64 + 64, n // 2, :]

                def region(n, j, skip=0):
                    o = 1536 * (n % 2) + SB_OFF[j]
                    return PSF[:, o + skip * P:o + SB_WID[j]]

                def scores(n):
                    if n >= 2:
                        pe.wait_ge(sems["sb_a"], n - 1)
                    for j in (0, 1, 3, 2):
                        last = mm(region(n, j), blk(head(KB, n), j), head(QB, n)[:, j * P:S], j != 3, False,
                                  skip_group_check=True)
                    last.then_inc(sems["sb_z"], 1)

                def tails(n):
                    e = n % 2
                    pe.wait_ge(sems["sb_t"], 2 * n + 2)
                    for j in range(NB):
                        if j < NB - 1:
                            src = SP[e][:, SB_OFF[3]:SB_OFF[3] + P] if j == 2 else \
                                TAIL[:, e, 256:640] if j == 0 else TAIL[:, e, 0:256]
                            mm(region(n, j, 1), con("neg_ones"), src, False, False, skip_group_check=True)
                        last = mm(region(n, j), con("neg_tri"), SP[e][:, SB_OFF[j]:SB_OFF[j] + SB_WID[j]],
                                  False, True, skip_group_check=True)
                    last.then_inc(sems["sb_rc"], 1)

                def apply(n):
                    e = n % 2
                    pe.wait_ge(sems["sb_cap"], 2 * n + 2)
                    if n >= 4:
                        pe.wait_ge(sems["hl"], split_done("B.mix", n // 2 - 2))
                    for j in range(NB):
                        last = mm(PS[64 * e:64 * e + 64, 6 + n // 2 % 2, j * P:S], VB[:, n // 2, j, 64 * e:64 * e + 64],
                                  AW[e][:, SB_OFF[j]:SB_OFF[j] + SB_WID[j]], j == 0, j == NB - 1)
                    last.then_inc(sems["sb_o"], 1)

                scores(0)
                scores(1)
                for n in range(12):
                    tails(n)
                    if n:
                        apply(n - 1)
                    if n + 2 < 12:
                        scores(n + 2)
                apply(11)
                pe.wait_ge(sems["hl"], split_done("B.mix", NT - 1))

            def rope_swap(t):
                pe.wait_ge(sems["emptied_dve"], emptied("dve", U0["C.qk"] + t // 2, t % 2))
                if t:
                    pe.wait_ge(sems["rope_sin"], t)
                x = (QC if t < 4 else KC)[:, t % 4, :]
                mm(PS[:, 7, :], con("swap"), x, True, True).then_inc(sems["rope_mm"], 1)

            def rope_projection(name, slots, after=None):
                late = []
                for r in range(NU[name]):
                    product(U0[name] + r, None, 0, HH, HL,
                            between=(lambda: rope_swap(late.pop())) if late else None)
                    if after and r:
                        after(r - 1)
                    for n, t in enumerate(slots[r]):
                        if n == 0:
                            rope_swap(t)
                        else:
                            late.append(t)
                if after:
                    after(NU[name] - 1)

            def layer_c_mixer():
                def scores(h, c):
                    if h == 0:
                        if c == 0:
                            pe.wait_ge(sems["rope_done"], 8)
                            pe.wait_ge(sems["emptied_dve"], emptied("dve", U0["C.gate"] + 3, 1))
                            pe.wait_ge(sems["vrow"], 10)
                    else:
                        pe.wait_ge(sems["df_exp"], 8 * (h - 1) + 4 * c + 4)
                    for b in (3, 2, 0, 1):
                        o = 1536 * c + DF_OFF[b]
                        last = mm(PSF[:, o:o + DF_WID[b]], QC[64 * c:64 * c + 64, h, b * P:(b + 1) * P],
                                  KC[64 * c:64 * c + 64, h, 0:DF_WID[b]], True, True)
                    last.then_inc(sems["df_s"], 1)

                def turn(h, r):
                    n = 3 * h + r
                    if n:
                        pe.wait_ge(sems["df_at"], n)
                    for j in ((0,), (1, 3), (2,))[r]:
                        for b in range(j, NB):
                            o = SB_OFF[j] + (b - j) * P - 512 * r
                            last = pe.transpose(PS[:, 7, o:o + P], DP0[h % 2][:, DF_OFF[b] + j * P:DF_OFF[b] + (j + 1) * P], I_)
                    last.then_inc(sems["df_tr"], 1)

                def apply(h, r):
                    pe.wait_ge(sems["df_at"], 3 * h + r + 1)
                    if h and r == 0:
                        pe.wait_ge(sems["df_sq"], h)
                    for j in ((0,), (1, 3), (2,))[r]:
                        last = mm(PS[:, 6, j * P:S], VC[:, h, j, :], DAT[:, SB_OFF[j]:SB_OFF[j] + SB_WID[j]], r == 0, r == 2,
                                  skip_group_check=True)
                    if r == 2:
                        last.then_inc(sems["df_o"], 1)

                scores(0, 0)
                scores(0, 1)
                for g in range(4):
                    pe.wait_ge(sems["pool_z"], g + 1)
                    if g >= 2:
                        pe.wait_ge(sems["mixed"], g - 1)
                    elif g == 1:
                        pe.wait_ge(sems["rope_sin"], 8)
                    mm(PS[:, 6 + g % 2, :], par("w_pool", g * P, P), UT[:, g, 16:16 + S], True, True).then_inc(sems["pool_mm"], 1)
                for h in range(4):
                    if h < 3:
                        scores(h + 1, 0)
                        scores(h + 1, 1)
                    pe.wait_ge(sems["df_a"], 4 * h + 4)
                    if h == 0:
                        pe.wait_ge(sems["mixed"], 4)
                    turn(h, 0)
                    turn(h, 1)
                    apply(h, 0)
                    turn(h, 2)
                    apply(h, 1)
                    apply(h, 2)
                pe.wait_ge(sems["df_sq"], 4)
                pe.wait_ge(sems["df_at"], 12)
                for h in range(4):
                    for b in range(NB):
                        last = mm(PS[:, 7, NB * h + b:NB * h + b + 1], blk(SQ[:, h, :], b), con("ones")[:, 0:1], True, True)
                last.then_inc(sems["df_ss"], 1)

            def head_factors():
                pe.wait_ge(sems["df_rs"], 3)
                for h in range(4):
                    for b in range(NB):
                        last = mm(PS[:, 4 + h, b * P:(b + 1) * P], COEF[:, NB * h + b:NB * h + b + 1].to_broadcast([P, P]),
                                  I_, True, True)
                    last.then_inc(sems["df_bc"], 1)

            for L in range(2):
                u = U0["AB"[L] + ".mem"]
                memory_rows(u, MH, ML, "mem" if L == 0 else None)
                if L == 0:
                    pe.wait_ge(sems["const_in"], 16)
                    sum_tokens("mem", MB)
                memory_rows(u + 1, MH, ML)
                pe.wait_ge(sems["emptied_act"], emptied("act", u, 1))
                if L:
                    pe.wait_ge(sems["kv_t"], 1)
                for f in range(2):
                    for t in range(MB):
                        last = pe.transpose(PS[:, 5, f * MEM + t * P:f * MEM + (t + 1) * P], KR[:, t, f * P:(f + 1) * P], I_)
                last.then_inc(sems["kv_tr"], 1)

            projection("A.qkv", split="A.in", norm="A.in")
            projection("A.memq")
            projection("A.bg")
            pe.wait_ge(sems["kv_t"], 2)

            def beside_gate(n):
                for t in (2 * n, 2 * n + 1):
                    pe.wait_ge(sems["l2sq"], t + 1)
                    for b in range(NB):
                        last = mm(PS[:, 6, NB * t + b:NB * t + b + 1], blk(SQ[:, t % 4, :], b), con("ones")[:, 0:1], True, True)
                    last.then_inc(sems["l2ss"], 1)
                if n == 0:
                    pe.wait_ge(sems["emptied_dve"], emptied("dve", U0["A.bg"], 1))
                    for b in range(NB):
                        last = pe.transpose(PS[:, 5, b * 12:(b + 1) * 12], blk(BGT[:, :], b), I_[0:12, 0:12])
                    last.then_inc(sems["bg_tr"], 1)
                if n == 3:
                    pe.wait_ge(sems["sc_dve"], 4)
                    mm(PS[:, 5, 64:88], con("tri_le"), SC[:, :, 0, :], True, True)
                    mm(PS[:, 5, 96:120], con("ones"), SC[:, :, 0, :], True, True).then_inc(sems["gc_mm"], 1)

            for r in range(NU["A.gate"]):
                product(U0["A.gate"] + r, None, 0, HH, HL, between=lambda: beside_gate(2 * r))
                beside_gate(2 * r + 1)
            pe.wait_ge(sems["emptied_dve"], emptied("dve", U0["A.gate"] + 2, 1))
            delta_net()
            memory_attention(0, lambda h, c: MQ[(h % 2) * 64:(h % 2) * 64 + 64, h // 2, :],
                             lambda h, c: KT_MEM[0][(h % 2) * 64:(h % 2) * 64 + 64, h // 2, :],
                             lambda h, c, m: V_MEM[0][:, m, h * 64:h * 64 + 64], 1, 64)
            projection("A.out", split="A.mix")
            finish_post("A.post")
            mlp(0)
            finish_post("A.post2")

            projection("B.qk", split="B.in", norm="B.in")
            projection("B.v", after=turn_values("B.v"))
            projection("B.memq")
            pe.wait_ge(sems["vrow"], 6)
            pe.wait_ge(sems["q_scaled"], 1)
            stick_breaking()
            memory_attention(1, lambda h, c: MQB[(h % 2) * 64:(h % 2) * 64 + 64, h // 2, :],
                             lambda h, c: KT_MEM[1][(h % 2) * 64:(h % 2) * 64 + 64, h // 2, :],
                             lambda h, c, m: V_MEM[1][:, m, h * 64:h * 64 + 64], 1, 64)
            projection("B.out", split="B.mix")
            finish_post("B.post")
            mlp(1)
            finish_post("B.post2")

            projection("C.u", split="C.in", norm="C.in")
            projection("C.qk")
            rope_projection("C.v", [[0], [1]], after=turn_values("C.v"))
            rope_projection("C.gate", [[2, 3], [4, 5], [6, 7], []])
            layer_c_mixer()
            projection("C.out", split="C.mix", halfway=head_factors)
            for r in range(4):
                memory_rows(U0["C.mem"] + 2 * r, MH2, ML2, "mem2" if r == 0 else None)
                if r == 0:
                    sum_tokens("mem2", MB)
                memory_rows(U0["C.mem"] + 2 * r + 1, MH2, ML2)
                if r in (1, 2):
                    pr = r - 1
                    pe.wait_ge(sems["emptied_act"], emptied("act", U0["C.mem"] + 2 * pr + 1, 1))
                    if pr:
                        pe.wait_ge(sems["kv_t"], 4)
                    for f in range(4):
                        for t in range(MB):
                            last = pe.transpose(PS[:, 5 + f // 2, (f % 2) * MEM + t * P:(f % 2) * MEM + (t + 1) * P],
                                                Y[:, 2 * pr + t, f * P:(f + 1) * P], I_)
                        if f % 2:
                            last.then_inc(sems["kv_tr"], 1)
            projection("C.cq", split="C.cross", norm="C.cross")
            pe.wait_ge(sems["kv_t"], 6)
            pe.wait_ge(sems["emptied_dve"], emptied("dve", U0["C.cq"] + 3, 1))
            memory_attention(2, lambda h, c: CQ[:, 2 * h + c, :], lambda h, c: CK[:, 2 * h + c, :],
                             lambda h, c, m: CV[:, m, h * 256 + c * P:h * 256 + (c + 1) * P], 2, 256)
            projection("C.co", split="C.att")
            mlp(2)
            finish_post("final")

        @block.scalar
        def _(act):
            def A(o, i, f, **kw):
                return act.activation(o, i, f, **kw)

            def split_hi(u, i=None, step=0):
                s = u % 2
                act.wait_ge(sems[f"load{s}"], lin(16 * (u // 2 + 1), 8 * step, i))
                if u >= 2:
                    act.wait_ge(sems["tile"], lin(2 * u - 2, 2 * step, i))
                A(WH[s][:, :, :], STG[s][:, :, :], ACT.Copy).then_inc(sems["hi"], 1)

            def square(name, k, src, n=S):
                m = SQ_BASE[name] + k
                if m >= 4:
                    act.wait_ge(sems["sqa"], added(m - 4))
                A(SQ[:, m % 4, 0:n], src, ACT.Square).then_inc(sems["sq"], 1)

            def operand(q, sums, src, gain, ready, used=None, hh=HH, n=S):
                if used is not None:
                    act.wait_ge(sems["tile"], 2 * used)
                for k in range(KD):
                    ready(k)
                    A(hh[:, k, 0:n], src[:, k, 0:n], ACT.Copy, scale=par(gain, k)).then_inc(sems["hh"], 1)
                    square(sums, k, src[:, k, 0:n], n)

            def root(name, nt=NB):
                act.wait_ge(sems["ss"], sums_done(name))
                A(RT[:, 0:nt], PS[:, 4, 0:nt], ACT.Sqrt, scale=1.0 / D, bias=EPST[:, 0:1]).then_inc(sems["sqrt"], 1)

            def factor(name):
                act.wait_ge(sems["bc"], bcast_done(name))
                A(RS[:, :], PS[:, 4, :], ACT.Copy).then_inc(sems["rs"], 1)

            def units(name, norm=None, evac=None, behind=None):
                def fn(u, i, step):
                    first = u == U0[name] and i is None
                    if norm and first:
                        root(norm)
                        if u + 2 < UNITS:
                            split_hi(u + 2)
                        factor(norm)
                    if evac:
                        for j in range(2):
                            evac(u, i, step, j)
                    if not (norm and first) and u + 2 < UNITS:
                        split_hi(u + 2, i, step)
                    if behind:
                        behind(u - U0[name])
                run_phase(act, name, fn)

            def memory_unit(u, dst, norm=None):
                if norm:
                    root(norm, MB)
                    split_hi(u + 2)
                    act.wait_ge(sems["rsc"], sums_done(norm))
                for t in range(MB):
                    act.wait_ge(sems["tile"], 2 * u + t + 1)
                    A(dst(t), PS[:, 2 * (u % 2) + t, 0:UC], ACT.Copy, scale=RSC[:, t:t + 1]).then_inc(sems["emptied_act"], 1)
                if not norm:
                    split_hi(u + 2)

            def mlp(L):
                name = "ABC"[L] + ".mlp"
                sums = ("A.post2", "B.post2", "final")[L]
                ub = U0[name]

                def up(u, i, step, t, j, q):
                    act.wait_ge(sems["emptied_dve"], emptied("dve", u, j, i, step))
                    A(UPH[:, t, :], RR[:, t % 2, :], ACT.Square).then_inc(sems["uh"], 1)

                for r in range(4):
                    if r == 0:
                        root(name)
                        split_hi(ub + 2)
                        factor(name)
                    for j in range(2):
                        up(ub + r, None, 0, 2 * r + j, j, 0)
                    if r:
                        split_hi(ub + r + 2)
                with act.Fori(0, QUARTERS - 1) as q:
                    for r in range(4):
                        split_hi(ub + 4 + r + 2, q, 8)
                    for r in range(4):
                        for j in range(2):
                            up(ub + 8 + r, q, 8, 2 * r + j, j, q)
                        split_hi(ub + 8 + r + 2, q, 8)
                for r in range(4):
                    if ub + 28 + r + 2 < UNITS:
                        split_hi(ub + 28 + r + 2)
                    for k in (2 * r, 2 * r + 1):
                        act.wait_ge(sems["emptied_dve"], emptied("dve", ub + 28 + r, k % 2))
                        square(sums, k, (XT if L == 2 else Y)[:, k, :])

            def post_factor(name):
                root(name)
                factor(name)

            def out_tile(name, sums):
                def evac(u, i, step, j):
                    k = 2 * (u - U0[name]) + j
                    act.wait_ge(sems["tile"], 2 * u + j + 1)
                    bank = PS[:, 2 * (u % 2) + j, :]
                    square(sums, k, bank)
                    A(Y[:, k, :], bank, ACT.Copy).then_inc(sems["emptied_act"], 1)
                return evac

            def x_new(name, k):
                act.wait_ge(sems["x_new"], 8 * POSTS.index(name) + k + 1)

            def memory_attention(a, dh, dst, scale):
                def soft(h):
                    e = h % 2
                    act.wait_ge(sems["ma_nm"], 4 * a + h + 1)
                    if h >= 2:
                        act.wait_ge(sems["ma_tr"], 4 * a + h - 1)
                    for b in range(NB):
                        A(PROB[e][:, b * MEM:(b + 1) * MEM], PSF[:, 2048 * e + b * MEM:2048 * e + (b + 1) * MEM], ACT.Exp,
                          scale=scale, bias=MST[:, e, 1, b:b + 1], accum_out=MST[:, e, 2, b:b + 1]).then_inc(sems["ma_exp"], 1)

                def turned(h):
                    e = h % 2
                    act.wait_ge(sems["ma_tr"], 4 * a + h + 1)
                    if h >= 2:
                        act.wait_ge(sems["ma_o"], 4 * a + h - 1)
                    A(PROBT[e], PSF[:, 2048 * e + 1024:2048 * e + 2048], ACT.Copy).then_inc(sems["ma_pt"], 1)

                def result(h):
                    e = h % 2
                    act.wait_ge(sems["ma_o"], 4 * a + h + 1)
                    if dh == 64:
                        last = A(dst(h, 0), PS[64 * e:64 * e + 64, 4 * e + 2, :], ACT.Copy)
                    else:
                        for c in range(2):
                            last = A(dst(h, c), PS[:, 4 * e + 2 + c, :], ACT.Copy)
                    last.then_inc(sems["ma_out"], 1)

                soft(0)
                soft(1)
                for h in range(4):
                    turned(h)
                    if h:
                        result(h - 1)
                    if h + 2 < 4:
                        soft(h + 2)
                result(3)

            def mix_hi(q, k, src):
                A(HH[:, k, :], src, ACT.Copy).then_inc(sems["hh"], 1)

            def delta_net():
                def per(n, k, e, g):
                    return lin(2 * (k - 1) + e + 1, 2 * n, g)
                with act.Fori(0, H_LIN // 2) as g:
                    for e in range(2):
                        vt = QKV[:, bass.ds(g * 2 + 12 + e, 1), :].rearrange("p a n -> p (a n)")
                        A(VS[e], vt, ACT.Copy).then_inc(sems["v_copy"], 1)
                    for e in range(2):
                        act.wait_ge(sems["bcast_mm"], per(1, 1, e, g))
                        A(EG[e], PS[:, 4 * e, :], ACT.Exp).then_inc(sems["eg_exp"], 1)
                    for e in range(2):
                        act.wait_ge(sems["dt_pre"], per(1, 1, e, g))
                        A(DT[e], DT[e], ACT.Exp).then_inc(sems["dt_exp"], 1)
                    for lv in range(1, 7):
                        for e in range(2):
                            act.wait_ge(sems["lv_y"], per(7, lv + 1, e, g))
                            if lv == 1:
                                act.wait_ge(sems["at"], per(1, 1, e, g))
                            A(YT[e], PS[:, 4 * e + 1, :], ACT.Copy).then_inc(sems["lv_yc"], 1)
                    for e in range(2):
                        act.wait_ge(sems["sc_o"], per(4, 4, e, g))
                        A(YT[e], PS[:, 4 * e + 3, :], ACT.Square).then_inc(sems["osq"], 1)
                    for e in range(2):
                        act.wait_ge(sems["ow"], per(1, 1, e, g))
                        A(ORT[e][:, 0, :], ORT[e][:, 0, :], ACT.Sqrt, scale=1.0 / P)\
                            .then_inc(sems["ort"], 1)
                    for e in range(2):
                        act.wait_ge(sems["obc"], per(1, 1, e, g))
                        A(BT[e], PS[:, 4 * e, :], ACT.Copy).then_inc(sems["obs"], 1)
                    for e in range(2):
                        act.wait_ge(sems["o_done"], per(1, 1, e, g))

            def stick_breaking():
                def logs(n):
                    e = n % 2
                    act.wait_ge(sems["sb_z"], n + 1)
                    if n >= 2:
                        act.wait_ge(sems["sb_rc"], n - 1)
                    A(SP[e], PSF[:, 1536 * e:1536 * e + SB_ALL], ACT.Abs).then_inc(sems["sb_az"], 1)
                    act.wait_ge(sems["sb_az"], n + 1)
                    A(SP[e], SP[e], ACT.Exp, scale=-1.0).then_inc(sems["sb_e"], 1)
                    act.wait_ge(sems["sb_e"], n + 1)
                    A(SP[e], SP[e], ACT.Ln, bias=ONE1[:, 0:1]).then_inc(sems["sb_l"], 1)

                logs(0)
                logs(1)
                for n in range(12):
                    e = n % 2
                    act.wait_ge(sems["sb_rc"], n + 1)
                    if n >= 2:
                        act.wait_ge(sems["sb_o"], n - 1)
                    A(AW[e], PSF[:, 1536 * e:1536 * e + SB_ALL], ACT.Exp).then_inc(sems["sb_a"], 1)
                    if n % 2 == 1 and n >= 3:
                        pair_out(n // 2 - 1)
                    if n + 2 < 12:
                        logs(n + 2)
                pair_out(NT - 1)

            def pair_out(g):
                act.wait_ge(sems["sb_o"], 2 * g + 2)
                A(HH[:, g, :], PS[:, 6 + g % 2, :], ACT.Copy).then_inc(sems["hh"], 1)

            def values(name, dst):
                def fn(r):
                    for j in range(2):
                        t = 2 * r + j
                        act.wait_ge(sems["vtr"], VIDX[name] + t + 1)
                        A(dst[:, t, :, :].rearrange("p b n -> p (b n)"), PS[:, 5 + t % 2, :], ACT.Copy).then_inc(sems["vrow"], 1)
                return fn

            def value_units(name, dst):
                turned = values(name, dst)
                for r in range(NU[name]):
                    if r:
                        turned(r - 1)
                    split_hi(U0[name] + r + 2)
                turned(NU[name] - 1)

            act.dma_start(PAR[:, :], par_in).then_inc(sems["par_in"], 16)
            for k in range(0, KD, 4):
                act.dma_start(MX[:, k:k + 4, :], memt_in[:, k:k + 4, :]).then_inc(sems[f"mem_in{k // 4}"], 16)
            act.dma_start(CON[:, :], con_in).then_inc(sems["const_in"], 16)
            act.dma_start(XT[:, :, :], xt_in).then_inc(sems["x_in"], 16)

            act.wait_ge(sems["par_in"], 16)
            act.wait_ge(sems["eps"], 2)
            split_hi(0)
            operand("mem", "mem", MX, "mem_norm", lambda k: act.wait_ge(sems[f"mem_in{k // 4}"], 16), hh=MH, n=MEM)
            split_hi(1)
            for L in range(2):
                if L:
                    act.wait_ge(sems["kv_tr"], 1)
                memory_unit(U0["AB"[L] + ".mem"], lambda t: KR[:, t, :], norm="mem" if L == 0 else None)
                memory_unit(U0["AB"[L] + ".mem"] + 1, lambda t: V_MEM[L][:, t, :])
                if L == 0:
                    act.wait_ge(sems["x_in"], 16)
                    operand("A.in", "A.in", XT, "pre_mix0", lambda k: None)
                act.wait_ge(sems["kv_tr"], L + 1)
                A(KT_MEM[L][:, :, :].rearrange("p f n -> p (f n)"), PS[:, 5, :], ACT.Copy).then_inc(sems["kv_t"], 1)

            def conv_tile(u, i, step, j):
                t = 2 * (u - U0["A.qkv"]) + j
                act.wait_ge(sems["emptied_dve"], emptied("dve", u, j, i, step))
                w = par("conv", 4 * t) if i is None else PAR[:, bass.ds(i * (8 * step) + (PCOL["conv"] + 4 * t), 1)]
                if u > U0["A.qkv"]:
                    act.wait_ge(sems["silu"], lin(t - 1, 2 * step, i))
                A(CONV_ACC[j], CONV_IN[j][:, 0:S], ACT.Copy, scale=w).then_inc(sems["conv0"], 1)
                if j:
                    for jj in range(2):
                        tt = 2 * (u - U0["A.qkv"]) + jj
                        act.wait_ge(sems["conv"], lin(3 * (tt - jj) + 5 + jj, 6 * step, i))
                        A(tile(QKV, tt if i is None else i * (2 * step) + tt), CONV_ACC[jj], ACT.Silu).then_inc(sems["silu"], 1)

            units("A.qkv", norm="A.in", evac=conv_tile)
            units("A.memq")
            units("A.bg")
            sm = [SMALL[:, r, :] for r in range(8)]

            def square_qk(t):
                if t >= 4:
                    act.wait_ge(sems["l2ss"], t - 3)
                elif t == 0:
                    act.wait_ge(sems["sqa"], 14)
                act.wait_ge(sems["silu"], t + 1)
                A(SQ[:, t % 4, :], QKV[:, t, :], ACT.Square).then_inc(sems["l2sq"], 1)

            def decays_1():
                act.wait_ge(sems["bg"], 1)
                A(sm[1], par("a_log", 0, 24), ACT.Exp).then_inc(sems["sc_act"], 1)
                A(sm[5], BG[:, 0:6, :].rearrange("p h b -> p (h b)"), ACT.Exp, scale=-1.0).then_inc(sems["sc_act"], 1)
                act.wait_ge(sems["sc_dve"], 2)
                A(sm[2], sm[2], ACT.Exp, scale=-1.0).then_inc(sems["sc_act"], 1)
                act.wait_ge(sems["sc_act"], 3)
                A(sm[2], sm[2], ACT.Ln, bias=ONE1[:, 0:1]).then_inc(sems["sc_act"], 1)

            def decays_2():
                act.wait_ge(sems["gc_mm"], 1)
                gc = PS[:, 5, 64:88].rearrange("p (h b) -> p h b", b=NB)
                gl = PS[:, 5, 96:120].rearrange("p (h b) -> p h b", b=NB)
                A(SC[:, :, 4, :], gc, ACT.Copy).then_inc(sems["sc_act"], 1)
                A(sm[7], PS[:, 5, 64:88], ACT.Exp).then_inc(sems["sc_act"], 1)
                A(SC[:, :, 7, :], gl, ACT.Exp).then_inc(sems["sc_act"], 1)
                act.wait_ge(sems["sc_dve"], 7)
                A(SC[:, :, 6, :], SMALL[:, 0, :].rearrange("p (h b) -> p h b", b=NB), ACT.Exp).then_inc(sems["sc_act"], 1)

            def behind_gate(r):
                if r == 0:
                    decays_1()
                if r < 2:
                    for t in range(4 * r + 4, 4 * r + 8):
                        square_qk(t)
                else:
                    decays_2()
                    act.wait_ge(sems["l2ss"], 2 * NT)
                    A(RQK[:, :, :].rearrange("p t b -> p (t b)"), PS[:, 6, 0:48], ACT.Sqrt, bias=EPST[:, 0:1])\
                        .then_inc(sems["l2rt"], 1)

            for t in range(4):
                square_qk(t)
            units("A.gate", behind=behind_gate)
            act.wait_ge(sems["tile"], 2 * U0["A.out"])
            for t in range(NT):
                act.wait_ge(sems["emptied_dve"], emptied("dve", U0["A.gate"] + t // 2, t % 2))
                A(GATES[:, t, :], TMP[t // 3][t % 3][:, :], ACT.Silu).then_inc(sems["gate_silu"], 1)
            act.wait_ge(sems["gate_silu"], NT)
            delta_net()

            memory_attention(0, 64, lambda h, c: CX[(h % 2) * 64:(h % 2) * 64 + 64, h // 2, :], 64 ** -0.5)
            for k in range(KD):
                if k < NT:
                    act.wait_ge(sems["gated"], k + 1)
                elif k == NT:
                    act.wait_ge(sems["ma_out"], 4)
                mix_hi("A.mix", k, QKV[:, k, :] if k < NT else CX[:, k - NT, :])
            units("A.out", evac=out_tile("A.out", "A.post"))
            post_factor("A.post")
            operand("A.mlp", "A.mlp", XT, "pre_mlp0", lambda k: x_new("A.post", k), used=U0["A.mlp"])
            mlp(0)
            post_factor("A.post2")

            operand("B.in", "B.in", XT, "pre_mix1", lambda k: x_new("A.post2", k), used=U0["B.qk"])
            units("B.qk", norm="B.in")
            value_units("B.v", VB)
            units("B.memq")
            act.wait_ge(sems["emptied_dve"], emptied("dve", U0["B.memq"], 1))
            act.wait_ge(sems["tile"], 2 * U0["B.out"])
            stick_breaking()
            memory_attention(1, 64, lambda h, c: MO[(h % 2) * 64:(h % 2) * 64 + 64, h // 2, :], 64 ** -0.5)
            act.wait_ge(sems["ma_out"], 8)
            for k in (6, 7):
                mix_hi("B.mix", k, MO[:, k - NT, :])
            units("B.out", evac=out_tile("B.out", "B.post"))
            post_factor("B.post")
            operand("B.mlp", "B.mlp", XT, "pre_mlp1", lambda k: x_new("B.post", k), used=U0["B.mlp"])
            mlp(1)
            post_factor("B.post2")

            operand("C.in", "C.in", XT, "g_mix", lambda k: x_new("B.post2", k), used=U0["C.u"])
            units("C.u", norm="C.in")
            units("C.qk")
            value_units("C.v", VC)

            def gate_sig(u, i, step, j):
                k = 2 * (u - U0["C.gate"]) + j
                act.wait_ge(sems["emptied_dve"], emptied("dve", u, j))
                A(GC_[:, k, :], GC_[:, k, :], ACT.Sigmoid).then_inc(sems["sig"], 1)

            units("C.gate", evac=gate_sig)
            act.wait_ge(sems["lam"], 2)
            A(LAM[:, 2:4], LAM[:, 0:2], ACT.Exp).then_inc(sems["lam_act"], 1)
            act.wait_ge(sems["tile"], 2 * U0["C.out"])
            def exponentials(h, c):
                act.wait_ge(sems["df_nm"], 2 * h + c + 1)
                if c:
                    if h:
                        act.wait_ge(sems["df_a"], 4 * h)
                elif h >= 2:
                    act.wait_ge(sems["df_tr"], 3 * h - 3)
                for b in range(NB):
                    o, n = DF_OFF[b], DF_WID[b]
                    A((DP1 if c else DP0[h % 2])[:, o:o + n], PSF[:, 1536 * c + o:1536 * c + o + n], ACT.Exp, scale=64 ** -0.5,
                      bias=DMX[:, c, 1, b:b + 1], accum_out=DST[:, c, NB * h + b:NB * h + b + 1]).then_inc(sems["df_exp"], 1)

            exponentials(0, 0)
            exponentials(0, 1)
            for g in range(4):
                act.wait_ge(sems["mixed"], g + 1)
                mix_hi("C.mix", g, GC_[:, g, :])
            for h in range(4):
                for r in range(3):
                    act.wait_ge(sems["df_tr"], 3 * h + r + 1)
                    if h and r == 0:
                        act.wait_ge(sems["df_o"], h)
                    n = SB_ALL - 1024 if r == 2 else 512
                    A(DAT[:, 512 * r:512 * r + n], PS[:, 7, 0:n], ACT.Copy).then_inc(sems["df_at"], 1)
                if h < 3:
                    exponentials(h + 1, 0)
                    exponentials(h + 1, 1)
                act.wait_ge(sems["df_o"], h + 1)
                A(QC[:, h, :], PS[:, 6, :], ACT.Copy)
                A(SQ[:, h, :], PS[:, 6, :], ACT.Square).then_inc(sems["df_sq"], 1)
            act.wait_ge(sems["df_w"], 2)
            A(RMSD, RMSD, ACT.Sqrt, scale=1.0 / P, bias=EPST[:, 0:1]).then_inc(sems["df_rt"], 1)
            for h in range(4):
                act.wait_ge(sems["df_g"], 2 * h + 2)
                mix_hi("C.mix", 4 + h, GC_[:, 4 + h, :])

            units("C.out")
            act.wait_ge(sems["mem2_in"], 16)
            operand("mem2", "mem2", MX2, "g_mem", lambda k: None, hh=MH2, n=MEM)
            for r in range(4):
                for c in range(2):
                    memory_unit(U0["C.mem"] + 2 * r + c,
                                (lambda t: Y[:, 2 * r + t, c * UC:(c + 1) * UC]) if r < 2 else
                                (lambda t: CV[:, t, 512 * (r - 2) + c * UC:512 * (r - 2) + (c + 1) * UC]),
                                norm="mem2" if r == c == 0 else None)
                if r in (1, 2):
                    for f in range(2):
                        act.wait_ge(sems["kv_tr"], 2 + 2 * (r - 1) + f + 1)
                        A(CK[:, 4 * (r - 1) + 2 * f:4 * (r - 1) + 2 * f + 2, :].rearrange("p f n -> p (f n)"),
                          PS[:, 5 + f, :], ACT.Copy).then_inc(sems["kv_t"], 1)
            operand("C.cross", "C.cross", XT, "g_cross",
                    lambda k: act.wait_ge(sems["emptied_dve"], emptied("dve", U0["C.out"] + k // 2, k % 2)), used=U0["C.mem"])
            units("C.cq", norm="C.cross")
            memory_attention(2, 256, lambda h, c: CQ[:, 2 * h + c, :], 256 ** -0.5)
            act.wait_ge(sems["tile"], 2 * U0["C.co"])
            act.wait_ge(sems["ma_out"], 12)
            for k in range(KD):
                mix_hi("C.att", k, CQ[:, k, :])
            units("C.co")
            operand("C.mlp", "C.mlp", XT, "g_mlp",
                    lambda k: act.wait_ge(sems["emptied_dve"], emptied("dve", U0["C.co"] + k // 2, k % 2)), used=U0["C.mlp"])
            mlp(2)
            post_factor("final")

        @block.vector
        def _(dve):
            def stt(o, a, s_, b, op0, op1):
                return dve.scalar_tensor_tensor(out=o, in0=a, scalar=s_, in1=b, op0=op0, op1=op1)

            def tt(o, a, b, op):
                return dve.tensor_tensor(o, a, b, op)

            def split_lo(u, i=None, step=0):
                s = u % 2
                dve.wait_ge(sems["hi"], lin(u + 1, step, i))
                tt(WL[s][:, :, :], STG[s][:, :, :], WH[s][:, :, :].bitcast(F32), ALU.subtract).then_inc(sems["lo"], 1)

            def operand_lo(q, src, gain, hh=HH, hl=HL, n=S, k0=0, k1=KD):
                for k in range(k0, k1):
                    dve.wait_ge(sems["hh"], split_done(q, k))
                    stt(hl[:, k, 0:n], src[:, k, 0:n], par(gain, k), hh[:, k, 0:n].bitcast(F32), ALU.mult, ALU.subtract)\
                        .then_inc(sems["hl"], 1)

            def invert(name, nt=NB):
                dve.wait_ge(sems["sqrt"], sums_done(name))
                dve.reciprocal(RSC[:, 0:nt], RT[:, 0:nt]).then_inc(sems["rsc"], 1)

            def units(name, norm=None, evac=None, behind=None):
                def fn(u, i, step):
                    first = u == U0[name] and i is None
                    if norm and first:
                        invert(norm)
                        split_lo(u + 2)
                        dve.wait_ge(sems["rs"], bcast_done(norm))
                    if evac:
                        for j in range(2):
                            dve.wait_ge(sems["tile"], lin(2 * u + j + 1, 2 * step, i))
                            evac(u, i, step, j)
                    if not (norm and first) and u + 2 < UNITS:
                        split_lo(u + 2, i, step)
                    if behind:
                        behind(u - U0[name])
                run_phase(dve, name, fn)

            def scaled_to(dst, name):
                def evac(u, i, step, j):
                    t = 2 * (u - U0[name]) + j
                    o = dst(t) if i is None else dst(i * (2 * step) + t)
                    tt(o, PS[:, 2 * (u % 2) + j, :], RS[:, :], ALU.mult).then_inc(sems["emptied_dve"], 1)
                return evac

            def add_to(dst, name):
                def evac(u, i, step, j):
                    k = 2 * (u - U0[name]) + j
                    tt(dst[:, k, :], dst[:, k, :], PS[:, 2 * (u % 2) + j, :], ALU.add).then_inc(sems["emptied_dve"], 1)
                return evac

            def mlp(L):
                name = "ABC"[L] + ".mlp"
                ub = U0[name]
                dst = XT if L == 2 else Y

                def up(u, i, step, t, j):
                    m = lin(32 * L + 8 * ((u - ub) // 8) + t, step, i)
                    bank = PS[:, 2 * (u % 2) + j, :]
                    dve.wait_ge(sems["tile"], lin(2 * u + j + 1, 2 * step, i))
                    stt(RR[:, t % 2, :], bank, 0.0, RS[:, :], ALU.max, ALU.mult).then_inc(sems["emptied_dve"], 1)
                    dve.wait_ge(sems["emptied_dve"], emptied("dve", u, j, i, step))
                    tt(RQ[:, t % 2, :], RR[:, t % 2, :], RR[:, t % 2, :], ALU.mult).then_inc(sems["rq"], 1)
                    dve.wait_ge(sems["rq"], m + 1)
                    dve.wait_ge(sems["uh"], m + 1)
                    tt(UPL[:, t, :], RQ[:, t % 2, :], UPH[:, t, :].bitcast(F32), ALU.subtract).then_inc(sems["ul"], 1)

                def down(u, i, step, t, j):
                    dve.wait_ge(sems["tile"], lin(2 * u + j + 1, 2 * step, i))
                    tt(dst[:, t, :], dst[:, t, :], PS[:, 2 * (u % 2) + j, :], ALU.add).then_inc(sems["emptied_dve"], 1)

                for r in range(4):
                    if r == 0:
                        invert(name)
                        split_lo(ub + 2)
                        dve.wait_ge(sems["rs"], bcast_done(name))
                    for j in range(2):
                        up(ub + r, None, 0, 2 * r + j, j)
                    if r:
                        split_lo(ub + r + 2)
                if L < 2:
                    dve.wait_ge(sems["y_zero"], L + 1)
                with dve.Fori(0, QUARTERS - 1) as q:
                    for r in range(4):
                        for j in range(2):
                            down(ub + 4 + r, q, 8, 2 * r + j, j)
                        split_lo(ub + 4 + r + 2, q, 8)
                    for r in range(4):
                        for j in range(2):
                            up(ub + 8 + r, q, 8, 2 * r + j, j)
                        split_lo(ub + 8 + r + 2, q, 8)
                for r in range(4):
                    for j in range(2):
                        down(ub + 28 + r, None, 0, 2 * r + j, j)
                    if ub + 28 + r + 2 < UNITS:
                        split_lo(ub + 28 + r + 2)

            def post_and_operand(post, gain, q, gain_in):
                invert(post)
                dve.wait_ge(sems["rs"], bcast_done(post))
                if post in ("A.post", "B.post"):
                    dve.wait_ge(sems["emptied_act"], emptied("act", U0[post[0] + ".out"] + 3, 1))
                for k in range(KD + 3):
                    if k < KD:
                        stt(Y[:, k, :], Y[:, k, :], par(gain, k), RS[:, :], ALU.mult, ALU.mult).then_inc(sems["y_scaled"], 1)
                    if k >= 3:
                        operand_lo(q, XT, gain_in, k0=k - 3, k1=k - 2)

            def memory_attention(a, scale, beside=None):
                def top(h):
                    e = h % 2
                    n = 4 * a + h
                    dve.wait_ge(sems["ma_s"], n + 1)
                    dve.tensor_reduce(MST[:, e, 0, :], PSF[:, 2048 * e:2048 * e + 1024].rearrange("p (b m) -> p b m", b=NB),
                                      AX.X, ALU.max).then_inc(sems["ma_max"], 1)
                    dve.wait_ge(sems["ma_max"], n + 1)
                    dve.tensor_scalar(MST[:, e, 1, :], MST[:, e, 0, :], -scale, None, ALU.mult).then_inc(sems["ma_nm"], 1)

                def normalise(h):
                    e = h % 2
                    n = 4 * a + h
                    dve.wait_ge(sems["ma_exp"], 4 * n + 4)
                    dve.reciprocal(MST[:, e, 3, :], MST[:, e, 2, :]).then_inc(sems["ma_ri"], 1)
                    dve.wait_ge(sems["ma_ri"], n + 1)
                    p = PROB[e].rearrange("p (b m) -> p b m", b=NB)
                    tt(p, p, MST[:, e, 3, :].unsqueeze(2).to_broadcast([P, NB, MEM]), ALU.mult).then_inc(sems["ma_p"], 1)

                top(0)
                top(1)
                for h in range(4):
                    normalise(h)
                    if h + 2 < 4:
                        top(h + 2)
                    if beside and h == 1:
                        beside()

            def mix_lo(q, k, src):
                dve.wait_ge(sems["hh"], split_done(q, k))
                tt(HL[:, k, :], src, HH[:, k, :].bitcast(F32), ALU.subtract).then_inc(sems["hl"], 1)

            def delta_net():
                def per(n, k, e, g):
                    return lin(2 * (k - 1) + e + 1, 2 * n, g)

                def row(base, e, g):
                    return QKV[:, bass.ds(g * 2 + base + e, 1), :].rearrange("p a n -> p (a n)")

                with dve.Fori(0, H_LIN // 2) as g:
                    for e in range(2):
                        src = SC[:, bass.ds(g * 2 + e, 1), :, :].rearrange("p a c b -> p (a c b)")
                        dve.tensor_copy(HS[e][:, :, :].rearrange("p c b -> p (c b)"), src).then_inc(sems["head_sc"], 1)
                    for e in range(2):
                        dve.wait_ge(sems["bcast_mm"], per(1, 1, e, g))
                        dve.wait_ge(sems["head_sc"], per(1, 1, e, g))
                        bank = lambda o: PS[:, 4 * e + o, :]
                        tt(KNS[e], row(6, e, g), bank(2), ALU.mult).then_inc(sems["kn"], 1)
                        dve.wait_ge(sems["eg_exp"], per(1, 1, e, g))
                        for b in range(NB):
                            last = dve.tensor_scalar(blk(DT[e], b), blk(bank(0), b), HS[e][:, 4, b:b + 1], 0.0,
                                                     ALU.subtract, ALU.min)
                        last.then_inc(sems["dt_pre"], 1)
                        dve.wait_ge(sems["kn"], per(1, 1, e, g))
                        tt(KBT[e], KNS[e], bank(1), ALU.mult).then_inc(sems["kbt"], 1)
                    for e in range(2):
                        bank = lambda o: PS[:, 4 * e + o, :]
                        dve.wait_ge(sems["dt_exp"], per(1, 1, e, g))
                        dve.wait_ge(sems["lt_mm"], per(1, 1, e, g))
                        tt(LT[e], bank(1), DT[e], ALU.mult).then_inc(sems["lt"], 1)
                        dve.wait_ge(sems["lt"], per(1, 1, e, g))
                        tt(blocks(DT[e]), blocks(DT[e]), bc_blocks(con("tri_le")), ALU.mult).then_inc(sems["dtm"], 1)
                        dve.wait_ge(sems["rows"], per(1, 1, e, g))
                        dve.wait_ge(sems["dtm"], per(1, 1, e, g))
                        tt(AT[e], bank(2), DT[e], ALU.mult).then_inc(sems["at"], 1)
                        dve.wait_ge(sems["eg_exp"], per(1, 1, e, g))
                        tt(row(0, e, g), row(0, e, g), EG[e], ALU.mult).then_inc(sems["qd"], 1)
                        dve.wait_ge(sems["qd"], per(1, 1, e, g))
                        dve.wait_ge(sems["gate_silu"], NT)
                        tt(blocks(RK[e]), blocks(bank(3)), per_block(HS[e][:, 5, :]), ALU.mult)
                        tt(blocks(KDC[e]), blocks(bank(3)), per_block(HS[e][:, 6, :]), ALU.mult).then_inc(sems["rk"], 1)
                        tt(blocks(row(12, e, g)), blocks(bank(0)), per_block(HS[e][:, 1, :]), ALU.mult).then_inc(sems["rv"], 1)
                    for e in range(2):
                        dve.wait_ge(sems["lv_y"], per(7, 1, e, g))
                        tt(blocks(XX[e]), bc_blocks(con("ident")), blocks(PS[:, 4 * e + 1, :]), ALU.subtract)
                        tt(blocks(XTr[e]), bc_blocks(con("ident")), blocks(BT[e]), ALU.subtract).then_inc(sems["lv_x"], 1)
                    for lv in range(1, 7):
                        for e in range(2):
                            dve.wait_ge(sems["lv_p"], per(6, lv, e, g))
                            dve.wait_ge(sems["lv_x"], per(7, lv, e, g))
                            if lv < 6:
                                tt(XX[e], XX[e], PS[:, 4 * e + 2, :], ALU.subtract)
                            tt(XTr[e], XTr[e], PS[:, 4 * e + 3, :], ALU.subtract).then_inc(sems["lv_x"], 1)
                    for e in range(2):
                        dve.wait_ge(sems["u_mm"], per(1, 1, e, g))
                        dve.tensor_scalar(row(12, e, g), PS[:, 4 * e, :], 1.0, None, ALU.mult).then_inc(sems["u_sb"], 1)
                        dve.tensor_copy(WT[e], PS[:, 4 * e + 1, :]).then_inc(sems["w_sb"], 1)
                    for b in range(NB):
                        for e in range(2):
                            ub = blk(row(12, e, g), b)
                            if b == 0:
                                dve.wait_ge(sems["u_sb"], per(1, 1, e, g))
                                dve.tensor_scalar(VN[e][:, :], ub, 1.0, None, ALU.mult).then_inc(sems["vn"], 1)
                            else:
                                dve.wait_ge(sems["sc_ws"], per(3, b, e, g))
                                tt(VN[e][:, :], ub, PS[:, 4 * e + 2, 0:P], ALU.subtract).then_inc(sems["vn"], 1)
                        for e in range(2):
                            if b == NB - 1:
                                continue
                            dve.wait_ge(sems["sc_o"], per(4, b + 1, e, g))
                            if b == 0:
                                dve.tensor_copy(ST8[e][:, :], PS[:, 4 * e + 2, P:2 * P]).then_inc(sems["st"], 1)
                            else:
                                dve.wait_ge(sems["st"], per(3, b, e, g))
                                stt(ST8[e][:, :], ST8[e][:, :], HS[e][:, 7, b:b + 1], PS[:, 4 * e + 2, P:2 * P],
                                    ALU.mult, ALU.add).then_inc(sems["st"], 1)
                    for e in range(2):
                        dve.wait_ge(sems["oss"], per(1, 1, e, g))
                        tt(ORT[e][:, 0, :], PS[:, 4 * e + 1, 0:NB], HS[e][:, 3, :], ALU.add).then_inc(sems["ow"], 1)
                    for e in range(2):
                        dve.wait_ge(sems["ort"], per(1, 1, e, g))
                        dve.reciprocal(ORT[e][:, 1, :], ORT[e][:, 0, :]).then_inc(sems["ors"], 1)
                    for e in range(2):
                        dve.wait_ge(sems["obs"], per(1, 1, e, g))
                        stt(row(0, e, g), PS[:, 4 * e + 3, :], par("onorm"), BT[e], ALU.mult, ALU.mult).then_inc(sems["o_done"], 1)
                    for e in range(2):
                        dve.wait_ge(sems["o_done"], per(1, 1, e, g))

            def diagonals(ap):
                v = ap[:, 0:1152].rearrange("p (a n) -> p a n", n=P)
                return v[:, 0:9:4, :], ap[:, SB_OFF[3]:SB_OFF[3] + P]

            def stick_breaking():
                def softplus(n):
                    e = n % 2
                    dve.wait_ge(sems["sb_l"], n + 1)
                    stt(SP[e], PSF[:, 1536 * e:1536 * e + SB_ALL], 0.0, SP[e], ALU.max, ALU.add).then_inc(sems["sb_sp"], 1)
                    dve.wait_ge(sems["sb_sp"], n + 1)
                    three, one = diagonals(SP[e])
                    tt(three, three, con("strict").unsqueeze(1).to_broadcast([P, 3, P]), ALU.mult)
                    tt(one, one, con("strict"), ALU.mult).then_inc(sems["sb_m"], 1)
                    dve.wait_ge(sems["sb_m"], n + 1)
                    two = TAIL[:, e, 0:256]
                    dve.tensor_copy(TAIL[:, e, 0:P], SP[e][:, SB_OFF[2]:SB_OFF[2] + P])
                    tt(TAIL[:, e, P:2 * P], SP[e][:, SB_OFF[2] + P:SB_OFF[2] + 2 * P], SP[e][:, SB_OFF[3]:SB_OFF[3] + P], ALU.add)\
                        .then_inc(sems["sb_t"], 1)
                    dve.wait_ge(sems["sb_t"], 2 * n + 1)
                    dve.tensor_copy(TAIL[:, e, 256:384], SP[e][:, SB_OFF[1]:SB_OFF[1] + P])
                    tt(TAIL[:, e, 384:640], SP[e][:, SB_OFF[1] + P:SB_OFF[1] + 3 * P], two, ALU.add).then_inc(sems["sb_t"], 1)

                softplus(0)
                softplus(1)
                for n in range(12):
                    e = n % 2
                    dve.wait_ge(sems["sb_a"], n + 1)
                    three, one = diagonals(AW[e])
                    tt(three, three, con("cap").unsqueeze(1).to_broadcast([P, 3, P]), ALU.min).then_inc(sems["sb_cap"], 1)
                    tt(one, one, con("cap"), ALU.min).then_inc(sems["sb_cap"], 1)
                    if n % 2 == 1 and n >= 3:
                        mix_lo("B.mix", n // 2 - 1, PS[:, 6 + (n // 2 - 1) % 2, :])
                    if n + 2 < 12:
                        softplus(n + 2)
                mix_lo("B.mix", NT - 1, PS[:, 6 + (NT - 1) % 2, :])

            def vstage(name):
                def evac(u, i, step, j):
                    t = 2 * (u - U0[name]) + j
                    if t >= 2:
                        dve.wait_ge(sems["vtr"], VIDX[name] + t - 1)
                    tt(Y[:, t % 2, :], PS[:, 2 * (u % 2) + j, :], RS[:, :], ALU.mult).then_inc(sems["emptied_dve"], 1)
                return evac

            dve.wait_ge(sems["par_in"], 16)
            split_lo(0)
            operand_lo("mem", MX, "mem_norm", MH, ML, MEM)
            split_lo(1)
            dve.wait_ge(sems["const_in"], 16)
            invert("mem", MB)
            split_lo(2)
            split_lo(3)
            operand_lo("A.in", XT, "pre_mix0")
            split_lo(4)
            split_lo(5)

            dve.wait_ge(sems["cb_zero"], 2)

            def conv_tile(u, i, step, j):
                r = u - U0["A.qkv"]
                if r:
                    dve.wait_ge(sems["conv"], lin(6 * r - 1 + j, 6 * step, i))
                tt(CONV_IN[j][:, 3:3 + S], PS[:, 2 * (u % 2) + j, :], RS[:, :], ALU.mult).then_inc(sems["emptied_dve"], 1)
                if j:
                    for tap in range(1, 4):
                        for jj in range(2):
                            tj = 2 * (u - U0["A.qkv"]) + jj
                            if tap == 1:
                                dve.wait_ge(sems["conv0"], lin(tj + 1, 2 * step, i))
                            else:
                                dve.wait_ge(sems["conv"], lin(6 * (tj // 2) + 2 * (tap - 2) + jj + 1, 6 * step, i))
                            c = PCOL["conv"] + 4 * tj + tap
                            w = PAR[:, c:c + 1] if i is None else PAR[:, bass.ds(i * (8 * step) + c, 1)]
                            stt(CONV_ACC[jj], CONV_IN[jj][:, tap:tap + S], w, CONV_ACC[jj], ALU.mult, ALU.add)\
                                .then_inc(sems["conv"], 1)

            units("A.qkv", norm="A.in", evac=conv_tile)
            units("A.memq", evac=scaled_to(lambda t: MQ[:, t, :], "A.memq"))

            def bg_tile(u, i, step, j):
                if j == 0:
                    tt(BGT[:, :], PS[0:12, 2 * (u % 2), :], RS[0:12, :], ALU.mult).then_inc(sems["emptied_dve"], 2)

            units("A.bg", evac=bg_tile)
            hb = lambda ap: ap.rearrange("p (h b) -> p h b", b=NB)
            sm = [SMALL[:, r, :] for r in range(8)]
            step_ = [0]

            def sc(ins):
                step_[0] += 1
                ins.then_inc(sems["sc_dve"], 1)
                dve.wait_ge(sems["sc_dve"], step_[0])

            def decays_1():
                dve.wait_ge(sems["bg_tr"], 1)
                dve.tensor_copy(BG[:, :, :], PS[:, 5, 0:48].rearrange("p (b h) -> p h b", b=NB)).then_inc(sems["bg"], 1)
                dve.wait_ge(sems["bg"], 1)
                sc(tt(sm[0], BG[:, 6:12, :].rearrange("p h b -> p (h b)"), par("dt", 0, 24), ALU.add))
                sc(stt(sm[2], sm[0], -1.0, sm[0], ALU.mult, ALU.max))
                dve.wait_ge(sems["sc_act"], 4)
                sc(stt(sm[3], sm[0], 0.0, sm[2], ALU.max, ALU.add))
                sc(stt(SC[:, :, 0, :], hb(sm[3]), -1.0, hb(sm[1]), ALU.mult, ALU.mult))
                sc(dve.tensor_scalar(sm[5], sm[5], 1.0, None, ALU.add))
                sc(dve.reciprocal(SC[:, :, 1, :], hb(sm[5])))

            def decays_2():
                dve.wait_ge(sems["sc_act"], 7)
                sc(tt(hb(sm[0]), hb(PS[:, 5, 96:120]), SC[:, :, 4, :], ALU.subtract))
                sc(tt(SC[:, :, 5, :], SC[:, :, 1, :], hb(sm[7]), ALU.mult))
                dve.wait_ge(sems["l2rt"], 1)
                sc(stt(SC[:, :, 3, :], RQK[:, 0:6, :], P * P * EPS, RQK[:, 0:6, :], ALU.mult, ALU.mult))
                sc(dve.reciprocal(SC[:, :, 2, :], RQK[:, 6:12, :]))
                dve.wait_ge(sems["sc_act"], 8)

            def gate_tile(u, i, step, j):
                t = 2 * (u - U0["A.gate"]) + j
                tt(TMP[t // 3][t % 3][:, :], PS[:, 2 * (u % 2) + j, :], RS[:, :], ALU.mult).then_inc(sems["emptied_dve"], 1)

            units("A.gate", evac=gate_tile, behind=lambda r: decays_1() if r == 0 else decays_2() if r == 2 else None)
            delta_net()

            def apply_gates():
                for t in range(NT):
                    tt(QKV[:, t, :], QKV[:, t, :], GATES[:, t, :], ALU.mult).then_inc(sems["gated"], 1)

            memory_attention(0, 64 ** -0.5, beside=apply_gates)
            for k in range(KD):
                mix_lo("A.mix", k, QKV[:, k, :] if k < NT else CX[:, k - NT, :])
            units("A.out")
            post_and_operand("A.post", "post_mix0", "A.mlp", "pre_mlp0")
            mlp(0)
            post_and_operand("A.post2", "post_mlp0", "B.in", "pre_mix1")

            def qk_tile(u, i, step, j):
                t = 2 * (u - U0["B.qk"]) + j
                if i is None:
                    o = QB[:, t, :] if t < NT else KB[:, t - NT, :]
                else:
                    o = tile(QKB, i * (2 * step) + t)
                stt(o, PS[:, 2 * (u % 2) + j, :], 1.0, RS[:, :], ALU.mult, ALU.mult).then_inc(sems["emptied_dve"], 1)

            units("B.qk", norm="B.in", evac=qk_tile)
            units("B.v", evac=vstage("B.v"))
            units("B.memq", evac=scaled_to(lambda t: MQB[:, t, :], "B.memq"))
            dve.wait_ge(sems["emptied_dve"], emptied("dve", U0["B.memq"], 1))
            dve.tensor_scalar(QB[:, :, :], QB[:, :, :], 64 ** -0.5, None, ALU.mult).then_inc(sems["q_scaled"], 1)
            stick_breaking()
            memory_attention(1, 64 ** -0.5)
            for k in (6, 7):
                mix_lo("B.mix", k, MO[:, k - NT, :])
            units("B.out")
            post_and_operand("B.post", "post_mix1", "B.mlp", "pre_mlp1")
            mlp(1)
            post_and_operand("B.post2", "post_mlp1", "C.in", "g_mix")

            for n in range(2):
                dve.tensor_tensor_reduce(out=PA[:, n, 64:128], in0=par(("lq1", "lq2")[n], 0, 64), in1=par(("lk1", "lk2")[n], 0, 64),
                                         scale=1.0, scalar=0.0, op0=ALU.mult, op1=ALU.add, accum_out=LAM[:, n:n + 1])\
                    .then_inc(sems["lam"], 1)
            dve.memset(PA[:, :, 0:16], 0.0).then_inc(sems["pool_s"], 1)
            dve.memset(UT[:, :, 0:16], 0.0).then_inc(sems["pool_s"], 1)

            def pool_windows(g):
                before = 2 + sum(gg + 2 for gg in range(g))
                src = UT[:, g, :]
                if g == 0:
                    dve.wait_ge(sems["rcnt_in"], 16)
                    dve.wait_ge(sems["lam"], 2)
                    dve.wait_ge(sems["emptied_dve"], emptied("dve", U0["C.u"] + 1, 1))
                else:
                    dve.wait_ge(sems["pool_z"], g)
                for lv in range(g + 1):
                    dve.wait_ge(sems["pool_s"], before + lv)
                    dst = PA[:, lv % 2, :]
                    sh = 2 ** lv
                    tt(dst[:, 16:16 + S], src[:, 16:16 + S], src[:, 16 - sh:16 - sh + S], ALU.add).then_inc(sems["pool_s"], 1)
                    src = dst
                dve.wait_ge(sems["pool_s"], before + g + 1)
                z = PA[:, (g + 1) % 2, 16:16 + S]
                tt(z, src[:, 16:16 + S], RCNT[:, g, :], ALU.mult).then_inc(sems["pool_s"], 1)
                dve.wait_ge(sems["pool_s"], before + g + 2)
                tt(UT[:, g, 16:16 + S], z, UT[:, g, 16:16 + S], ALU.subtract).then_inc(sems["pool_z"], 1)

            def rope(t):
                x = (QC if t < 4 else KC)[:, t % 4, :]
                r = PA[:, t % 2, 0:S]
                if t == 0:
                    dve.wait_ge(sems["rope_in"], 16)
                    dve.wait_ge(sems["pool_z"], 4)
                if t >= 2:
                    dve.wait_ge(sems["rope_done"], t - 1)
                dve.wait_ge(sems["rope_mm"], t + 1)
                tt(r, PS[:, 7, :], COSIN[:, 1, :], ALU.mult).then_inc(sems["rope_sin"], 1)
                tt(x, x, COSIN[:, 0, :], ALU.mult).then_inc(sems["rope_cos"], 1)
                dve.wait_ge(sems["rope_cos"], t + 1)
                tt(x, x, r, ALU.add).then_inc(sems["rope_done"], 1)

            units("C.u", norm="C.in", evac=scaled_to(lambda t: UT[:, t, 16:16 + S], "C.u"))
            units("C.qk", evac=scaled_to(lambda t: QC[:, t, :] if t < 4 else KC[:, t - 4, :], "C.qk"), behind=pool_windows)
            units("C.v", evac=vstage("C.v"), behind=rope)

            def two_ropes(r):
                if r < 3:
                    rope(2 + 2 * r)
                    rope(3 + 2 * r)

            units("C.gate", evac=scaled_to(lambda t: GC_[:, t, :], "C.gate"), behind=two_ropes)
            dve.wait_ge(sems["lam_act"], 1)
            tt(LAM[:, 4:5], LAM[:, 3:4], LAM[:, 2:3], ALU.subtract).then_inc(sems["lam"], 1)
            dve.wait_ge(sems["lam"], 3)
            dve.tensor_scalar(LAM[:, 5:6], LAM[:, 4:5], -LAM_INIT, None, ALU.add).then_inc(sems["lam"], 1)

            def top(h, c):
                dve.wait_ge(sems["df_s"], 2 * h + c + 1)
                s0 = PSF[:, 1536 * c:1536 * c + SB_ALL]
                three = s0[:, 384:1280].rearrange("p (a n) -> p a n", n=P)[:, 0:7:3, :]
                tt(three, three, con("causal_add").unsqueeze(1).to_broadcast([P, 3, P]), ALU.add).then_inc(sems["df_mask"], 1)
                tt(s0[:, 896:1024], s0[:, 896:1024], con("causal_add"), ALU.add).then_inc(sems["df_mask"], 1)
                dve.wait_ge(sems["df_mask"], 4 * h + 2 * c + 2)
                for b in range(NB):
                    last = dve.tensor_reduce(DMX[:, c, 0, b:b + 1], s0[:, DF_OFF[b]:DF_OFF[b] + DF_WID[b]], AX.X, ALU.max)
                last.then_inc(sems["df_max"], 1)
                dve.wait_ge(sems["df_max"], 2 * h + c + 1)
                dve.tensor_scalar(DMX[:, c, 1, :], DMX[:, c, 0, :], -(64 ** -0.5), None, ALU.mult).then_inc(sems["df_nm"], 1)

            top(0, 0)
            top(0, 1)
            for g in range(4):
                dve.wait_ge(sems["pool_mm"], g + 1)
                dve.wait_ge(sems["sig"], g + 1)
                stt(GC_[:, g, :], PS[:, 6 + g % 2, :], par("pool_scale", g), GC_[:, g, :], ALU.mult, ALU.mult)\
                    .then_inc(sems["mixed"], 1)
            for g in range(4):
                mix_lo("C.mix", g, GC_[:, g, :])
            dve.wait_ge(sems["lam"], 4)
            for h in range(4):
                hb4 = slice(NB * h, NB * h + NB)
                dve.wait_ge(sems["df_exp"], 8 * h + 8)
                dve.reciprocal(COEF[:, hb4], SUM1[:, hb4]).then_inc(sems["df_ri"], 1)
                dve.wait_ge(sems["df_ri"], 2 * h + 1)
                stt(COEF[:, hb4], COEF[:, hb4], LAM[:, 5:6], SUM0[:, hb4], ALU.mult, ALU.mult).then_inc(sems["df_ri"], 1)
                dve.wait_ge(sems["df_ri"], 2 * h + 2)
                for b in range(NB):
                    o = slice(DF_OFF[b], DF_OFF[b] + DF_WID[b])
                    stt(DP0[h % 2][:, o], DP1[:, o], COEF[:, NB * h + b:NB * h + b + 1], DP0[h % 2][:, o], ALU.mult, ALU.add)\
                        .then_inc(sems["df_a"], 1)
                if h < 3:
                    top(h + 1, 0)
                    top(h + 1, 1)
            dve.reciprocal(RI0, SUM0).then_inc(sems["df_r0"], 1)
            dve.wait_ge(sems["df_r0"], 1)
            dve.wait_ge(sems["df_ss"], 1)
            tt(RMSD, PS[:, 7, 0:4 * NB], RI0, ALU.mult).then_inc(sems["df_w"], 1)
            dve.wait_ge(sems["df_w"], 1)
            tt(RMSD, RMSD, RI0, ALU.mult).then_inc(sems["df_w"], 1)
            dve.wait_ge(sems["df_rt"], 1)
            dve.reciprocal(COEF, RMSD).then_inc(sems["df_rs"], 1)
            dve.wait_ge(sems["df_rs"], 1)
            tt(COEF, COEF, RI0, ALU.mult).then_inc(sems["df_rs"], 2)
            for h in range(5):
                if h < 4:
                    dve.wait_ge(sems["df_bc"], h + 1)
                    stt(QC[:, h, :], QC[:, h, :], par("g_subln"), PS[:, 4 + h, :], ALU.mult, ALU.mult).then_inc(sems["df_g"], 1)
                    dve.wait_ge(sems["df_g"], 2 * h + 1)
                    stt(GC_[:, 4 + h, :], QC[:, h, :], 1.0 - LAM_INIT, GC_[:, 4 + h, :], ALU.mult, ALU.mult)\
                        .then_inc(sems["df_g"], 1)
                if h:
                    mix_lo("C.mix", 3 + h, GC_[:, 3 + h, :])

            units("C.out", evac=add_to(XT, "C.out"))
            operand_lo("mem2", MX2, "g_mem", MH2, ML2, MEM)
            for r in range(4):
                if r == 0:
                    invert("mem2", MB)
                split_lo(U0["C.mem"] + 2 * r + 2)
                split_lo(U0["C.mem"] + 2 * r + 3)
            operand_lo("C.cross", XT, "g_cross")
            units("C.cq", norm="C.cross", evac=scaled_to(lambda t: CQ[:, t, :], "C.cq"))
            memory_attention(2, 256 ** -0.5)
            for k in range(KD):
                mix_lo("C.att", k, CQ[:, k, :])
            units("C.co", evac=add_to(XT, "C.co"))
            operand_lo("C.mlp", XT, "g_mlp")
            mlp(2)
            invert("final")
            dve.wait_ge(sems["rs"], bcast_done("final"))
            for k in range(KD):
                stt(Y[:, k, :], XT[:, k, :], par("g_final", k), RS[:, :], ALU.mult, ALU.mult).then_inc(sems["out_ready"], 1)


def kernel(**inputs):
    import concourse.bacc as bacc
    from concourse.bass_utils import run_bass_kernel_spmd

    a = {k: np.asarray(v) for k, v in inputs.items()}
    f = np.float32

    def unit(w, c0, r0=0):
        return w[r0:r0 + D, c0:c0 + UC].reshape(KD, P, UC).transpose(1, 0, 2).reshape(P, KD * UC)

    ws = np.zeros((UNITS, P, KD * UC), f)

    def place(name, w, c0=0, r0=0, at=0, n=None):
        for r in range(NU[name] if n is None else n):
            ws[U0[name] + at + r] = unit(w, c0 + UC * r, r0)

    def place_mlp(name, up, down):
        for q in range(QUARTERS):
            place(name, up, c0=D * q, at=8 * q, n=4)
            place(name, down, r0=D * q, at=8 * q + 4, n=4)

    wa, wb, wc = a["w_in_a"][0], a["w_in_b"][0], a["w_in_2"][0]
    place("A.mem", a["w_mem_kv"][0])
    place("B.mem", a["w_mem_kv"][1])
    place("A.qkv", wa)
    place("A.gate", wa, 3 * W)
    ws[U0["A.bg"]].reshape(P, KD, UC)[:, :, 0:12] = wa[:, 4 * W:4 * W + 12].reshape(KD, P, 12).transpose(1, 0, 2)
    place("A.memq", wa, 4 * W + 12)
    place("A.out", a["w_out"][0])
    place_mlp("A.mlp", a["w_up"][0], a["w_down"][0])
    place("B.qk", wb)
    place("B.v", wb, 2 * W)
    place("B.memq", wb, 3 * W)
    place("B.out", a["w_out"][1])
    place_mlp("B.mlp", a["w_up"][1], a["w_down"][1])
    place("C.u", wc)
    place("C.qk", wc, 512)
    place("C.v", wc, 1536)
    place("C.gate", wc, 2048)
    place("C.out", a["w_out_2"][0])
    place("C.mem", a["w_ckv_2"][0])
    place("C.cq", a["w_cq_2"][0])
    place("C.co", a["w_co_2"][0])
    place_mlp("C.mlp", a["w_up_2"][0], a["w_down_2"][0])

    par = np.zeros((P, NPAR), f)

    def put(name, v):
        par[:, PCOL[name]:PCOL[name] + v.shape[1]] = v

    cols = lambda v: v.reshape(-1, P).T
    rows = lambda v: np.broadcast_to(v.reshape(1, -1), (P, v.size))
    put("mem_norm", cols(a["mem_norm"]))
    for i in range(2):
        for p, n in (("pre_mix", "norm_pre_mix"), ("post_mix", "norm_post_mix"), ("pre_mlp", "norm_pre_mlp"),
                     ("post_mlp", "norm_post_mlp")):
            put(f"{p}{i}", cols(a[n][i]))
    for p, n in (("g_mix", "g_mix_2"), ("g_cross", "g_cross_2"), ("g_mem", "g_mem_2"), ("g_mlp", "g_mlp_2"),
                 ("g_final", "g_final_2"), ("pool_scale", "pool_scale_2")):
        put(p, cols(a[n]))
    put("conv", a["conv_w_a"][0].reshape(4, 18, P).transpose(2, 1, 0).reshape(P, 72))
    put("a_log", rows(np.repeat(a["a_log_a"][0], NB)))
    put("dt", rows(np.repeat(a["dt_bias_a"][0], NB)))
    put("onorm", cols(a["onorm_a"][0]))
    put("g_subln", cols(a["g_subln_2"][0]))
    for p, n in (("lq1", "lambda_q1_2"), ("lk1", "lambda_k1_2"), ("lq2", "lambda_q2_2"), ("lk2", "lambda_k2_2")):
        put(p, rows(a[n][0]))
    put("w_pool", a["w_pool_2"][0].transpose(1, 0, 2).reshape(P, 4 * P))

    con = np.zeros((P, NCON), f)
    r, c = np.arange(P)[:, None], np.arange(P)[None, :]

    def const(name, v, at=0):
        con[:, CCOL[name] + at:CCOL[name] + at + P] = v

    const("ident", r == c)
    const("tri_le", r <= c)
    const("strict", r < c)
    const("cap", np.where(r < c, 3e38, 0))
    const("neg_tri", -(r >= c).astype(f))
    const("neg_ones", -1)
    const("ones", 1)
    const("causal_add", np.where(c <= r, 0, -1e30))
    const("swap", r == (c ^ 32))
    for lv in range(7):
        b = 2 ** lv
        const("level", (r // (2 * b) == c // (2 * b)) & (r % (2 * b) < b) & (c % (2 * b) >= b), lv * P)

    inv = f(10000.0) ** (-np.arange(0, 64, 2, dtype=f) / f(64))
    ang = (np.arange(S, dtype=f)[:, None] * inv[None, :]).astype(f)
    cos, sin = np.cos(ang).T, np.sin(ang).T
    rope = np.stack([np.concatenate([cos] * 4), np.concatenate([-sin, sin] * 2)], 1).astype(f)
    cnt = np.minimum(np.arange(S) + 1, np.array([2, 4, 8, 16])[:, None])
    rcnt = np.ascontiguousarray(np.broadcast_to((1.0 / cnt).astype(f), (P, 4, S)))

    def turned(x):
        return np.ascontiguousarray(x.T.reshape(KD, P, -1).transpose(1, 0, 2))

    arrays = {"weights": ws, "x_t": turned(a["x"][0]), "mem_t": turned(a["mem"][0]), "mem2_t": turned(a["mem_2"][0]),
              "params": par, "consts": con, "rope": rope, "recip_counts": rcnt}
    nc = bacc.Bacc("TRN2", target_bir_lowering=False, num_devices=1)
    aps = [nc.dram_tensor(k, v.shape, mybir.dt.from_np(v.dtype), kind="ExternalInput").ap() for k, v in arrays.items()]
    out = nc.dram_tensor("out_t", (D, S), F32, kind="ExternalOutput").ap()
    program(nc, *aps, out)
    r = run_bass_kernel_spmd(nc, [arrays], core_ids=[0])
    return np.ascontiguousarray(r.results[0]["out_t"].T)[None]
```
